# Optimizing a Trainium2 kernel written in Bass

```python
import math
import jax, jax.numpy as jnp
from jax import lax
import numpy as np

D_MODEL = 1024
BATCH = 1
SEQ = 512
DEPTH = 1

N_META = 16
GRID_W = 64
Q_BLOCK = 128
HEAD_DIM = 64
ROPE_THETA = 10000.0
EPS = 1e-6
A_HEADS = 8
A_KV_HEADS = 2
A_GROUP = A_HEADS // A_KV_HEADS
A_WIDTH = A_HEADS * HEAD_DIM
A_KV_WIDTH = A_KV_HEADS * HEAD_DIM
B_HEADS = 4
B_VDIM = 2 * HEAD_DIM
B_WIDTH = B_HEADS * B_VDIM
MIX_WIDTH = A_WIDTH + B_WIDTH
IN_WIDTH = A_WIDTH + 2 * A_KV_WIDTH + 3 * B_WIDTH
D_FF = -(-8 * D_MODEL // (3 * 256)) * 256


def rms_norm(x, g):
    xf = x.astype(jnp.float32)
    y = xf * lax.rsqrt(jnp.mean(xf * xf, axis=-1, keepdims=True) + EPS)
    return (y * g.astype(jnp.float32)).astype(x.dtype)

def apply_rope(x, ang):
    xf = x.astype(jnp.float32).reshape(x.shape[:-1] + (x.shape[-1] // 2, 2))
    c = jnp.cos(ang)[None, :, None, :]
    s = jnp.sin(ang)[None, :, None, :]
    x1, x2 = xf[..., 0], xf[..., 1]
    out = jnp.stack([x1 * c - x2 * s, x1 * s + x2 * c], axis=-1)
    return out.reshape(x.shape).astype(x.dtype)

def rope_angles_1d(length):
    pos = jnp.arange(length, dtype=jnp.float32)
    inv = ROPE_THETA ** (-jnp.arange(0, HEAD_DIM, 2, dtype=jnp.float32) / HEAD_DIM)
    return pos[:, None] * inv[None, :]

def rope_angles_axial(n_tokens):
    rows = n_tokens // GRID_W
    r = jnp.repeat(jnp.arange(rows, dtype=jnp.float32), GRID_W)
    c = jnp.tile(jnp.arange(GRID_W, dtype=jnp.float32), rows)
    half = HEAD_DIM // 2
    inv = ROPE_THETA ** (-jnp.arange(0, half, 2, dtype=jnp.float32) / half)
    ang = jnp.concatenate([r[:, None] * inv[None, :], c[:, None] * inv[None, :]], axis=-1)
    meta = jnp.zeros((N_META, HEAD_DIM // 2), jnp.float32)
    return jnp.concatenate([meta, ang], axis=0)

def sweep_queries(fn, q):
    out_meta = fn(q[:, :N_META])
    real = q[:, N_META:]
    bsz, s = real.shape[0], real.shape[1]
    nb = s // Q_BLOCK
    blocks = jnp.moveaxis(real.reshape((bsz, nb, Q_BLOCK) + real.shape[2:]), 1, 0)
    out = lax.map(fn, blocks)
    out = jnp.moveaxis(out, 0, 1).reshape((bsz, s) + out.shape[3:])
    return jnp.concatenate([out_meta, out], axis=1)

def first_inputs(seed: int = 0) -> dict:
    key = jax.random.key(seed)
    ks = jax.random.split(key, 20)
    f32 = jnp.float32

    def gain(k, shape):
        return 1.0 + 0.1 * jax.random.normal(k, shape, f32)

    return {
        "x": jax.random.normal(ks[0], (BATCH, SEQ, D_MODEL), f32),
        "meta_tokens": jax.random.normal(ks[1], (N_META, D_MODEL), f32),
        "attn_norm_g": gain(ks[2], (DEPTH, D_MODEL)),
        "w_in": jax.random.normal(ks[3], (DEPTH, D_MODEL, IN_WIDTH), f32) * D_MODEL ** -0.5,
        "a_q_norm_g": gain(ks[4], (DEPTH, HEAD_DIM)),
        "a_k_norm_g": gain(ks[5], (DEPTH, HEAD_DIM)),
        "b_q_norm_g": gain(ks[6], (DEPTH, HEAD_DIM)),
        "b_k_norm_g": gain(ks[7], (DEPTH, HEAD_DIM)),
        "b_lambda_q1": 0.1 * jax.random.normal(ks[8], (DEPTH, HEAD_DIM), f32),
        "b_lambda_k1": 0.1 * jax.random.normal(ks[9], (DEPTH, HEAD_DIM), f32),
        "b_lambda_q2": 0.1 * jax.random.normal(ks[10], (DEPTH, HEAD_DIM), f32),
        "b_lambda_k2": 0.1 * jax.random.normal(ks[11], (DEPTH, HEAD_DIM), f32),
        "b_subln_g": gain(ks[12], (DEPTH, B_VDIM)),
        "w_out": jax.random.normal(ks[13], (DEPTH, MIX_WIDTH, D_MODEL), f32) * MIX_WIDTH ** -0.5,
        "ffn_norm_g": gain(ks[14], (DEPTH, D_MODEL)),
        "w_gate": jax.random.normal(ks[15], (DEPTH, D_MODEL, D_FF), f32) * D_MODEL ** -0.5,
        "w_up": jax.random.normal(ks[16], (DEPTH, D_MODEL, D_FF), f32) * D_MODEL ** -0.5,
        "w_down": jax.random.normal(ks[17], (DEPTH, D_FF, D_MODEL), f32) * D_FF ** -0.5,
    }

def first_block(x, meta_tokens, attn_norm_g, w_in, a_q_norm_g, a_k_norm_g, b_q_norm_g, b_k_norm_g,
              b_lambda_q1, b_lambda_k1, b_lambda_q2, b_lambda_k2, b_subln_g, w_out,
              ffn_norm_g, w_gate, w_up, w_down):
    bsz, s, _ = x.shape
    meta = jnp.broadcast_to(meta_tokens.astype(x.dtype)[None], (bsz, N_META, D_MODEL))
    x = jnp.concatenate([meta, x], axis=1)
    length = N_META + s

    ang_a = rope_angles_axial(s)
    ang_b = rope_angles_1d(length)
    scale = HEAD_DIM ** -0.5
    splits = np.cumsum([A_WIDTH, A_KV_WIDTH, A_KV_WIDTH, B_WIDTH, B_WIDTH]).tolist()

    for l in range(DEPTH):
        lam_init = 0.8 - 0.6 * math.exp(-0.3 * l)
        h = rms_norm(x, attn_norm_g[l])
        proj = jnp.einsum('bld,de->ble', h, w_in[l])
        qa, ka, va, qb, kb, vb = jnp.split(proj, splits, axis=-1)

        qa = apply_rope(rms_norm(qa.reshape(bsz, length, A_HEADS, HEAD_DIM), a_q_norm_g[l]), ang_a)
        ka = apply_rope(rms_norm(ka.reshape(bsz, length, A_KV_HEADS, HEAD_DIM), a_k_norm_g[l]), ang_a)
        va = va.reshape(bsz, length, A_KV_HEADS, HEAD_DIM)

        def gqa_block(q):
            nq = q.shape[1]
            qg = q.reshape(q.shape[0], nq, A_KV_HEADS, A_GROUP, HEAD_DIM)
            sc = jnp.einsum('bqkgd,blkd->bkgql', qg, ka).astype(jnp.float32) * scale
            p = jax.nn.softmax(sc, axis=-1).astype(va.dtype)
            o = jnp.einsum('bkgql,blkd->bqkgd', p, va)
            return o.reshape(q.shape[0], nq, A_WIDTH)

        out_a = sweep_queries(gqa_block, qa)

        qb = apply_rope(rms_norm(qb.reshape(bsz, length, 2 * B_HEADS, HEAD_DIM), b_q_norm_g[l]), ang_b)
        kb = apply_rope(rms_norm(kb.reshape(bsz, length, 2 * B_HEADS, HEAD_DIM), b_k_norm_g[l]), ang_b)
        qb = qb.reshape(bsz, length, B_HEADS, 2, HEAD_DIM)
        kb = kb.reshape(bsz, length, B_HEADS, 2, HEAD_DIM)
        vb = vb.reshape(bsz, length, B_HEADS, B_VDIM)
        lam = (jnp.exp(jnp.sum(b_lambda_q1[l].astype(jnp.float32) * b_lambda_k1[l].astype(jnp.float32)))
               - jnp.exp(jnp.sum(b_lambda_q2[l].astype(jnp.float32) * b_lambda_k2[l].astype(jnp.float32)))
               + lam_init)
        subln_g = b_subln_g[l]

        def diff_block(q):
            nq = q.shape[1]
            sc = jnp.einsum('bqhjd,blhjd->bhjql', q, kb).astype(jnp.float32) * scale
            p = jax.nn.softmax(sc, axis=-1)
            w = (p[:, :, 0] - lam * p[:, :, 1]).astype(vb.dtype)
            o = jnp.einsum('bhql,blhe->bqhe', w, vb)
            o = rms_norm(o, subln_g) * (1.0 - lam_init)
            return o.reshape(q.shape[0], nq, B_WIDTH)

        out_b = sweep_queries(diff_block, qb)

        mixed = jnp.concatenate([out_a, out_b], axis=-1)
        x = x + jnp.einsum('ble,ed->bld', mixed, w_out[l])

        h = rms_norm(x, ffn_norm_g[l])
        g = jnp.einsum('bld,df->blf', h, w_gate[l])
        u = jnp.einsum('bld,df->blf', h, w_up[l])
        x = x + jnp.einsum('blf,fd->bld', jax.nn.silu(g) * u, w_down[l])

    return x[:, N_META:]


MLA_HEADS = 8
MLA_Q_RANK = 384
MLA_KV_RANK = 256
MLA_NOPE_DIM = 64
MLA_ROPE_DIM = 32
MLA_V_DIM = 64
MLA_QK_DIM = MLA_NOPE_DIM + MLA_ROPE_DIM
FOX_HEADS = 8
FOX_HEAD_DIM = 64
FOX_WIDTH = FOX_HEADS * FOX_HEAD_DIM
MIX_WIDTH_2 = MLA_HEADS * MLA_V_DIM + FOX_WIDTH
BLOCK_Q = 128
IN_SPLITS = (MLA_Q_RANK, MLA_KV_RANK, MLA_ROPE_DIM, FOX_WIDTH, FOX_WIDTH, FOX_WIDTH, FOX_HEADS)
IN_WIDTH_2 = sum(IN_SPLITS)
PEER_HEADS = 8
N_KEYS = 128
N_EXPERTS = N_KEYS * N_KEYS
PEER_QDIM = 256
PEER_HALF = PEER_QDIM // 2
PEER_TOPK = 16
PEER_CHUNK = 64


def _rms_norm(x, g):
    xf = x.astype(jnp.float32)
    y = xf * lax.rsqrt(jnp.mean(xf * xf, axis=-1, keepdims=True) + EPS)
    return (y * g.astype(jnp.float32)).astype(x.dtype)

def _modulate(x, g, shift, scale):
    return _rms_norm(x, g) * (1.0 + scale) + shift

def _rope(x, ang):
    half = x.shape[-1] // 2
    x1, x2 = x[..., :half], x[..., half:]
    cos = jnp.cos(ang).astype(x.dtype)
    sin = jnp.sin(ang).astype(x.dtype)
    return jnp.concatenate([x1 * cos - x2 * sin, x2 * cos + x1 * sin], axis=-1)

def _causal_block_attention(q, k, v, scale, fcum=None):
    b, h, s, dk = q.shape
    dv = v.shape[-1]
    nblk = s // BLOCK_Q
    qb = q.reshape(b, h, nblk, BLOCK_Q, dk).transpose(2, 0, 1, 3, 4)
    kf = k.astype(jnp.float32)
    vf = v.astype(jnp.float32)
    key_pos = jnp.arange(s)
    blk_ids = jnp.arange(nblk)

    def scores(q_i):
        return jnp.einsum("bhqd,bhkd->bhqk", q_i.astype(jnp.float32), kf) * scale

    def finish(i, sc):
        q_pos = i * BLOCK_Q + jnp.arange(BLOCK_Q)
        sc = jnp.where(key_pos[None, :] <= q_pos[:, None], sc, -jnp.inf)
        p = jax.nn.softmax(sc, axis=-1)
        return jnp.einsum("bhqk,bhkd->bhqd", p, vf)

    if fcum is None:
        out = lax.map(lambda a: finish(a[0], scores(a[1])), (blk_ids, qb))
    else:
        fb = fcum.reshape(b, h, nblk, BLOCK_Q).transpose(2, 0, 1, 3)

        def blk(a):
            i, q_i, f_i = a
            sc = scores(q_i) + f_i[..., None] - fcum[:, :, None, :]
            return finish(i, sc)

        out = lax.map(blk, (blk_ids, qb, fb))
    return out.transpose(1, 2, 0, 3, 4).reshape(b, h, s, dv).astype(v.dtype)

def _peer(h, w_pq, sub_keys, peer_u, peer_v):
    b, s, d = h.shape
    qp = (h @ w_pq).astype(jnp.float32).reshape(b, s, PEER_HEADS, 2, PEER_HALF)
    sc = jnp.einsum("bshpd,hpnd->bshpn", qp, sub_keys.astype(jnp.float32))
    s1, i1 = lax.top_k(sc[..., 0, :], PEER_TOPK)
    s2, i2 = lax.top_k(sc[..., 1, :], PEER_TOPK)
    cand = (s1[..., :, None] + s2[..., None, :]).reshape(b, s, PEER_HEADS, PEER_TOPK * PEER_TOPK)
    top_s, top_c = lax.top_k(cand, PEER_TOPK)
    e1 = jnp.take_along_axis(i1, top_c // PEER_TOPK, axis=-1)
    e2 = jnp.take_along_axis(i2, top_c % PEER_TOPK, axis=-1)
    expert = e1 * N_KEYS + e2
    gate = jax.nn.softmax(top_s, axis=-1)
    nc = s // PEER_CHUNK

    def to_chunks(a):
        return a.reshape((b, nc, PEER_CHUNK) + a.shape[2:]).swapaxes(0, 1)

    def chunk(args):
        h_c, e_c, g_c = args
        u = jnp.take(peer_u, e_c, axis=0)
        a = jnp.einsum("bcd,bchkd->bchk", h_c.astype(jnp.float32), u.astype(jnp.float32))
        w = g_c * jax.nn.gelu(a)
        vv = jnp.take(peer_v, e_c, axis=0)
        return jnp.einsum("bchk,bchkd->bcd", w, vv.astype(jnp.float32))

    y = lax.map(chunk, (to_chunks(h), to_chunks(expert), to_chunks(gate)))
    return y.swapaxes(0, 1).reshape(b, s, d).astype(h.dtype)

def second_inputs(seed: int = 0) -> dict:
    key = jax.random.key(seed)
    ks = jax.random.split(key, 24)
    f32 = jnp.float32
    D = D_MODEL

    def nrm(k, shape, scale):
        return jax.random.normal(k, shape, f32) * scale

    def gain(k, n):
        return 1.0 + 0.02 * jax.random.normal(k, (n,), f32)

    x = jax.random.normal(ks[0], (BATCH, SEQ, D), f32)
    c = jax.random.normal(ks[1], (BATCH, D), f32)
    offset = jax.random.randint(ks[2], (BATCH, 1), 0, 1024, dtype=jnp.int32)
    positions = (offset + jnp.arange(SEQ, dtype=jnp.int32)[None, :]).astype(jnp.int32)
    return {
        "x": x,
        "c": c,
        "positions": positions,
        "w_ada": nrm(ks[3], (D, 6 * D), 0.5 * D ** -0.5),
        "b_ada": nrm(ks[4], (6 * D,), 0.01),
        "norm1_g": gain(ks[5], D),
        "w_in": nrm(ks[6], (D, IN_WIDTH_2), D ** -0.5),
        "mla_qa_g": gain(ks[7], MLA_Q_RANK),
        "mla_kva_g": gain(ks[8], MLA_KV_RANK),
        "w_uq": nrm(ks[9], (MLA_Q_RANK, MLA_HEADS * MLA_QK_DIM), MLA_Q_RANK ** -0.5),
        "w_ukv": nrm(ks[10], (MLA_KV_RANK, MLA_HEADS * (MLA_NOPE_DIM + MLA_V_DIM)), MLA_KV_RANK ** -0.5),
        "mla_q_g": gain(ks[11], MLA_QK_DIM),
        "mla_k_g": gain(ks[12], MLA_QK_DIM),
        "fox_q_g": gain(ks[13], FOX_HEAD_DIM),
        "fox_k_g": gain(ks[14], FOX_HEAD_DIM),
        "b_f": 2.0 + 0.5 * jax.random.normal(ks[15], (FOX_HEADS,), f32),
        "w_o": nrm(ks[16], (MIX_WIDTH_2, D), MIX_WIDTH_2 ** -0.5),
        "norm2_g": gain(ks[17], D),
        "w_pq": nrm(ks[18], (D, PEER_HEADS * PEER_QDIM), D ** -0.5),
        "sub_keys": nrm(ks[19], (PEER_HEADS, 2, N_KEYS, PEER_HALF), PEER_HALF ** -0.5),
        "peer_u": nrm(ks[20], (N_EXPERTS, D), D ** -0.5),
        "peer_v": nrm(ks[21], (N_EXPERTS, D), PEER_HEADS ** -0.5),
    }

def second_block(x, c, positions, w_ada, b_ada, norm1_g, w_in, mla_qa_g, mla_kva_g, w_uq, w_ukv,
              mla_q_g, mla_k_g, fox_q_g, fox_k_g, b_f, w_o, norm2_g, w_pq, sub_keys, peer_u, peer_v):
    dt = x.dtype
    b, s, d = x.shape
    mod = jax.nn.silu(c.astype(jnp.float32)) @ w_ada.astype(jnp.float32) + b_ada.astype(jnp.float32)
    mod = mod.reshape(b, 6, 1, d).astype(dt)
    shift1, scale1, gate1 = mod[:, 0], mod[:, 1], mod[:, 2]
    shift2, scale2, gate2 = mod[:, 3], mod[:, 4], mod[:, 5]
    inv_freq = ROPE_THETA ** (-jnp.arange(0, MLA_ROPE_DIM, 2, dtype=jnp.float32) / MLA_ROPE_DIM)
    ang = (positions.astype(jnp.float32)[..., None] * inv_freq)[:, :, None, :]

    for _ in range(DEPTH):
        h = _modulate(x, norm1_g, shift1, scale1)
        proj = h @ w_in
        cq, ckv, kpe, fq, fk, fv, fl = jnp.split(proj, list(np.cumsum(IN_SPLITS)[:-1]), axis=-1)

        q_a = (_rms_norm(cq, mla_qa_g) @ w_uq).reshape(b, s, MLA_HEADS, MLA_QK_DIM)
        kv_a = (_rms_norm(ckv, mla_kva_g) @ w_ukv).reshape(b, s, MLA_HEADS, MLA_NOPE_DIM + MLA_V_DIM)
        k_nope, v_a = kv_a[..., :MLA_NOPE_DIM], kv_a[..., MLA_NOPE_DIM:]
        k_pe = jnp.broadcast_to(kpe[:, :, None, :], (b, s, MLA_HEADS, MLA_ROPE_DIM))
        k_a = jnp.concatenate([k_nope, k_pe], axis=-1)
        q_a = _rms_norm(q_a, mla_q_g)
        k_a = _rms_norm(k_a, mla_k_g)
        q_a = jnp.concatenate([q_a[..., :MLA_NOPE_DIM], _rope(q_a[..., MLA_NOPE_DIM:], ang)], axis=-1)
        k_a = jnp.concatenate([k_a[..., :MLA_NOPE_DIM], _rope(k_a[..., MLA_NOPE_DIM:], ang)], axis=-1)
        o_a = _causal_block_attention(q_a.transpose(0, 2, 1, 3), k_a.transpose(0, 2, 1, 3),
                                      v_a.transpose(0, 2, 1, 3), MLA_QK_DIM ** -0.5)

        q_b = _rms_norm(fq.reshape(b, s, FOX_HEADS, FOX_HEAD_DIM), fox_q_g)
        k_b = _rms_norm(fk.reshape(b, s, FOX_HEADS, FOX_HEAD_DIM), fox_k_g)
        v_b = fv.reshape(b, s, FOX_HEADS, FOX_HEAD_DIM)
        log_f = jax.nn.log_sigmoid(fl.astype(jnp.float32) + b_f.astype(jnp.float32))
        fcum = jnp.cumsum(log_f, axis=1).transpose(0, 2, 1)
        o_b = _causal_block_attention(q_b.transpose(0, 2, 1, 3), k_b.transpose(0, 2, 1, 3),
                                      v_b.transpose(0, 2, 1, 3), FOX_HEAD_DIM ** -0.5, fcum)

        o = jnp.concatenate([o_a, o_b], axis=1).transpose(0, 2, 1, 3).reshape(b, s, MIX_WIDTH_2)
        x = x + gate1 * (o @ w_o)

        h2 = _modulate(x, norm2_g, shift2, scale2)
        x = x + gate2 * _peer(h2, w_pq, sub_keys, peer_u, peer_v)
    return x


def setup_inputs(seed=0):
    out = dict(first_inputs(seed))
    for name, value in second_inputs(seed + 1).items():
        if name != "x":
            out[name + "_2"] = value
    return out


def reference(
    x, meta_tokens, attn_norm_g, w_in, a_q_norm_g, a_k_norm_g, b_q_norm_g, b_k_norm_g,
    b_lambda_q1, b_lambda_k1, b_lambda_q2, b_lambda_k2, b_subln_g, w_out, ffn_norm_g, w_gate,
    w_up, w_down, c_2, positions_2, w_ada_2, b_ada_2, norm1_g_2, w_in_2, mla_qa_g_2,
    mla_kva_g_2, w_uq_2, w_ukv_2, mla_q_g_2, mla_k_g_2, fox_q_g_2, fox_k_g_2, b_f_2, w_o_2,
    norm2_g_2, w_pq_2, sub_keys_2, peer_u_2, peer_v_2,
):
    x = first_block(
        x, meta_tokens, attn_norm_g, w_in, a_q_norm_g, a_k_norm_g, b_q_norm_g, b_k_norm_g,
        b_lambda_q1, b_lambda_k1, b_lambda_q2, b_lambda_k2, b_subln_g, w_out, ffn_norm_g,
        w_gate, w_up, w_down,
    )
    return second_block(
        x, c_2, positions_2, w_ada_2, b_ada_2, norm1_g_2, w_in_2, mla_qa_g_2, mla_kva_g_2,
        w_uq_2, w_ukv_2, mla_q_g_2, mla_k_g_2, fox_q_g_2, fox_k_g_2, b_f_2, w_o_2, norm2_g_2,
        w_pq_2, sub_keys_2, peer_u_2, peer_v_2,
    )


_drawn_inputs = setup_inputs


def setup_inputs(seed=0):
    import zlib

    import numpy as np

    out = dict(_drawn_inputs(seed))
    spreads = {}
    factors = {'a_q_norm_g': 8.0,
     'a_k_norm_g': 8.0,
     'b_lambda_k1': 8.0,
     'b_lambda_q2': 8.0,
     'b_ada_2': 7.54,
     'norm1_g_2': 8.0,
     'mla_qa_g_2': 8.0,
     'mla_kva_g_2': 8.0,
     'w_uq_2': 2.899,
     'mla_q_g_2': 8.0,
     'mla_k_g_2': 8.0,
     'fox_q_g_2': 8.0,
     'fox_k_g_2': 8.0,
     'norm2_g_2': 8.0}
    for name, (base, spread) in spreads.items():
        noise = np.random.default_rng([zlib.crc32(name.encode()), seed]).standard_normal(out[name].shape)
        drawn = base * np.exp(spread * noise) if base else spread * noise
        out[name] = __import__('jax').numpy.asarray(drawn.astype(out[name].dtype))
    for name, factor in factors.items():
        out[name] = (out[name] * factor).astype(out[name].dtype)
    return out
```

```python
from contextlib import ExitStack

import numpy as np

import concourse.bass as bass
from concourse import mybir

ALU = mybir.AluOpType
ACT = mybir.ActivationFunctionType
F32 = mybir.dt.float32
I32 = mybir.dt.int32
U32 = mybir.dt.uint32
AX = mybir.AxisListType

P = 128
D = 1024
KD = D // P
T = 4
META = 16
KEYS = T * P + META
HALF = KEYS // 2
FF = 2816
NF = FF // P
EPS = 1e-6
HD = 64
SCALE = HD ** -0.5
LAM_INIT = 0.2
MLA_QK = 96
MLA_SCALE = MLA_QK ** -0.5
QR, KVR = 384, 256
LAT = 680
HEADS2 = 16
PH, TOPK, NKEYS = 8, 16, 128
SLOTS = PH * TOPK
LOW = -3.0e38
MASK = -(2.0 ** 100)

CH = 2048
W_IN, W_OUT = 0, 9
W_GU = W_OUT + 4
W_DOWN = W_GU + NF
W_IN2 = W_DOWN + NF // 2
W_LAT = W_IN2 + 9
W_O2 = W_LAT + 3
W_PQ = W_O2 + 4
NCHUNK = W_PQ + 8
WR = 6

C_G1, C_GF, C_N1, C_N2, C_BADA, C_QA, C_KVA, NCOL = 0, 8, 16, 24, 32, 80, 83, 85
K_ID, K_TRIU, K_MASK, K_ONES, K_IOTA, K_FREQ, NCONST = 0, 128, 256, 384, 512, 528, 544
RA_ROPE, RA_SUB, RA_LAM, NRA = 0, 512, 640, 896
RB_C, RB_MQ, RB_MK, RB_FQ, RB_FK, RB_BF, NRB = 0, 1024, 1120, 1216, 1280, 1344, 1352

TWO_PI = 2.0 * np.pi
PI2_A = 6.28125
PI2_B = float(np.floor((TWO_PI - PI2_A) * 2.0 ** 20) / 2.0 ** 20)
PI2_C = float(TWO_PI - PI2_A - PI2_B)
ROUND = 1.5 * 2.0 ** 23
PI_F = 3.1415925


def build(nc, wst, wada, x_in, meta_in, cols_in, rowsa_in, rowsb_in, rope_in, const_in, pos_in,
          subk_in, peer_u, peer_v, out):
    ctx = ExitStack()
    with ctx:
        def sb(name, shape, dt=F32):
            return ctx.enter_context(nc.sbuf_tensor(name, shape, dt))

        def sem(name):
            return ctx.enter_context(nc.semaphore(name))

        def cut(arena, at, *dims):
            n = int(np.prod(dims))
            v = arena[:, at:at + n]
            if len(dims) == 2:
                return v.rearrange("p (a b) -> p a b", a=dims[0])
            if len(dims) == 3:
                return v.rearrange("p (a b c) -> p a b c", a=dims[0], b=dims[1])
            return v

        def over(ap, n):
            return ap.unsqueeze(len(ap.shape)).broadcast_to([*ap.shape, n])

        def each(ap, n):
            return ap.unsqueeze(1).broadcast_to([ap.shape[0], n, *ap.shape[1:]])

        ps = ctx.enter_context(nc.psum_tensor("ps", [P, 8, 512], F32))

        x = sb("x", [P, T, D])
        big = sb("big", [P, WR * CH + 4224])
        r1 = sb("r1", [P, 11360])
        r2 = sb("r2", [P, 17312])
        gates = sb("gates", [P, 2, D])
        const = sb("const", [P, NCONST])
        cols = sb("cols", [P, NCOL])
        rowsa = sb("rowsa", [P, NRA - 512])
        rowsb = sb("rowsb", [P, NRB - D])
        mod = sb("mod", [P, 48])
        gs = sb("gs", [P, 2, KD])
        lnst = sb("lnst", [P, 3, 20])
        neglam = sb("neglam", [P, 4])
        zero = sb("zero", [P, 1])
        eps = sb("eps", [P, 1])
        pos = sb("pos", [P, T], I32)

        ident = const[:, K_ID:K_ID + P]
        triu = const[:, K_TRIU:K_TRIU + P]
        maskt = const[:, K_MASK:K_MASK + P]
        ones = const[:, K_ONES:K_ONES + P]
        iota = const[:, K_IOTA:K_IOTA + 16]
        freq = const[:, K_FREQ:K_FREQ + 16]

        ring = cut(big, 0, WR, CH)
        hT = cut(big, WR * CH, KD, KEYS)
        qz = cut(r1, 0, 16, 512)
        kTa = cut(r1, 8192, 2, KEYS)
        kTb = cut(r1, 8192 + 2 * KEYS, 4, KEYS)
        va = cut(r2, 0, T + 1, 128)
        vb = cut(r2, 640, T + 1, 512)
        rope = cut(r2, 3200, 8, 5, HD)
        sqb = cut(r2, 5760, 2, 256)
        raw = cut(r2, 6272, 3, 256)
        xr = cut(r2, 7040, 256)
        ra = cut(r2, 7296, 256)
        rb = cut(r2, 7552, 256)
        tok = cut(r2, 7808, 3, 256)
        qst = cut(r2, 8576, 4, 3, 4)
        mixed = cut(r2, 8832, T, D)
        xmeta = cut(r2, 8832, D)
        ropec = cut(r2, 9856, 4, 5, HD)
        ropeg = cut(r2, 11136, 8, HD)
        xn = cut(r2, 12928, 2, D)
        prob = cut(r2, 12928, 4, KEYS)
        probT = cut(r2, 15040, 2, 640)
        sqo = cut(r2, 16320, 512)
        sst = sb("sst", [P, 4, 64])
        ost = sb("ost", [P, 3, 16])
        coef = sb("coef", [P, 32])
        aT = cut(r1, 0, NF, 512)
        sg = cut(r2, 8832, 2, 512)
        adar = cut(r2, 0, 4, D)
        crow = cut(r2, 4096, D)
        ctmp = cut(r2, 5120, D)
        gbc = cut(r2, 6144, KD, P)
        kT_mla = cut(r1, 0, 8, 512)
        kT_fox = cut(r1, 4096, 8, 512)
        v_fox = cut(r1, 8192, T, 512)
        qT_mla = cut(r2, 0, 8, 512)
        qT_fox = cut(r2, 4096, 8, 512)
        v_mla = cut(r2, 8192, T, 512)
        lat = cut(r2, 10240, T, LAT)
        qtok = cut(r2, 12960, 8, MLA_QK)
        ktok = cut(r2, 13728, 8, MLA_QK)
        ftok = cut(r2, 14496, 4, 4, P)
        fsq = cut(r2, 16544, 256)
        fraw = cut(r2, 16800, 2, 256)
        mixed2 = cut(r2, 10240, T, D)
        latn = cut(big, WR * CH, 640)
        latT = cut(big, WR * CH + 640, 2, 5 * P)
        msq = cut(big, WR * CH + 1920, 8, MLA_QK)
        rp = cut(big, WR * CH + 2688, 4, 8, 16)
        prob2 = cut(big, WR * CH, 4, 512)
        probT2 = cut(big, WR * CH + 2048, 2, 512)
        trig = cut(r1, 10240, 5, T * 16)
        fst = cut(r1, 10560, 3, 16, 4)
        mst = cut(r1, 10752, 3, T, 16)
        logf = cut(r1, 10944, 3, 32)
        fcum = cut(r1, 11040, 2, T, 8)
        lst = cut(r1, 11104, 3, 8)
        sst2 = sst
        qpT = cut(r1, 0, 16, 512)
        subk = cut(r1, 8192, 16, P)
        sc = cut(r2, 0, T, 2048)
        h2 = cut(r2, 8192, T, D)
        gtmp = cut(r2, 0, 2, 256)
        xn4 = cut(r2, 12288, 2, D)
        oh = cut(r2, 12288, PH, TOPK * 16)
        sc2 = cut(r2, 14336, P)
        cand = cut(r2, 14464, 2, 256)
        topv = cut(r2, 14976, PH, 2, TOPK)
        topf = cut(r2, 15232, PH, 2, TOPK)
        topi = cut(r1, 0, PH, 2, TOPK).bitcast(U32)
        bestv = cut(r2, 15488, PH, TOPK)
        besti = cut(r1, 256, PH, TOPK).bitcast(U32)
        bits = cut(r1, 384, 2, SLOTS).bitcast(U32)
        bitf = cut(r2, 15616, 2, SLOTS)
        e12 = cut(r2, 15872, 2, SLOTS)
        gate = cut(r2, 16128, 2, SLOTS)
        gst = cut(r2, 16384, 2, PH)
        dots = cut(r2, 16400, SLOTS)
        dstage = cut(r2, 16528, TOPK)
        wts = cut(r2, 16544, 2, SLOTS)
        diag = cut(r2, 16800, 4, P)
        idx = cut(r1, 640, T, SLOTS).bitcast(U32)
        istage = sb("istage", [P, 2 * TOPK], U32)
        zmat = cut(r1, 1152, P)
        rows = cut(big, 0, 16, D)

        x_in_s = [sem(f"x_in{t}") for t in range(5)]
        const_in_s, rope_in_s, rowsb_in_s = sem("const_in_s"), sem("rope_in_s"), sem("rowsb_in_s")
        crow_in_s, subk_in_s = sem("crow_in_s"), sem("subk_in_s")
        w_load = [sem(f"w_load{i}") for i in range(WR)]
        w_used = sem("w_used")
        setup_pool, setup_dve, rope_ready = sem("setup_pool"), sem("setup_dve"), sem("rope_ready")
        ln_rms, ln_xn, ln_tr, ln_hT = sem("ln_rms"), sem("ln_xn"), sem("ln_tr"), sem("ln_hT")
        pj_acc, pj_raw, pj_red, pj_rms, pj_tok, pj_tr, pj_ev = (
            sem(n) for n in ("pj_acc", "pj_raw", "pj_red", "pj_rms", "pj_tok", "pj_tr", "pj_ev"))
        s_ready, max_ready, exp_done, comb_done, pt_ready, pta_done, ptb_done, av_ready, o_done = (
            sem(n) for n in ("s_ready", "max_ready", "exp_done", "comb_done", "pt_ready", "pta_done",
                             "ptb_done", "av_ready", "o_done"))
        lam_dve, lam_act = sem("lam_dve"), sem("lam_act")
        sub_sq, sub_rms, mix_ready = sem("sub_sq"), sem("sub_rms"), sem("mix_ready")
        mixt_tr, mixt_ev = sem("mixt_tr"), sem("mixt_ev")
        out_acc, out_add = sem("out_acc"), sem("out_add")
        gu_acc, silu_done, act_ready = sem("gu_acc"), sem("silu_done"), sem("act_ready")
        down_acc, down_add = sem("down_acc"), sem("down_add")
        ada_load = [sem(f"ada_load{i}") for i in range(4)]
        ada_used, c_exp, gbc_ready, gate_acc, gate_ev = (
            sem(n) for n in ("ada_used", "c_exp", "gbc_ready", "gate_acc", "gate_ev"))
        p2_acc, p2_ev = sem("p2_acc"), sem("p2_ev")
        fx_red, fx_rms, fx_tok, fx_tr, fx_ev = (sem(n) for n in ("fx_red", "fx_rms", "fx_tok", "fx_tr", "fx_ev"))
        fc_y, fc_exp, fc_ln, fc_log, fc_acc, fc_ready, ang_ready, trig_ready = (
            sem(n) for n in ("fc_y", "fc_exp", "fc_ln", "fc_log", "fc_acc", "fc_ready", "ang_ready", "trig_ready"))
        la_rms, la_n, la_tr, la_T, la_acc, la_ev = (
            sem(n) for n in ("la_rms", "la_n", "la_tr", "la_T", "la_acc", "la_ev"))
        mq_red, mq_rms, mq_tok, mq_tr, mq_ev = (sem(n) for n in ("mq_red", "mq_rms", "mq_tok", "mq_tr", "mq_ev"))
        s2_ready, max2, exp2, pt2, pt2_done, av2, o2_done = (
            sem(n) for n in ("s2_ready", "max2", "exp2", "pt2", "pt2_done", "av2", "o2_done"))
        h2_tr, h2_ev, qp_acc, qp_ev, sk_acc, sk_ev = (
            sem(n) for n in ("h2_tr", "h2_ev", "qp_acc", "qp_ev", "sk_acc", "sk_ev"))
        best_ready, gate_exp, idx_ready, dots_done, gelu_done, w_ready = (
            sem(n) for n in ("best_ready", "gate_exp", "idx_ready", "dots_done", "gelu_done", "w_ready"))
        row_in = [sem(f"row_in{i}") for i in range(16)]
        slot_free = [sem(f"slot_free{i}") for i in range(16)]
        staged, diag_ready, y_acc, y_ready, y_out, issued = (
            sem(n) for n in ("staged", "diag_ready", "y_acc", "y_ready", "y_out", "issued"))

        pj_jobs = [(n, t) for n in range(9) for t in range(T + (n in (2, 5, 6, 7, 8)))]
        QK = sum(n < 7 for n, _ in pj_jobs)
        ln_base = [0, 5, 9, 13]

        def chunk(eng, c):
            eng.wait_ge(w_load[c % WR], 16 * (c // WR + 1))

        def rows_of(t):
            return P if t < T else META

        pv_jobs = []
        for t in range(T):
            for h in range(8):
                pv_jobs.append((t, 16 * t + h, 1, h))
            for h in range(4):
                pv_jobs.append((t, 16 * t + 8 + 2 * h, 2, h))
        pv_of = {s + j: i for i, (t, s, n, h) in enumerate(pv_jobs) for j in range(n)}
        NPV = len(pv_jobs)

        block = ctx.enter_context(nc.Block())

        @block.sync
        def _(sp):
            for t in range(T):
                sp.dma_start(x[:, t, :], x_in[t]).then_inc(x_in_s[t], 16)
            for c in range(WR):
                sp.dma_start(ring[:, c, :], wst[c]).then_inc(w_load[c], 16)
            whole = (NCHUNK - WR) // WR
            with sp.Fori(0, whole) as i:
                for c in range(WR):
                    sp.wait_ge(w_used, i * WR + (c + 1))
                    sp.dma_start(ring[:, c, :], wst[bass.ds(i * WR + (WR + c), 1), :, :].rearrange("a p n -> p (a n)")
                                 ).then_inc(w_load[c], 16)
            for c in range(WR * (whole + 1), NCHUNK):
                sp.wait_ge(w_used, c - WR + 1)
                sp.dma_start(ring[:, c % WR, :], wst[c]).then_inc(w_load[c % WR], 16)
            for t in range(T):
                sp.wait_ge(y_ready, t + 1)
                sp.dma_start(out[t], x[:, t, :]).then_inc(y_out, 16)
            sp.wait_ge(y_out, 16 * T)

        @block.gpsimd
        def _(pool):
            pool.memset(qz, 0.0).then_inc(setup_pool, 1)
            pool.wait_ge(mixt_ev, T)
            pool.dma_start(crow, rowsb_in[:, RB_C:RB_C + D].broadcast_to([P, D])).then_inc(crow_in_s, 16)
            for m in range(48):
                if m >= 4:
                    pool.wait_ge(ada_used, m - 3)
                pool.dma_start(adar[:, m % 4, :], wada[m]).then_inc(ada_load[m % 4], 16)
            pool.wait_ge(gate_ev, 2)
            pool.wait_ge(ln_tr, 13)
            pool.memset(ftok, 0.0)
            pool.drain()
            pool.memset(ftok[:, 0:2, :, HD:HD + 1], 1.0)
            pool.memset(ftok[:, 2:4, :, HD + 1:HD + 2], 1.0)
            pool.drain().then_inc(setup_pool, 1)
            pool.wait_ge(av2, T * HEADS2)
            pool.dma_start(subk, subk_in).then_inc(subk_in_s, 16)

            pool.wait_ge(w_used, NCHUNK)
            pool.wait_ge(qp_ev, 16)
            for k in range(TOPK):
                pool.sem_inc(slot_free[k], 1)
            for t in range(T):
                pool.wait_ge(idx_ready, t + 1)
                for phase, table in ((0, peer_u), (1, peer_v)):
                    lap = (2 * t + phase) * PH
                    with pool.Fori(0, PH // 2) as pair:
                        for g in range(2):
                            stage = istage[:, g * TOPK:(g + 1) * TOPK]
                            pool.tensor_copy(stage, idx[:, t, bass.ds(pair * (2 * TOPK) + g * TOPK, TOPK)]).then_inc(staged, 1)
                            pool.wait_ge(staged, pair * 2 + (lap + g + 1))
                            pool.sem_inc(issued, 1)
                            for k in range(TOPK):
                                pool.wait_ge(slot_free[k], pair * 2 + (lap + g + 1))
                                pool.sem_inc(issued, 1)
                                pool.indirect_dma_start(
                                    rows[:, k, :], None, table,
                                    bass.IndirectOffsetOnAxis(ap=stage[:, k:k + 1], axis=0)
                                ).then_inc(row_in[k], 16)

        @block.scalar
        def _(act):
            act.dma_start(const[:], const_in).then_inc(const_in_s, 16)
            act.dma_start(cols[:], cols_in).then_inc(const_in_s, 16)
            act.dma_start(xmeta[0:META, :], meta_in).then_inc(x_in_s[4], 16)
            act.dma_start(ropec, rope_in).then_inc(rope_in_s, 16)
            act.dma_start(ropeg, rowsa_in[:, 0:512].broadcast_to([P, 512])).then_inc(rope_in_s, 16)
            act.dma_start(rowsa[:], rowsa_in[:, 512:NRA].broadcast_to([P, NRA - 512])).then_inc(rope_in_s, 16)
            act.dma_start(rowsb[:], rowsb_in[:, D:NRB].broadcast_to([P, NRB - D])).then_inc(rowsb_in_s, 16)
            act.dma_start(pos[:], pos_in).then_inc(rowsb_in_s, 16)

            def norm(layer, tiles, junk):
                for t in tiles:
                    o, n = ln_base[layer] + t, rows_of(t)
                    if layer == 0:
                        act.wait_ge(x_in_s[t], 16)
                        if t == 0:
                            act.wait_ge(setup_dve, 1)
                    elif layer == 2:
                        act.wait_ge(down_add, 2 * (t + 1))
                    else:
                        act.wait_ge(out_add, 16 * (layer // 3) + 12 + t + 1)
                    if t >= 2:
                        act.wait_ge(ln_tr, o - 1)
                    src = xmeta[0:n, :] if t == T else x[:, t, :]
                    act.activation(junk[0:n, t % 2, :], src, ACT.Square, scale=1 / 32, bias=zero[0:n, :],
                                   accum_out=lnst[0:n, 0, o:o + 1])
                    act.drain()
                    act.activation(lnst[0:n, 1, o:o + 1], lnst[0:n, 0, o:o + 1], ACT.Sqrt,
                                   bias=eps[0:n, :]).then_inc(ln_rms, 1)

            norm(0, range(T + 1), xn)

            def pj_sqrt(j):
                n, t = pj_jobs[j]
                r = rows_of(t)
                act.wait_ge(pj_red, j + 1)
                act.activation(qst[0:r, j % 4, 1, :], qst[0:r, j % 4, 0, :], ACT.Sqrt,
                               bias=eps[0:r, :]).then_inc(pj_rms, 1)

            def pj_evac(j):
                n, t = pj_jobs[j]
                r, s = rows_of(t), t * P
                act.wait_ge(pj_tr, j + 1)
                if j == 0:
                    act.wait_ge(setup_pool, 1)
                b = ps[:, j % 4, 0:256].rearrange("p (c n) -> p c n", c=2)
                if n in (0, 1, 3, 4):
                    h = 4 * n if n < 2 else 8 + 4 * (n - 3)
                    act.activation(qz[0:64, h:h + 4:2, s:s + P], b[0:64], ACT.Copy)
                    act.activation(qz[64:P, h + 1:h + 4:2, s:s + P], b[64:P], ACT.Copy).then_inc(pj_ev, 1)
                elif n == 2:
                    act.activation(kTa[:, :, s:s + r], b[:, :, 0:r], ACT.Copy).then_inc(pj_ev, 1)
                else:
                    act.activation(kTb[:, 2 * (n - 5):2 * (n - 5) + 2, s:s + r], b[:, :, 0:r],
                                   ACT.Copy).then_inc(pj_ev, 1)

            for j, (n, t) in enumerate(pj_jobs):
                r = rows_of(t)
                act.wait_ge(pj_acc, j + 1)
                b = ps[0:r, 4 + j % 4, 0:256]
                if n < 7:
                    w = P if n == 2 else 256
                    if j >= 2:
                        act.wait_ge(pj_red, j - 1)
                    if j >= 3:
                        act.wait_ge(pj_tok, j - 2)
                    act.activation(sqb[0:r, j % 2, 0:w], b[:, 0:w], ACT.Square, scale=1 / 8, bias=zero[0:r, :])
                    if n == 2:
                        act.activation(va[0:r, t, :], b[:, P:256], ACT.Copy)
                    act.activation(raw[0:r, j % 3, 0:w], b[:, 0:w], ACT.Copy)
                else:
                    act.activation(vb[0:r, t, (n - 7) * 256:(n - 6) * 256], b, ACT.Copy)
                act.drain().then_inc(pj_raw, 1)
                if 1 <= j <= QK:
                    pj_sqrt(j - 1)
                if 3 <= j < QK + 3:
                    pj_evac(j - 3)

            act.wait_ge(lam_dve, 1)
            act.activation(neglam[:, 2:4], neglam[:, 0:2], ACT.Exp, bias=zero[:]).then_inc(lam_act, 1)

            def softmax(s):
                act.wait_ge(max_ready, s + 1)
                if s >= 4:
                    act.wait_ge(pt_ready, pv_of[s - 4] + 1)
                act.activation(prob[:, s % 4, :].rearrange("p (a b) -> p a b", a=2),
                               ps[:, 2 * (s % 2):2 * (s % 2) + 2, 0:HALF], ACT.Exp, scale=SCALE,
                               bias=sst[:, 1, s:s + 1], accum_out=sst[:, 2, s:s + 1])
                act.drain().then_inc(exp_done, 1)

            def prob_evac(p):
                act.wait_ge(pt_ready, p + 1)
                if p >= 2:
                    act.wait_ge(av_ready, p - 1)
                act.activation(probT[:, p % 2, 0:512], ps[:, 4 + p % 2, :], ACT.Copy).then_inc(pta_done, 1)

            for i in range(NPV + 1):
                if i < NPV:
                    _, s, n, _ = pv_jobs[i]
                    for j in range(n):
                        softmax(s + j)
                if i >= 1:
                    prob_evac(i - 1)

            for t in range(T):
                act.wait_ge(sub_sq, t + 1)
                act.activation(ost[:, 1, 4 * t:4 * t + 4], ost[:, 0, 4 * t:4 * t + 4], ACT.Sqrt,
                               bias=eps[:], scale=1 / 128).then_inc(sub_rms, 1)
            for t in range(T):
                act.wait_ge(mixt_tr, t + 1)
                act.activation(hT[:, :, t * P:(t + 1) * P],
                               ps[:, 2 * (t % 2):2 * (t % 2) + 2, :].rearrange("p a (b n) -> p (a b) n", n=P),
                               ACT.Copy).then_inc(mixt_ev, 1)

            act.wait_ge(crow_in_s, 16)
            act.activation(ctmp, crow, ACT.Exp, scale=-1.0, bias=zero[:]).then_inc(c_exp, 1)

            norm(1, range(T), xn)

            for f in range(NF):
                act.wait_ge(gu_acc, f + 1)
                if f >= 2:
                    act.wait_ge(act_ready, f - 1)
                act.activation(sg[:, f % 2, :], ps[:, 2 * (f % 2), :], ACT.Silu, bias=zero[:]).then_inc(silu_done, 1)
            for g in range(2):
                act.wait_ge(gate_acc, g + 1)
                act.activation(gates[:, g, :].rearrange("p (a b) -> p a b", a=2),
                               ps[:, 4 + 2 * g:6 + 2 * g, :], ACT.Copy).then_inc(gate_ev, 1)

            norm(2, range(T), xn)

            act.wait_ge(ang_ready, 1)
            act.activation(trig[:, 0:2, :], trig[:, 2:4, :], ACT.Sin, bias=zero[:]).then_inc(trig_ready, 1)

            def fx_sqrt(k):
                act.wait_ge(fx_red, k + 1)
                act.activation(fst[:, 1, k, :], fst[:, 0, k, :], ACT.Sqrt, bias=eps[:]).then_inc(fx_rms, 1)

            def fx_evac(k):
                n, t = 3 + k // T, k % T
                dst = qT_fox if n < 5 else kT_fox
                h = 4 * ((n - 3) % 2)
                act.wait_ge(fx_tr, k + 1)
                act.activation(dst[:, h:h + 4, t * P:(t + 1) * P],
                               ps[:, k % 4, :].rearrange("p (a n) -> p a n", a=4), ACT.Copy).then_inc(fx_ev, 1)

            for j in range(9 * T):
                n, t = j // T, j % T
                k = j - 3 * T
                act.wait_ge(p2_acc, j + 1)
                b = ps[:, 4 + j % 4, 0:256]
                if n < 3:
                    w = 256 if n < 2 else LAT - 512
                    act.activation(lat[:, t, 256 * n:256 * n + w], b[:, 0:w], ACT.Copy)
                elif n < 7:
                    if k >= 1:
                        act.wait_ge(fx_red, k)
                    if k >= 2:
                        act.wait_ge(fx_tok, k - 1)
                    act.activation(fsq, b, ACT.Square, scale=1 / 8, bias=zero[:])
                    act.activation(fraw[:, k % 2, :], b, ACT.Copy)
                else:
                    act.activation(v_fox[:, t, 256 * (n - 7):256 * (n - 6)], b, ACT.Copy)
                act.drain().then_inc(p2_ev, 1)
                if n == 2 and t == T - 1:
                    act.wait_ge(fc_y, 1)
                    act.activation(logf[:, 1, :], logf[:, 1, :], ACT.Exp, bias=zero[:])
                    act.drain()
                    act.activation(logf[:, 1, :], logf[:, 1, :], ACT.Ln, bias=ones[:, 0:1]).then_inc(fc_ln, 1)
                if 1 <= k <= 16:
                    fx_sqrt(k - 1)
                if 3 <= k < 19:
                    fx_evac(k - 3)

            act.wait_ge(p2_acc, 9 * T)
            junk = msq.rearrange("p a b -> p (a b)")
            for t in range(T):
                for i, (at, n) in enumerate(((0, QR), (QR, KVR))):
                    act.drain()
                    act.activation(junk[:, 0:n], lat[:, t, at:at + n], ACT.Square, scale=n ** -0.5, bias=zero[:],
                                   accum_out=lst[:, 0, 2 * t + i:2 * t + i + 1])
            act.drain()
            act.activation(lst[:, 1, :], lst[:, 0, :], ACT.Sqrt, bias=eps[:]).then_inc(la_rms, 1)
            for t in range(T):
                act.wait_ge(la_acc, t + 1)
                if t >= 1:
                    act.wait_ge(mq_tr, 4 * t)
                act.activation(qtok, ps[:, 2:4, 0:384].rearrange("p a (b n) -> p a b n", n=MLA_QK), ACT.Copy)
                kv = ps[:, 4:6, :].rearrange("p a (b n) -> p (a b) n", n=P)
                act.activation(ktok[:, :, 0:64], kv[:, :, 0:64], ACT.Copy)
                act.activation(v_mla[:, t, :].rearrange("p (h n) -> p h n", h=8), kv[:, :, 64:P], ACT.Copy)
                act.drain().then_inc(la_ev, 1)
                act.wait_ge(mq_red, t + 1)
                act.activation(mst[:, 1, t, :], mst[:, 0, t, :], ACT.Sqrt, bias=eps[:],
                               scale=1 / MLA_QK).then_inc(mq_rms, 1)
                for g in range(4):
                    dst = qT_mla if g < 2 else kT_mla
                    act.wait_ge(mq_tr, 4 * t + g + 1)
                    act.activation(dst[0:MLA_QK, 4 * (g % 2):4 * (g % 2) + 4, t * P:(t + 1) * P],
                                   ps[0:MLA_QK, 6 + g % 2, :].rearrange("p (a n) -> p a n", a=4),
                                   ACT.Copy).then_inc(mq_ev, 1)

            for i in range(T * HEADS2 + 1):
                if i < T * HEADS2:
                    t, h = i // HEADS2, i % HEADS2
                    act.wait_ge(max2, i + 1)
                    if i >= 4:
                        act.wait_ge(pt2, i - 3)
                    act.activation(prob2[:, i % 4, 0:(t + 1) * P], ps[:, i % 2, 0:(t + 1) * P], ACT.Exp,
                                   scale=MLA_SCALE if h < 8 else SCALE, bias=sst2[:, 1, i:i + 1],
                                   accum_out=sst2[:, 2, i:i + 1])
                    act.drain().then_inc(exp2, 1)
                if i >= 1:
                    u = i - 1
                    act.wait_ge(pt2, u + 1)
                    if u >= 2:
                        act.wait_ge(av2, u - 1)
                    n = (u // HEADS2 + 1) * P
                    act.activation(probT2[:, u % 2, 0:n], ps[:, 2 + u % 2, 0:n], ACT.Copy).then_inc(pt2_done, 1)

            for t in range(T):
                act.wait_ge(mixt_tr, T + t + 1)
                act.activation(hT[:, :, t * P:(t + 1) * P],
                               ps[:, 2 * (t % 2):2 * (t % 2) + 2, :].rearrange("p a (b n) -> p (a b) n", n=P),
                               ACT.Copy).then_inc(mixt_ev, 1)

            norm(3, range(T), xn4)
            for t in range(T):
                act.wait_ge(h2_tr, t + 1)
                act.activation(h2[:, t, :].rearrange("p (a b) -> p a b", a=2),
                               ps[:, 4 + 2 * (t % 2):6 + 2 * (t % 2), :], ACT.Copy).then_inc(h2_ev, 1)
            for c in range(17):
                if c < 16:
                    act.wait_ge(qp_acc, c + 1)
                    act.activation(qpT[:, c, :], ps[:, c % 4, :], ACT.Copy).then_inc(qp_ev, 1)
                if c >= 1:
                    act.wait_ge(sk_acc, c)
                    act.activation(sc[:, :, (c - 1) * P:c * P],
                                   ps[:, 4 + (c - 1) % 4, :].rearrange("p (t n) -> p t n", t=T),
                                   ACT.Copy).then_inc(sk_ev, 1)
            act.wait_ge(best_ready, 1)
            act.activation(gate[:, 0, :], gate[:, 0, :], ACT.Exp, bias=zero[:]).then_inc(gate_exp, 1)
            for t in range(T):
                act.wait_ge(dots_done, PH * (t + 1))
                act.activation(dots, dots, ACT.Gelu_apprx_tanh, bias=zero[:]).then_inc(gelu_done, 1)
                if t + 1 < T:
                    act.wait_ge(best_ready, t + 2)
                    act.activation(gate[:, (t + 1) % 2, :], gate[:, (t + 1) % 2, :], ACT.Exp,
                                   bias=zero[:]).then_inc(gate_exp, 1)
                act.wait_ge(w_ready, t + 1)
                with act.Fori(0, PH) as h:
                    for k in range(TOPK):
                        if k >= 4:
                            act.wait_ge(slot_free[k - 4], h + ((2 * t + 1) * PH + 2))
                        else:
                            act.wait_ge(slot_free[k + 12], h + ((2 * t + 1) * PH + 1))
                        act.activation(diag[:, k % 4, :], ident, ACT.Copy,
                                       scale=wts[:, t % 2, bass.ds(h * TOPK + k, 1)]).then_inc(diag_ready, 1)

        @block.vector
        def _(v):
            v.memset(zero[:], 0.0)
            v.memset(eps[:], EPS)
            v.drain().then_inc(setup_dve, 1)

            def norm(layer, tiles, buf):
                tiles = list(tiles)

                def scaled(t):
                    o, n = ln_base[layer] + t, rows_of(t)
                    v.wait_ge(ln_rms, o + 1)
                    v.reciprocal(lnst[0:n, 2, o:o + 1], lnst[0:n, 1, o:o + 1])
                    v.drain()
                    src = xmeta[0:n, :] if t == T else x[:, t, :]
                    v.tensor_scalar(buf[0:n, t % 2, :], src, lnst[0:n, 2, o:o + 1], None, ALU.mult).then_inc(ln_xn, 1)

                def evac(t):
                    o, n = ln_base[layer] + t, rows_of(t)
                    v.wait_ge(ln_tr, o + 1)
                    b = 2 * (t % 2)
                    src = ps[:, b:b + 2, :].rearrange("p a (b n) -> p (a b) n", n=P)[:, :, 0:n]
                    dst = hT[:, :, t * P:t * P + n]
                    g = [cols[:, C_G1:C_G1 + KD], cols[:, C_GF:C_GF + KD], gs[:, 0, :], gs[:, 1, :]][layer]
                    if layer < 2:
                        v.tensor_tensor(dst, src, over(g, n), ALU.mult).then_inc(ln_hT, 1)
                    else:
                        shift = mod[:, 24 * (layer - 2):24 * (layer - 2) + KD]
                        v.tensor_tensor(dst, src, over(g, n), ALU.mult)
                        v.drain()
                        v.tensor_tensor(dst, dst, over(shift, n), ALU.add).then_inc(ln_hT, 1)

                for t in tiles:
                    scaled(t)
                    if t:
                        evac(t - 1)
                evac(tiles[-1])

            v.wait_ge(const_in_s, 32)
            norm(0, range(T + 1), xn)
            v.wait_ge(rope_in_s, 48)
            for kind in range(4):
                for sw in range(2):
                    v.tensor_tensor(rope[:, 2 * kind + sw], ropec[:, 2 * (kind // 2) + sw],
                                    each(ropeg[:, 2 * kind + sw, :], 5), ALU.mult)
            v.drain()

            def pj_reduce(j):
                n, t = pj_jobs[j]
                r, hh = rows_of(t), 2 if n == 2 else 4
                v.wait_ge(pj_raw, j + 1)
                v.tensor_reduce(qst[0:r, j % 4, 0, 0:hh],
                                sqb[0:r, j % 2, 0:64 * hh].rearrange("p (h d) -> p h d", h=hh), AX.X, ALU.add)
                if hh == 2:
                    v.memset(qst[0:r, j % 4, 0, 2:4], 1.0)
                v.drain().then_inc(pj_red, 1)

            def pj_rope(j):
                n, t = pj_jobs[j]
                r, hh = rows_of(t), 2 if n == 2 else 4
                kind = (0, 0, 1, 2, 2, 3, 3)[n]
                w = 64 * hh
                v.wait_ge(pj_rms, j + 1)
                v.reciprocal(qst[0:r, j % 4, 2, 0:hh], qst[0:r, j % 4, 1, 0:hh])
                v.drain()
                src = raw[0:r, j % 3, 0:w].rearrange("p (h d) -> p h d", h=hh)
                a = xr[0:r, 0:w].rearrange("p (h d) -> p h d", h=hh)
                v.tensor_tensor(a, src, over(qst[0:r, j % 4, 2, 0:hh], HD), ALU.mult)
                v.drain()
                straight = ra[0:r, 0:w].rearrange("p (h d) -> p h d", h=hh)
                swapped = rb[0:r, 0:w].rearrange("p (h i two) -> p h i two", h=hh, two=2)
                a2 = xr[0:r, 0:w].rearrange("p (h i two) -> p h i two", h=hh, two=2)
                tb = rope[0:r, 2 * kind + 1, t, :].rearrange("p (i two) -> p i two", two=2)
                v.tensor_tensor(straight, a, each(rope[0:r, 2 * kind, t, :], hh), ALU.mult)
                v.tensor_tensor(swapped[:, :, :, 0], a2[:, :, :, 1], each(tb[:, :, 0], hh), ALU.mult)
                v.tensor_tensor(swapped[:, :, :, 1], a2[:, :, :, 0], each(tb[:, :, 1], hh), ALU.mult)
                v.drain()
                if j >= 3:
                    v.wait_ge(pj_tr, j - 2)
                if n == 2:
                    dst = tok[0:r, j % 3, :].rearrange("p (h two d) -> p h two d", h=2, two=2)
                    rb3 = rb[0:r, 0:w].rearrange("p (h d) -> p h d", h=hh)
                    v.tensor_tensor(dst[:, :, 0, :], straight, rb3, ALU.add)
                    v.tensor_tensor(dst[:, :, 1, :], straight, rb3, ALU.add)
                    v.drain().then_inc(pj_tok, 1)
                else:
                    v.tensor_tensor(tok[0:r, j % 3, :], ra[0:r, :], rb[0:r, :], ALU.add).then_inc(pj_tok, 1)
                    v.drain()

            for j in range(QK + 1):
                if j < QK:
                    pj_reduce(j)
                if j >= 1:
                    pj_rope(j - 1)

            lq = rowsa[:, RA_LAM - 512:RA_LAM - 256].rearrange("p (a d) -> p a d", a=4)
            v.tensor_tensor(xr[:, 0:64], lq[:, 0, :], lq[:, 1, :], ALU.mult)
            v.tensor_tensor(xr[:, 64:128], lq[:, 2, :], lq[:, 3, :], ALU.mult)
            v.drain()
            v.tensor_reduce(neglam[:, 0:2], xr[:, 0:128].rearrange("p (a d) -> p a d", a=2), AX.X,
                            ALU.add).then_inc(lam_dve, 1)
            v.wait_ge(lam_act, 1)
            v.tensor_tensor(neglam[:, 0:1], neglam[:, 3:4], neglam[:, 2:3], ALU.subtract)
            v.drain()
            v.tensor_scalar(neglam[:, 1:2], neglam[:, 0:1], LAM_INIT, None, ALU.subtract)
            v.drain()

            def score_max(s):
                v.wait_ge(s_ready, s + 1)
                v.tensor_reduce(sst[:, 0, s:s + 1], ps[:, 2 * (s % 2):2 * (s % 2) + 2, 0:HALF], AX.XY, ALU.max)
                v.drain()
                v.tensor_scalar(sst[:, 1, s:s + 1], sst[:, 0, s:s + 1], -SCALE, None, ALU.mult).then_inc(max_ready, 1)

            def finish_probs(i):
                t, s, n, h = pv_jobs[i]
                v.wait_ge(exp_done, s + n)
                v.reciprocal(sst[:, 3, s:s + n], sst[:, 2, s:s + n])
                v.drain()
                if n == 2:
                    c = 4 * t + h
                    v.tensor_scalar(coef[:, c:c + 1], sst[:, 2, s:s + 1], sst[:, 3, s + 1:s + 2], neglam[:, 1:2],
                                    ALU.mult, ALU.mult)
                    v.drain()
                    v.scalar_tensor_tensor(out=prob[:, s % 4, :], in0=prob[:, (s + 1) % 4, :], scalar=coef[:, c:c + 1],
                                           in1=prob[:, s % 4, :], op0=ALU.mult, op1=ALU.add)
                    v.drain().then_inc(comb_done, 1)

            def meta_probs(i):
                v.wait_ge(pt_ready, i + 1)
                if i >= 2:
                    v.wait_ge(av_ready, i - 1)
                v.tensor_copy(probT[0:META, i % 2, 512:640], ps[0:META, 6 + i % 2, 0:P]).then_inc(ptb_done, 1)

            def head_out(i):
                t, s, n, h = pv_jobs[i]
                v.wait_ge(av_ready, i + 1)
                o = P
                if n == 1:
                    o += 64 * (h // 4)
                    v.tensor_scalar(mixed[:, t, 64 * h:64 * h + 64], ps[:, 6 + i % 2, o:o + 64], sst[:, 3, s:s + 1], None,
                                    ALU.mult).then_inc(o_done, 1)
                else:
                    at = 512 + P * h
                    v.tensor_scalar(mixed[:, t, at:at + P], ps[:, 6 + i % 2, o:o + P], sst[:, 3, s:s + 1], None,
                                    ALU.mult).then_inc(o_done, 1)

            for i in range(NPV + 2):
                if i < NPV:
                    _, s, n, _ = pv_jobs[i]
                    for j in range(n):
                        score_max(s + j)
                if i >= 1 and i - 1 < NPV:
                    finish_probs(i - 1) if i - 1 < 0 else None
                if i < NPV:
                    finish_probs(i)
                if 1 <= i <= NPV:
                    meta_probs(i - 1)
                if i >= 2:
                    head_out(i - 2)

            for t in range(T):
                o = mixed[:, t, 512:D]
                v.drain()
                v.tensor_tensor(sqo, o, o, ALU.mult)
                v.drain()
                v.tensor_reduce(ost[:, 0, 4 * t:4 * t + 4], sqo.rearrange("p (h d) -> p h d", h=4), AX.X,
                                ALU.add).then_inc(sub_sq, 1)
            for t in range(T):
                o = mixed[:, t, 512:D].rearrange("p (h d) -> p h d", h=4)
                v.wait_ge(sub_rms, t + 1)
                v.reciprocal(ost[:, 2, 4 * t:4 * t + 4], ost[:, 1, 4 * t:4 * t + 4])
                v.drain()
                v.tensor_tensor(o, o, over(ost[:, 2, 4 * t:4 * t + 4], P), ALU.mult)
                v.drain()
                v.scalar_tensor_tensor(out=o, in0=o, scalar=1.0 - LAM_INIT,
                                       in1=each(rowsa[:, 0:P], 4), op0=ALU.mult, op1=ALU.mult).then_inc(mix_ready, 1)

            for j in range(4 * T):
                n, t = j // T, j % T
                v.wait_ge(out_acc, j + 1)
                xs = x[:, t, 256 * n:256 * n + 256]
                v.tensor_tensor(xs, xs, ps[:, 4 + j % 4, 0:256], ALU.add).then_inc(out_add, 1)

            norm(1, range(T), xn)

            v.wait_ge(c_exp, 1)
            v.tensor_scalar(ctmp, ctmp, 1.0, None, ALU.add)
            v.drain()
            v.reciprocal(ctmp, ctmp)
            v.drain()
            v.tensor_tensor(crow, crow, ctmp, ALU.mult)
            v.drain()

            def modulation(m):
                v.wait_ge(ada_load[m % 4], 16 * (m // 4 + 1))
                v.tensor_tensor_reduce(out=adar[:, m % 4, :], in0=adar[:, m % 4, :], in1=crow, scale=1.0, scalar=0.0,
                                       op0=ALU.mult, op1=ALU.add, accum_out=mod[:, m:m + 1])
                v.drain().then_inc(ada_used, 1)

            for f in range(NF):
                v.wait_ge(silu_done, f + 1)
                v.tensor_tensor(aT[:, f, :], sg[:, f % 2, :], ps[:, 2 * (f % 2) + 1, :], ALU.mult).then_inc(act_ready, 1)
                for m in range(3 * f, min(3 * f + 3, 48)):
                    modulation(m)
            v.tensor_tensor(mod[:], mod[:], cols[:, C_BADA:C_BADA + 48], ALU.add)
            v.drain()
            for g in range(2):
                scale = mod[:, 24 * g + KD:24 * g + 2 * KD]
                gain = cols[:, C_N1 + KD * g:C_N1 + KD * g + KD]
                v.scalar_tensor_tensor(out=gs[:, g, :], in0=scale, scalar=1.0, in1=gain, op0=ALU.add, op1=ALU.mult)
                if g:
                    v.wait_ge(gate_acc, 1)
                v.tensor_copy(gbc, over(mod[:, 24 * g + 16:24 * g + 24], P)).then_inc(gbc_ready, 1)

            for t in range(T):
                for half in range(2):
                    v.wait_ge(down_acc, 2 * t + half + 1)
                    xs = x[:, t, 512 * half:512 * half + 512]
                    v.tensor_tensor(xs, xs, ps[:, 2 * t + half, :], ALU.add).then_inc(down_add, 1)

            norm(2, range(T), xn)

            v.wait_ge(rowsb_in_s, 32)
            posf = fst[:, 0, 0, :]
            v.tensor_copy(posf, pos[:])
            v.drain()
            ang, turn = trig[:, 4, :], trig[:, 0, :]
            v.tensor_tensor(ang.rearrange("p (t f) -> p t f", t=T), over(posf, 16), each(freq, T), ALU.mult)
            v.drain()
            for q, quarter in ((2, 0.25), (3, 0.0)):
                red = trig[:, q, :]
                v.tensor_scalar(turn, ang, 1.0 / TWO_PI, quarter, ALU.mult, ALU.add)
                v.drain()
                v.tensor_scalar(turn, turn, ROUND, None, ALU.add)
                v.drain()
                v.tensor_scalar(turn, turn, ROUND, None, ALU.subtract)
                v.drain()
                src = ang
                for part in (PI2_A, PI2_B, PI2_C):
                    v.scalar_tensor_tensor(out=red, in0=turn, scalar=-part, in1=src, op0=ALU.mult, op1=ALU.add)
                    v.drain()
                    src = red
                if quarter:
                    v.tensor_scalar(red, red, float(np.pi / 2), None, ALU.add)
                    v.drain()
                v.tensor_scalar(red, red, PI_F, -PI_F, ALU.min, ALU.max)
                v.drain()
            v.drain().then_inc(ang_ready, 1)

            v.wait_ge(p2_ev, 3 * T)
            y = logf[:, 0, :]
            v.tensor_tensor(y.rearrange("p (t h) -> p t h", t=T), lat[:, :, 672:680],
                            each(rowsb[:, RB_BF - D:RB_BF - D + 8], T), ALU.add)
            v.drain()
            v.scalar_tensor_tensor(out=logf[:, 1, :], in0=y, scalar=-1.0, in1=y, op0=ALU.mult, op1=ALU.min).then_inc(fc_y, 1)
            v.wait_ge(fc_ln, 1)
            v.tensor_scalar(logf[:, 2, :], y, 0.0, None, ALU.min)
            v.drain()
            v.tensor_tensor(logf[:, 2, :], logf[:, 2, :], logf[:, 1, :], ALU.subtract).then_inc(fc_log, 1)
            v.wait_ge(fc_acc, 1)
            f8 = ps[:, 3, 0:32].rearrange("p (t h) -> p t h", t=T)
            v.tensor_scalar(fcum[:, 0], f8, 8.0, None, ALU.mult)
            v.tensor_scalar(fcum[:, 1], f8, -8.0, None, ALU.mult)
            v.drain().then_inc(fc_ready, 1)

            v.wait_ge(setup_pool, 2)
            for k in range(17):
                if k < 16:
                    v.wait_ge(p2_ev, 3 * T + k + 1)
                    v.tensor_reduce(fst[:, 0, k, :], fsq.rearrange("p (h d) -> p h d", h=4), AX.X, ALU.add).then_inc(fx_red, 1)
                if k >= 1:
                    q = k - 1
                    n, t = 3 + q // T, q % T
                    isk = n >= 5
                    g = rowsb[:, (RB_FK if isk else RB_FQ) - D:][:, 0:64]
                    v.wait_ge(fx_rms, q + 1)
                    v.reciprocal(fst[:, 2, q, :], fst[:, 1, q, :])
                    v.drain()
                    src = fraw[:, q % 2, :].rearrange("p (h d) -> p h d", h=4)
                    v.tensor_tensor(src, src, over(fst[:, 2, q, :], HD), ALU.mult)
                    if q >= 2:
                        v.wait_ge(fx_tr, q - 1)
                    else:
                        v.drain()
                    buf = ftok[:, 2 * isk + q % 2]
                    v.drain()
                    v.tensor_tensor(buf[:, :, 0:64], src, each(g, 4), ALU.mult)
                    at = HD if isk else HD + 1
                    h = 4 * ((n - 3) % 2)
                    v.tensor_copy(buf[:, :, at], fcum[:, 1 if isk else 0, t, h:h + 4])
                    v.drain().then_inc(fx_tok, 1)

            v.wait_ge(la_rms, 1)
            v.reciprocal(lst[:, 2, :], lst[:, 1, :])
            v.drain()
            v.wait_ge(trig_ready, 1)
            for t in range(T):
                if t:
                    v.wait_ge(la_tr, t)
                v.tensor_scalar(latn[:, 0:QR], lat[:, t, 0:QR], lst[:, 2, 2 * t:2 * t + 1], None, ALU.mult)
                v.tensor_scalar(latn[:, QR:640], lat[:, t, QR:640], lst[:, 2, 2 * t + 1:2 * t + 2], None, ALU.mult)
                v.drain().then_inc(la_n, 1)
                v.wait_ge(la_tr, t + 1)
                dst = latT[:, t % 2, :].rearrange("p (a n) -> p a n", a=5)
                v.tensor_tensor(dst[:, 0:3], ps[:, 0, 0:QR].rearrange("p (a n) -> p a n", a=3),
                                over(cols[:, C_QA:C_QA + 3], P), ALU.mult)
                v.tensor_tensor(dst[:, 3:5], ps[:, 1, 0:KVR].rearrange("p (a n) -> p a n", a=2),
                                over(cols[:, C_KVA:C_KVA + 2], P), ALU.mult)
                v.drain().then_inc(la_T, 1)
                v.wait_ge(la_ev, t + 1)
                v.tensor_copy(ktok[:, :, 64:96], each(lat[:, t, 640:672], 8))
                v.tensor_tensor(msq, qtok, qtok, ALU.mult)
                v.drain()
                v.tensor_reduce(mst[:, 0, t, 0:8], msq, AX.X, ALU.add)
                v.drain()
                v.tensor_tensor(msq, ktok, ktok, ALU.mult)
                v.drain()
                v.tensor_reduce(mst[:, 0, t, 8:16], msq, AX.X, ALU.add)
                v.drain().then_inc(mq_red, 1)
                v.wait_ge(mq_rms, t + 1)
                v.reciprocal(mst[:, 2, t, :], mst[:, 1, t, :])
                v.drain()
                for i, (buf, row) in enumerate(((qtok, RB_MQ), (ktok, RB_MK))):
                    v.tensor_tensor(buf, buf, over(mst[:, 2, t, 8 * i:8 * i + 8], MLA_QK), ALU.mult)
                    v.drain()
                    v.tensor_tensor(buf, buf, each(rowsb[:, row - D:row - D + MLA_QK], 8), ALU.mult)
                    v.drain()
                    lo, hi = buf[:, :, 64:80], buf[:, :, 80:96]
                    cos = each(trig[:, 0, 16 * t:16 * t + 16], 8)
                    sin = each(trig[:, 1, 16 * t:16 * t + 16], 8)
                    v.tensor_tensor(rp[:, 0], lo, cos, ALU.mult)
                    v.tensor_tensor(rp[:, 1], hi, sin, ALU.mult)
                    v.tensor_tensor(rp[:, 2], hi, cos, ALU.mult)
                    v.tensor_tensor(rp[:, 3], lo, sin, ALU.mult)
                    v.drain()
                    v.tensor_tensor(lo, rp[:, 0], rp[:, 1], ALU.subtract)
                    v.tensor_tensor(hi, rp[:, 2], rp[:, 3], ALU.add)
                    v.drain()
                v.drain().then_inc(mq_tok, 1)

            for i in range(T * HEADS2 + 2):
                if i < T * HEADS2:
                    t, h = i // HEADS2, i % HEADS2
                    v.wait_ge(s2_ready, i + 1)
                    v.tensor_reduce(sst2[:, 0, i:i + 1], ps[:, i % 2, 0:(t + 1) * P], AX.X, ALU.max)
                    v.drain()
                    v.tensor_scalar(sst2[:, 1, i:i + 1], sst2[:, 0, i:i + 1], -MLA_SCALE if h < 8 else -SCALE, None,
                                    ALU.mult).then_inc(max2, 1)
                if i >= 2:
                    u = i - 2
                    t, h = u // HEADS2, u % HEADS2
                    v.wait_ge(exp2, u + 1)
                    v.reciprocal(sst2[:, 3, u:u + 1], sst2[:, 2, u:u + 1])
                    v.drain()
                    v.wait_ge(av2, u + 1)
                    o = 64 * (h % 2)
                    v.tensor_scalar(mixed2[:, t, 64 * h:64 * h + 64], ps[:, 4 + u % 2, o:o + 64], sst2[:, 3, u:u + 1],
                                    None, ALU.mult).then_inc(o2_done, 1)

            for j in range(4 * T):
                n, t = j // T, j % T
                v.wait_ge(out_acc, 4 * T + j + 1)
                b = ps[:, 4 + j % 4, 0:256]
                tmp = gtmp[:, j % 2, :]
                v.tensor_tensor(tmp, b, gates[:, 0, 256 * n:256 * n + 256], ALU.mult)
                v.drain()
                xs = x[:, t, 256 * n:256 * n + 256]
                v.tensor_tensor(xs, xs, tmp, ALU.add).then_inc(out_add, 1)
            v.drain()

            norm(3, range(T), xn4)

            def best(src, spare, vals, inds):
                v.max(vals[:, 0:8], src)
                v.drain()
                v.max_index(inds[:, 0:8], vals[:, 0:8], src)
                v.match_replace(out=spare, in_to_replace=vals[:, 0:8], in_values=src, imm_value=LOW)
                v.drain()
                v.max(vals[:, 8:16], spare)
                v.drain()
                v.max_index(inds[:, 8:16], vals[:, 8:16], spare)

            def choose(t):
                if t == 0:
                    v.wait_ge(sk_ev, 16)
                    v.wait_ge(h2_ev, T)
                    v.memset(zmat, 0.0)
                for h in range(PH):
                    for half in range(2):
                        c = 2 * h + half
                        best(sc[:, t, c * P:(c + 1) * P], sc2, topv[:, h, half, :], topi[:, h, half, :])
                        v.drain()
                v.tensor_copy(topf.rearrange("p a b c -> p (a b c)"), topi.rearrange("p a b c -> p (a b c)"))
                for h in range(PH):
                    v.tensor_tensor(cand[:, 0, :].rearrange("p (a b) -> p a b", a=TOPK), over(topv[:, h, 0, :], TOPK),
                                    each(topv[:, h, 1, :], TOPK), ALU.add)
                    v.drain()
                    best(cand[:, 0, :], cand[:, 1, :], bestv[:, h, :], besti[:, h, :])
                    v.drain()
                g3 = gate[:, t % 2, :].rearrange("p (h k) -> p h k", h=PH)
                v.tensor_tensor(g3, bestv, over(bestv[:, :, 0], TOPK), ALU.subtract).then_inc(best_ready, 1)
                bi = besti.rearrange("p h k -> p (h k)")
                v.tensor_scalar(bits[:, 0, :], bi, 4, None, ALU.logical_shift_right)
                v.tensor_scalar(bits[:, 1, :], bi, 15, None, ALU.bitwise_and)
                v.drain()
                v.tensor_copy(bitf, bits)
                v.drain()
                hot = oh.rearrange("p h (k j) -> p h k j", k=TOPK)
                for half in range(2):
                    b3 = bitf[:, half, :].rearrange("p (h k) -> p h k", h=PH)
                    v.tensor_tensor(hot, over(b3, 16),
                                    iota.unsqueeze(1).unsqueeze(1).broadcast_to([P, PH, TOPK, 16]), ALU.is_equal)
                    v.drain()
                    v.tensor_tensor(hot, hot, topf[:, :, half, :].unsqueeze(2).broadcast_to([P, PH, TOPK, 16]), ALU.mult)
                    v.drain()
                    v.tensor_reduce(e12[:, half, :].rearrange("p (h k) -> p h k", h=PH), hot, AX.X, ALU.add)
                    v.drain()
                v.scalar_tensor_tensor(out=bitf[:, 0, :], in0=e12[:, 0, :], scalar=float(NKEYS), in1=e12[:, 1, :],
                                       op0=ALU.mult, op1=ALU.add)
                v.drain()
                v.tensor_copy(idx[:, t, :], bitf[:, 0, :]).then_inc(idx_ready, 1)
                v.wait_ge(gate_exp, t + 1)
                v.tensor_reduce(gst[:, 0, :], g3, AX.X, ALU.add)
                v.drain()
                v.reciprocal(gst[:, 1, :], gst[:, 0, :])
                v.drain()
                v.tensor_tensor(g3, g3, over(gst[:, 1, :], TOPK), ALU.mult)
                v.drain()

            def finish(t):
                v.wait_ge(y_acc, t + 1)
                tmp = oh.rearrange("p a b -> p (a b)")[:, 0:D]
                b = 2 * (t % 2)
                v.tensor_tensor(tmp.rearrange("p (a b) -> p a b", a=2), ps[:, b:b + 2, :],
                                gates[:, 1, :].rearrange("p (a b) -> p a b", a=2), ALU.mult)
                v.drain()
                v.tensor_tensor(x[:, t, :], x[:, t, :], tmp, ALU.add).then_inc(y_ready, 1)
                v.drain()

            choose(0)
            for t in range(T):
                with v.Fori(0, PH) as h:
                    for k in range(TOPK):
                        v.wait_ge(row_in[k], h * 16 + (2 * t * PH + 1) * 16)
                        v.tensor_tensor_reduce(out=rows[:, k, :], in0=rows[:, k, :], in1=h2[:, t, :], scale=1.0,
                                               scalar=0.0, op0=ALU.mult, op1=ALU.add,
                                               accum_out=dstage[:, k:k + 1]).then_inc(slot_free[k], 1)
                    v.drain()
                    v.tensor_copy(dots[:, bass.ds(h * TOPK, TOPK)], dstage).then_inc(dots_done, 1)
                    v.drain()
                v.wait_ge(gelu_done, t + 1)
                v.tensor_tensor(wts[:, t % 2, :], dots, gate[:, t % 2, :], ALU.mult).then_inc(w_ready, 1)
                v.drain()
                if t:
                    finish(t - 1)
                if t + 1 < T:
                    choose(t + 1)
            finish(T - 1)

        @block.tensor
        def _(pe):
            pe.wait_ge(const_in_s, 32)

            def norm(layer, tiles, buf):
                for t in tiles:
                    o, n = ln_base[layer] + t, rows_of(t)
                    pe.wait_ge(ln_xn, o + 1)
                    if t >= 2:
                        pe.wait_ge(ln_hT, o - 1)
                    b = 2 * (t % 2)
                    for k in range(KD):
                        mm = pe.transpose(ps[:, b + k // 4, P * (k % 4):P * (k % 4) + n],
                                          buf[0:n, t % 2, P * k:P * k + P], ident[0:n, 0:n])
                    mm.then_inc(ln_tr, 1)

            norm(0, range(T + 1), xn)

            def linear(c, t, bank, r=P, w=256):
                wt = ring[:, c % WR, :].rearrange("p (k n) -> p k n", k=KD)
                for k in range(KD):
                    mm = pe.matmul(ps[0:r, bank, 0:w], hT[:, k, t * P:t * P + r], wt[:, k, 0:w],
                                   start=(k == 0), stop=(k == KD - 1))
                return mm

            def pj_transposes(j):
                n, t = pj_jobs[j]
                r = rows_of(t)
                pe.wait_ge(pj_tok, j + 1)
                if j >= 4:
                    pe.wait_ge(pj_ev, j - 3)
                for c in range(2):
                    mm = pe.transpose(ps[:, j % 4, P * c:P * c + r], tok[0:r, j % 3, P * c:P * c + P], ident[0:r, 0:r])
                mm.then_inc(pj_tr, 1)

            for j, (n, t) in enumerate(pj_jobs):
                chunk(pe, W_IN + n)
                pe.wait_ge(ln_hT, t + 1)
                if j >= 4:
                    pe.wait_ge(pj_raw, j - 3)
                mm = linear(W_IN + n, t, 4 + j % 4, rows_of(t))
                mm.then_inc(pj_acc, 1)
                if j + 1 == len(pj_jobs) or pj_jobs[j + 1][0] != n:
                    pe.drain().then_inc(w_used, 1)
                if 3 <= j < QK + 3:
                    pj_transposes(j - 3)

            pe.wait_ge(pj_ev, QK)
            pe.wait_ge(pj_raw, len(pj_jobs))

            def scores(s):
                t, l = s // 16, s % 16
                head = l
                kT = kTa[:, l // 4, :] if l < 8 else kTb[:, (l - 8) // 2, :]
                if s >= 2:
                    pe.wait_ge(exp_done, s - 1)
                for a in range(2):
                    mm = pe.matmul(ps[:, 2 * (s % 2) + a, 0:HALF], qz[:, head, t * P:(t + 1) * P],
                                   kT[:, a * HALF:(a + 1) * HALF], start=True, stop=True)
                mm.then_inc(s_ready, 1)

            def prob_transposes(i):
                t, s, n, h = pv_jobs[i]
                pe.wait_ge(exp_done, s + n)
                if n == 2:
                    pe.wait_ge(comb_done, 4 * t + h + 1)
                if i >= 2:
                    pe.wait_ge(pta_done, i - 1)
                    pe.wait_ge(ptb_done, i - 1)
                    pe.wait_ge(o_done, i - 1)
                pr = prob[:, s % 4, :]
                for k in range(T):
                    pe.transpose(ps[:, 4 + i % 2, P * k:P * k + P], pr[:, P * k:P * k + P], ident)
                mm = pe.transpose(ps[0:META, 6 + i % 2, 0:P], pr[:, 512:KEYS], ident)
                mm.then_inc(pt_ready, 1)

            def values(i):
                t, s, n, h = pv_jobs[i]
                pe.wait_ge(pta_done, i + 1)
                pe.wait_ge(ptb_done, i + 1)
                if i >= 2:
                    pe.wait_ge(o_done, i - 1)
                for k in range(T + 1):
                    r = rows_of(k)
                    vals = va[0:r, k, :] if n == 1 else vb[0:r, k, P * h:P * h + P]
                    mm = pe.matmul(ps[:, 6 + i % 2, P:2 * P], probT[0:r, i % 2, P * k:P * k + P],
                                   vals, start=(k == 0), stop=(k == T))
                mm.then_inc(av_ready, 1)

            for i in range(NPV + 2):
                if i < NPV:
                    _, s, n, _ = pv_jobs[i]
                    for j in range(n):
                        scores(s + j)
                if 1 <= i <= NPV:
                    prob_transposes(i - 1)
                if i >= 2:
                    values(i - 2)

            def mixed_transposes(src, first):
                for t in range(T):
                    if t >= 2:
                        pe.wait_ge(mixt_ev, first + t - 1)
                    b = 2 * (t % 2)
                    for k in range(KD):
                        mm = pe.transpose(ps[:, b + k // 4, P * (k % 4):P * (k % 4) + P], src[:, t, P * k:P * k + P], ident)
                    mm.then_inc(mixt_tr, 1)

            def out_linear(c0, first):
                pe.wait_ge(mixt_ev, first // 4 + T)
                for j in range(4 * T):
                    n, t = j // T, j % T
                    chunk(pe, c0 + n)
                    if j >= 4:
                        pe.wait_ge(out_add, first + j - 3)
                    mm = linear(c0 + n, t, 4 + j % 4)
                    mm.then_inc(out_acc, 1)
                    if t == T - 1:
                        pe.drain().then_inc(w_used, 1)

            pe.wait_ge(mix_ready, T)
            mixed_transposes(mixed, 0)
            pe.wait_ge(o_done, NPV)
            out_linear(W_OUT, 0)
            norm(1, range(T), xn)

            pe.wait_ge(ln_hT, 9)
            for f in range(NF):
                chunk(pe, W_GU + f)
                if f >= 2:
                    pe.wait_ge(act_ready, f - 1)
                wt = ring[:, (W_GU + f) % WR, :].rearrange("p (k u n) -> p k u n", k=KD, u=2)
                for u in range(2):
                    for k in range(KD):
                        mm = pe.matmul(ps[:, 2 * (f % 2) + u, :], wt[:, k, u, :], hT[:, k, 0:512],
                                       start=(k == 0), stop=(k == KD - 1))
                mm.then_inc(gu_acc, 1)
                pe.drain().then_inc(w_used, 1)
            pe.wait_ge(act_ready, NF)
            for g in range(2):
                pe.wait_ge(gbc_ready, g + 1)
                for k in range(KD):
                    mm = pe.matmul(ps[:, 4 + 2 * g + k // 4, P * (k % 4):P * (k % 4) + P], gbc[:, k, :], ident,
                                   start=True, stop=True)
                mm.then_inc(gate_acc, 1)
            pe.wait_ge(gate_ev, 2)
            for f in range(NF):
                c = W_DOWN + f // 2
                chunk(pe, c)
                wt = ring[:, c % WR, :].rearrange("p (j n) -> p j n", j=2)
                for t in range(T):
                    for half in range(2):
                        mm = pe.matmul(ps[:, 2 * t + half, :], aT[:, f, t * P:(t + 1) * P],
                                       wt[:, f % 2, 512 * half:512 * half + 512], start=(f == 0), stop=(f == NF - 1))
                        if f == NF - 1:
                            mm.then_inc(down_acc, 1)
                if f % 2:
                    pe.drain().then_inc(w_used, 1)

            norm(2, range(T), xn)

            pe.wait_ge(ln_hT, 13)

            def fx_transposes(k):
                pe.wait_ge(fx_tok, k + 1)
                if k >= 4:
                    pe.wait_ge(fx_ev, k - 3)
                buf = ftok[:, 2 * (k >= 8) + k % 2]
                for c in range(4):
                    mm = pe.transpose(ps[:, k % 4, P * c:P * c + P], buf[:, c, :], ident)
                mm.then_inc(fx_tr, 1)

            for j in range(9 * T):
                n, t = j // T, j % T
                k = j - 3 * T
                chunk(pe, W_IN2 + n)
                if j >= 4:
                    pe.wait_ge(p2_ev, j - 3)
                mm = linear(W_IN2 + n, t, 4 + j % 4, w=256 if n != 2 else LAT - 512)
                mm.then_inc(p2_acc, 1)
                if t == T - 1:
                    pe.drain().then_inc(w_used, 1)
                if k == 0:
                    pe.wait_ge(fc_log, 1)
                    for u in range(T):
                        for w in range(u + 1):
                            mm = pe.matmul(ps[:, 3, 8 * u:8 * u + 8], triu if w == u else ones,
                                           logf[:, 2, 8 * w:8 * w + 8], start=(w == 0), stop=(w == u))
                    mm.then_inc(fc_acc, 1)
                    pe.wait_ge(fc_ready, 1)
                if 3 <= k < 19:
                    fx_transposes(k - 3)

            for c in range(3):
                chunk(pe, W_LAT + c)
            uq = [ring[:, (W_LAT + k // 2) % WR, 768 * (k % 2):768 * (k % 2) + 768] for k in range(3)]
            ukv = ring[:, (W_LAT + 2) % WR, :].rearrange("p (k n) -> p k n", k=2)
            pe.wait_ge(fx_ev, 16)
            pe.wait_ge(p2_ev, 9 * T)
            for t in range(T):
                pe.wait_ge(la_n, t + 1)
                if t:
                    pe.wait_ge(la_ev, t)
                for k in range(5):
                    bank, at = (0, P * k) if k < 3 else (1, P * (k - 3))
                    mm = pe.transpose(ps[:, bank, at:at + P], latn[:, P * k:P * k + P], ident)
                mm.then_inc(la_tr, 1)
                pe.wait_ge(la_T, t + 1)
                lT = latT[:, t % 2, :].rearrange("p (a n) -> p a n", a=5)
                for half in range(2):
                    for k in range(3):
                        pe.matmul(ps[:, 2 + half, 0:384], lT[:, k, :], uq[k][:, 384 * half:384 * half + 384],
                                  start=(k == 0), stop=(k == 2))
                for half in range(2):
                    for k in range(2):
                        mm = pe.matmul(ps[:, 4 + half, :], lT[:, 3 + k, :], ukv[:, k, 512 * half:512 * half + 512],
                                       start=(k == 0), stop=(k == 1))
                mm.then_inc(la_acc, 1)
                pe.wait_ge(mq_tok, t + 1)
                for g in range(4):
                    buf = qtok if g < 2 else ktok
                    if 4 * t + g >= 2:
                        pe.wait_ge(mq_ev, 4 * t + g - 1)
                    for c in range(4):
                        mm = pe.transpose(ps[0:MLA_QK, 6 + g % 2, P * c:P * c + P], buf[:, 4 * (g % 2) + c, :], ident)
                    mm.then_inc(mq_tr, 1)
            pe.drain().then_inc(w_used, 3)
            pe.wait_ge(mq_ev, 4 * T)

            NU = T * HEADS2
            for i in range(NU + 2):
                if i < NU:
                    t, h = i // HEADS2, i % HEADS2
                    if i >= 2:
                        pe.wait_ge(exp2, i - 1)
                    n = (t + 1) * P
                    q = qT_mla[0:MLA_QK, h, t * P:n] if h < 8 else qT_fox[:, h - 8, t * P:n]
                    kk = kT_mla[0:MLA_QK, h, 0:n] if h < 8 else kT_fox[:, h - 8, 0:n]
                    pe.matmul(ps[:, i % 2, 0:n], q, kk, start=True, stop=False)
                    pe.matmul(ps[:, i % 2, t * P:n], ident, maskt, start=False, stop=True).then_inc(s2_ready, 1)
                if 1 <= i <= NU:
                    u = i - 1
                    pe.wait_ge(exp2, u + 1)
                    if u >= 2:
                        pe.wait_ge(pt2_done, u - 1)
                    for k in range(u // HEADS2 + 1):
                        mm = pe.transpose(ps[:, 2 + u % 2, P * k:P * k + P], prob2[:, u % 4, P * k:P * k + P], ident)
                    mm.then_inc(pt2, 1)
                if i >= 2:
                    u = i - 2
                    t, h = u // HEADS2, u % HEADS2
                    pe.wait_ge(pt2_done, u + 1)
                    if u >= 2:
                        pe.wait_ge(o2_done, u - 1)
                    for k in range(t + 1):
                        vv, hh = (v_mla, h) if h < 8 else (v_fox, h - 8)
                        mm = pe.matmul(ps[:, 4 + u % 2, 0:P], probT2[:, u % 2, P * k:P * k + P],
                                       vv[:, k, P * (hh // 2):P * (hh // 2) + P], start=(k == 0), stop=(k == t))
                    mm.then_inc(av2, 1)

            pe.wait_ge(o2_done, NU)
            mixed_transposes(mixed2, T)
            out_linear(W_O2, 4 * T)
            norm(3, range(T), xn4)
            for t in range(T):
                pe.wait_ge(ln_hT, 13 + t + 1)
                if t == 0:
                    pe.wait_ge(out_add, 8 * T)
                if t >= 2:
                    pe.wait_ge(h2_ev, t - 1)
                b = 4 + 2 * (t % 2)
                for k in range(KD):
                    mm = pe.transpose(ps[:, b + k // 4, P * (k % 4):P * (k % 4) + P], hT[:, k, t * P:(t + 1) * P], ident)
                mm.then_inc(h2_tr, 1)
            pe.wait_ge(ln_hT, 17)
            pe.wait_ge(subk_in_s, 16)
            for c in range(17):
                if c < 16:
                    w = W_PQ + c // 2
                    chunk(pe, w)
                    if c >= 4:
                        pe.wait_ge(qp_ev, c - 3)
                    wt = ring[:, w % WR, :].rearrange("p (k n) -> p k n", k=KD)
                    for k in range(KD):
                        mm = pe.matmul(ps[:, c % 4, :], wt[:, k, P * (c % 2):P * (c % 2) + P], hT[:, k, 0:512],
                                       start=(k == 0), stop=(k == KD - 1))
                    mm.then_inc(qp_acc, 1)
                    if c % 2:
                        pe.drain().then_inc(w_used, 1)
                if c >= 1:
                    q = c - 1
                    pe.wait_ge(qp_ev, q + 1)
                    pe.wait_ge(h2_ev, T)
                    if q >= 4:
                        pe.wait_ge(sk_ev, q - 3)
                    for t in range(T):
                        mm = pe.matmul(ps[:, 4 + q % 4, P * t:P * t + P], qpT[:, q, t * P:(t + 1) * P], subk[:, q, :],
                                       start=True, stop=True)
                    mm.then_inc(sk_acc, 1)

            pe.wait_ge(idx_ready, 1)
            for t in range(T):
                b = 2 * (t % 2)
                if t >= 2:
                    pe.wait_ge(y_ready, t - 1)
                for half in range(2):
                    pe.matmul(ps[:, b + half, :], zmat, const[:, 0:512], start=True, stop=False,
                              skip_group_check=True)
                with pe.Fori(0, PH) as h:
                    for k in range(TOPK):
                        pe.wait_ge(diag_ready, h * TOPK + (t * SLOTS + k + 1))
                        pe.wait_ge(row_in[k], h * 16 + ((2 * t + 1) * PH + 1) * 16)
                        for half in range(2):
                            mm = pe.matmul(ps[:, b + half, :], diag[:, k % 4, :], rows[:, k, 512 * half:512 * half + 512],
                                           start=False, stop=False, skip_group_check=True)
                        mm.then_inc(slot_free[k], 1)
                pe.drain().then_inc(y_acc, 1)


def _chunks(w, np):
    k, n = w.shape
    w = np.pad(w, ((0, 0), (0, -n % 256)))
    return w.reshape(k // P, P, -1, 256).transpose(2, 1, 0, 3).reshape(-1, P, CH)


def kernel(**inputs):
    import numpy as _np
    import concourse.bacc as _bacc
    from concourse import mybir as _mybir
    from concourse.bass_utils import run_bass_kernel_spmd as _run

    g = {k: _np.asarray(v) for k, v in inputs.items()}
    f = _np.float32

    gu = _np.stack([g["w_gate"][0], g["w_up"][0]]).reshape(2, KD, P, NF, P).transpose(3, 2, 1, 0, 4).reshape(NF, P, CH)
    down = g["w_down"][0].reshape(NF // 2, 2, P, D).transpose(0, 2, 1, 3).reshape(NF // 2, P, CH)
    w2 = g["w_in_2"]
    lat = _np.concatenate([w2[:, 0:672], w2[:, 2208:2216]], axis=1)
    w2 = _np.concatenate([_np.pad(lat, ((0, 0), (0, 768 - LAT))), w2[:, 672:2208]], axis=1)
    uq = g["w_uq_2"].reshape(3, P, 768)
    uq01 = _np.pad(_np.concatenate([uq[0], uq[1]], axis=1), ((0, 0), (0, CH - 1536)))
    uq2 = _np.pad(uq[2], ((0, 0), (0, CH - 768)))
    ukv = g["w_ukv_2"].reshape(2, P, D).transpose(1, 0, 2).reshape(P, CH)
    wst = _np.concatenate([_chunks(g["w_in"][0], _np), _chunks(g["w_out"][0], _np), gu, down, _chunks(w2, _np),
                           uq01[None], uq2[None], ukv[None], _chunks(g["w_o_2"], _np), _chunks(g["w_pq_2"], _np)])
    wada = _np.ascontiguousarray(g["w_ada_2"].T).reshape(48, P, D)

    def by_partition(v):
        return v.reshape(-1, P).T

    cols = _np.concatenate([by_partition(g[n]) for n in ("attn_norm_g", "ffn_norm_g", "norm1_g_2", "norm2_g_2",
                                                         "b_ada_2", "mla_qa_g_2", "mla_kva_g_2")], axis=1)
    gains = []
    for n in ("a_q_norm_g", "a_k_norm_g", "b_q_norm_g", "b_k_norm_g"):
        v = g[n][0]
        gains += [v, v.reshape(-1, 2)[:, ::-1].reshape(-1)]
    rowsa = _np.concatenate([*gains, g["b_subln_g"][0], g["b_lambda_q1"][0], g["b_lambda_k1"][0], g["b_lambda_q2"][0],
                             g["b_lambda_k2"][0]])[None]
    rowsb = _np.concatenate([g["c_2"][0], g["mla_q_g_2"], g["mla_k_g_2"], g["fox_q_g_2"], g["fox_k_g_2"],
                             g["b_f_2"]])[None]
    real = _np.arange(T * P)
    inv = (10000.0 ** (-_np.arange(0, HD, 2, dtype=f) / HD)).astype(f)
    inva = (10000.0 ** (-_np.arange(0, HD // 2, 2, dtype=f) / (HD // 2))).astype(f)
    ang_a = _np.zeros((5 * P, HD // 2), f)
    ang_a[:T * P] = _np.concatenate([(real // 64).astype(f)[:, None] * inva, (real % 64).astype(f)[:, None] * inva], 1)
    ang_b = _np.zeros((5 * P, HD // 2), f)
    ang_b[:T * P] = (real + META).astype(f)[:, None] * inv
    ang_b[T * P:T * P + META] = _np.arange(META, dtype=f)[:, None] * inv
    tables = []
    for ang in (ang_a, ang_b):
        c, s = _np.cos(ang), _np.sin(ang)
        tables += [_np.stack([c, c], -1), _np.stack([-s, s], -1)]
    rope = _np.stack(tables).reshape(4, 5, P, HD).transpose(2, 0, 1, 3).reshape(P, 4 * 5 * HD).astype(f)
    const = _np.zeros((P, NCONST), f)
    const[:, K_ID:K_ID + P] = _np.eye(P)
    const[:, K_TRIU:K_TRIU + P] = _np.triu(_np.ones((P, P)))
    const[:, K_MASK:K_MASK + P] = _np.triu(_np.ones((P, P)), 1) * MASK
    const[:, K_ONES:K_ONES + P] = 1.0
    const[:, K_IOTA:K_IOTA + 16] = _np.arange(16)
    const[:, K_FREQ:K_FREQ + 16] = 10000.0 ** (-_np.arange(0, 32, 2, dtype=f) / 32)
    arrays = {
        "wst": wst, "wada": wada, "x_in": g["x"].reshape(T, P, D), "meta_in": g["meta_tokens"], "cols_in": cols,
        "rowsa_in": rowsa, "rowsb_in": rowsb, "rope_in": rope, "const_in": const,
        "pos_in": g["positions_2"].reshape(T, P).T,
        "subk_in": g["sub_keys_2"].reshape(16, NKEYS, P).transpose(2, 0, 1).reshape(P, CH),
        "peer_u": g["peer_u_2"], "peer_v": g["peer_v_2"],
    }
    arrays = {k: _np.ascontiguousarray(v) for k, v in arrays.items()}
    nc = _bacc.Bacc("TRN2", target_bir_lowering=False, num_devices=1)
    args = {n: nc.dram_tensor(n, a.shape, _mybir.dt.from_np(a.dtype), kind="ExternalInput").ap()
            for n, a in arrays.items()}
    out = nc.dram_tensor("out", (T, P, D), F32, kind="ExternalOutput").ap()
    build(nc, out=out, **args)
    r = _run(nc, [arrays], core_ids=[0])
    return r.results[0]["out"].reshape(1, T * P, D)
```

```python
from contextlib import ExitStack

import numpy as np

import concourse.bass as bass
from concourse import mybir

ALU = mybir.AluOpType
ACT = mybir.ActivationFunctionType
F32 = mybir.dt.float32
F32R = mybir.dt.float32r
I32 = mybir.dt.int32
U32 = mybir.dt.uint32
AX = mybir.AxisListType

P = 128
D = 1024
KD = D // P
T = 4
META = 16
KEYS = T * P + META
HALF = KEYS // 2
FF = 2816
NF = FF // P
EPS = 1e-6
HD = 64
SCALE = HD ** -0.5
LAM_INIT = 0.2
MLA_QK = 96
MLA_SCALE = MLA_QK ** -0.5
QR, KVR = 384, 256
LAT = 680
HEADS2 = 16
PH, TOPK, NKEYS = 8, 16, 128
SLOTS = PH * TOPK
UR = 8
LOW = -3.0e38
MASK = -(2.0 ** 100)

CH = 2048
W_IN, W_OUT = 0, 9
W_GU = W_OUT + 4
W_DOWN = W_GU + NF
W_IN2 = W_DOWN + NF // 2
W_LAT = W_IN2 + 9
W_O2 = W_LAT + 3
W_PQ = W_O2 + 4
NCHUNK = W_PQ + 8
WR = 6

C_G1, C_GF, C_N1, C_N2, C_BADA, C_QA, C_KVA, NCOL = 0, 8, 16, 24, 32, 80, 83, 85
K_ID, K_TRIU, K_MASK, K_ONES, K_IOTA, K_FREQ, NCONST = 0, 128, 256, 384, 512, 528, 544
RA_ROPE, RA_SUB, RA_LAM, NRA = 0, 512, 640, 896
RB_C, RB_MQ, RB_MK, RB_FQ, RB_FK, RB_BF, NRB = 0, 1024, 1120, 1216, 1280, 1344, 1352

TWO_PI = 2.0 * np.pi
PI2_A = 6.28125
PI2_B = float(np.floor((TWO_PI - PI2_A) * 2.0 ** 20) / 2.0 ** 20)
PI2_C = float(TWO_PI - PI2_A - PI2_B)
ROUND = 1.5 * 2.0 ** 23
PI_F = 3.1415925


def build(nc, wst, wada, x_in, meta_in, cols_in, rowsa_in, rowsb_in, rope_in, const_in, pos_in,
          subk_in, peer_u, peer_v, out):
    ctx = ExitStack()
    with ctx:
        def sb(name, shape, dt=F32):
            return ctx.enter_context(nc.sbuf_tensor(name, shape, dt))

        def sem(name):
            return ctx.enter_context(nc.semaphore(name))

        def cut(arena, at, *dims):
            n = int(np.prod(dims))
            v = arena[:, at:at + n]
            if len(dims) == 2:
                return v.rearrange("p (a b) -> p a b", a=dims[0])
            if len(dims) == 3:
                return v.rearrange("p (a b c) -> p a b c", a=dims[0], b=dims[1])
            return v

        def over(ap, n):
            return ap.unsqueeze(len(ap.shape)).broadcast_to([*ap.shape, n])

        def each(ap, n):
            return ap.unsqueeze(1).broadcast_to([ap.shape[0], n, *ap.shape[1:]])

        ps = ctx.enter_context(nc.psum_tensor("ps", [P, 8, 512], F32))

        x = sb("x", [P, T, D])
        big_at = -(-nc.sbuf_base // 32) * 32
        big = sb("big", [P, WR * CH + 4224])
        r2 = sb("r2", [P, 17312])
        r2_at = big_at + 4 * (WR * CH + 4224)
        assert nc.sbuf_base == r2_at + 4 * 17312
        r1 = sb("r1", [P, 11360])
        gates = sb("gates", [P, 2, D])
        const = sb("const", [P, NCONST])
        cols = sb("cols", [P, NCOL])
        rowsa = sb("rowsa", [P, NRA - 512])
        rowsb = sb("rowsb", [P, NRB - D])
        mod = sb("mod", [P, 48])
        gs = sb("gs", [P, 2, KD])
        lnst = sb("lnst", [P, 3, 20])
        neglam = sb("neglam", [P, 4])
        zero = sb("zero", [P, 1])
        eps = sb("eps", [P, 1])
        pos = sb("pos", [P, T], I32)

        ident = const[:, K_ID:K_ID + P]
        triu = const[:, K_TRIU:K_TRIU + P]
        maskt = const[:, K_MASK:K_MASK + P]
        ones = const[:, K_ONES:K_ONES + P]
        iota = const[:, K_IOTA:K_IOTA + 16]
        freq = const[:, K_FREQ:K_FREQ + 16]

        ring = cut(big, 0, WR, CH)
        hT = cut(big, WR * CH, KD, KEYS)
        qz = cut(r1, 0, 16, 512)
        kTa = cut(r1, 8192, 2, KEYS)
        kTb = cut(r1, 8192 + 2 * KEYS, 4, KEYS)
        va = cut(r2, 0, T + 1, 128)
        vb = cut(r2, 640, T + 1, 512)
        rope = cut(r2, 3200, 8, 5, HD)
        sqb = cut(r2, 5760, 2, 256)
        raw = cut(r2, 6272, 3, 256)
        xr = cut(r2, 7040, 256)
        ra = cut(r2, 7296, 256)
        rb = cut(r2, 7552, 256)
        tok = cut(r2, 7808, 3, 256)
        qst = cut(r2, 8576, 4, 3, 4)
        mixed = cut(r2, 8832, T, D)
        xmeta = cut(r2, 8832, D)
        ropec = cut(r2, 9856, 4, 5, HD)
        ropeg = cut(r2, 11136, 8, HD)
        xn = cut(r2, 12928, 2, D)
        prob = cut(r2, 12928, 4, KEYS)
        probT = cut(r2, 15040, 2, 640)
        sqo = cut(r2, 16320, 512)
        sst = sb("sst", [P, 4, 64])
        ost = sb("ost", [P, 3, 16])
        coef = sb("coef", [P, 32])
        aT = cut(r1, 0, NF, 512)
        sg = cut(r2, 7168, 2, 512)
        xn1 = cut(r1, 0, 2, D)
        adar = cut(r2, 0, 4, D)
        crow = cut(r2, 4096, D)
        ctmp = cut(r2, 5120, D)
        gbc = cut(r2, 6144, KD, P)
        def halves(name, byte, n):
            return nc.alloc_sbuf_tensor_at(name, [P, n], F32R, offset=byte)

        w_hi_f = halves("w_hi", r2_at + 4 * 8192, 2 * CH)
        w_lo_f = halves("w_lo", big_at, WR * CH)
        h_hi_f = halves("h_hi", big_at + 4 * WR * CH, KD * KEYS)
        h_lo_f = halves("h_lo", r2_at + 4 * 13216, KD * 512)
        w_hi, w_lo = cut(w_hi_f, 0, 2, CH), cut(w_lo_f, 0, WR, CH)
        h_hi, h_lo = cut(h_hi_f, 0, KD, KEYS), cut(h_lo_f, 0, KD, 512)
        h_full = cut(r2, 13216, KD, 512)
        kT_mla = cut(r1, 0, 8, 512)
        kT_fox = cut(r1, 4096, 8, 512)
        v_fox = cut(r1, 8192, T, 512)
        qT_mla = cut(r2, 0, 8, 512)
        qT_fox = cut(r2, 4096, 8, 512)
        v_mla = cut(r2, 8192, T, 512)
        lat = cut(r2, 10240, T, LAT)
        qktok = [[cut(r2, at, 8, MLA_QK), cut(r2, at + 768, 8, MLA_QK)] for at in (12960, 14496)]
        ftok = cut(r2, 14496, 4, 4, P)
        fsq = cut(r2, 16544, 256)
        fraw = cut(r2, 16800, 2, 256)
        mixed2 = cut(r2, 10240, T, D)
        latn = cut(big, WR * CH, 640)
        latT = cut(big, WR * CH + 640, 2, 5 * P)
        msq = cut(big, WR * CH + 1920, 2, 8, MLA_QK)
        rp = cut(big, WR * CH + 3456, 4, 8, 16)
        prob2 = cut(big, WR * CH, 4, 512)
        probT2 = cut(big, WR * CH + 2048, 2, 512)
        trig = cut(r1, 10240, 5, T * 16)
        fst = cut(r1, 10560, 3, 16, 4)
        mst = cut(r1, 10752, 3, T, 16)
        logf = cut(r1, 10944, 3, 32)
        fcum = cut(r1, 11040, 2, T, 8)
        lst = cut(r1, 11104, 3, 8)
        sst2 = sst
        qpT = cut(r1, 0, 4, 512)
        subk = cut(r1, 2048, 16, P)
        zmat = cut(r1, 4096, P)
        idx = cut(r1, 4224, T * SLOTS).bitcast(U32)
        topi = cut(r1, 4736, 2, TOPK).bitcast(U32)
        besti = cut(r1, 4768, TOPK).bitcast(U32)
        bits = cut(r1, 4784, 2, TOPK).bitcast(U32)
        sc = cut(r2, 0, T * 2048)
        scf = cut(r2, 0, T, 2048)
        h2 = cut(r2, 8192, T, D)
        xn4 = cut(r2, 14336, 2, D)
        urows = [cut(r1, 4992 + D * i, D) for i in range(6)] + [cut(r2, 12288 + D * i, D) for i in range(2)]
        vrows = cut(big, 0, TOPK, D)
        hsc = cut(r2, 14336, 2, P)
        sc2 = cut(r2, 14592, P)
        cand = cut(r2, 14720, 2, 256)
        topv = cut(r2, 15232, 2, TOPK)
        topf = cut(r2, 15264, 2, TOPK)
        bestv = cut(r2, 15296, TOPK)
        bitf = cut(r2, 15312, 2, TOPK)
        e12 = cut(r2, 15344, 2, TOPK)
        hot = cut(r2, 15376, TOPK, 16)
        dstage = cut(r2, 15632, TOPK)
        gst = cut(r2, 15648, 2, PH)
        gate = cut(r2, 15664, T * SLOTS)
        dots = cut(r2, 16176, SLOTS)
        wts = cut(r2, 16304, 2, SLOTS)
        diag = cut(r2, 16560, 4, P)
        expf = cut(r2, 17072, TOPK)
        gtmp = cut(r2, 0, 2, 256)
        yacc = cut(r2, 0, D)
        istage = cut(r1, 11136, 4 * TOPK).bitcast(U32)

        x_in_s = [sem(f"x_in{t}") for t in range(5)]
        const_in_s, rope_in_s, rowsb_in_s = sem("const_in_s"), sem("rope_in_s"), sem("rowsb_in_s")
        crow_in_s, subk_in_s = sem("crow_in_s"), sem("subk_in_s")
        w_load = [sem(f"w_load{i}") for i in range(WR)]
        w_used = sem("w_used")
        setup_pool, setup_dve, rope_ready = sem("setup_pool"), sem("setup_dve"), sem("rope_ready")
        ln_rms, ln_xn, ln_tr, ln_hT = sem("ln_rms"), sem("ln_xn"), sem("ln_tr"), sem("ln_hT")
        pj_acc, pj_raw, pj_red, pj_rms, pj_tok, pj_tr, pj_ev = (
            sem(n) for n in ("pj_acc", "pj_raw", "pj_red", "pj_rms", "pj_tok", "pj_tr", "pj_ev"))
        s_ready, max_ready, exp_done, comb_done, pt_ready, pta_done, ptb_done, av_ready, o_done = (
            sem(n) for n in ("s_ready", "max_ready", "exp_done", "comb_done", "pt_ready", "pta_done",
                             "ptb_done", "av_ready", "o_done"))
        once_act, once_dve = sem("once_act"), sem("once_dve")
        LAM_EXP, C_EXP, SINES, LOG = 1, 2, 3, 4
        LAM_SUMS, ANGLES, LOGITS, LOG_GATES, GATE_SUMS = 1, 2, 3, 4, 5
        sub_sq, sub_rms, mix_ready = sem("sub_sq"), sem("sub_rms"), sem("mix_ready")
        mixt_tr, mixt_ev = sem("mixt_tr"), sem("mixt_ev")
        out_acc, out_add = sem("out_acc"), sem("out_add")
        gu_acc, silu_done, act_ready = sem("gu_acc"), sem("silu_done"), sem("act_ready")
        w_hi_done, w_lo_done = sem("w_hi_done"), sem("w_lo_done")
        down_acc, down_add = sem("down_acc"), sem("down_add")
        ada_load = [sem(f"ada_load{i}") for i in range(4)]
        ada_used, gbc_ready, gate_acc, gate_ev = (
            sem(n) for n in ("ada_used", "gbc_ready", "gate_acc", "gate_ev"))
        p2_acc, p2_ev = sem("p2_acc"), sem("p2_ev")
        fx_red, fx_rms, fx_tok, fx_tr, fx_ev = (sem(n) for n in ("fx_red", "fx_rms", "fx_tok", "fx_tr", "fx_ev"))
        fc_acc = sem("fc_acc")
        la_rms, la_n, la_tr, la_T, la_acc, la_ev = (
            sem(n) for n in ("la_rms", "la_n", "la_tr", "la_T", "la_acc", "la_ev"))
        mq_red, mq_rms, mq_tok, mq_tr, mq_ev = (sem(n) for n in ("mq_red", "mq_rms", "mq_tok", "mq_tr", "mq_ev"))
        s2_ready, max2, exp2, pt2, pt2_done, av2, o2_done = (
            sem(n) for n in ("s2_ready", "max2", "exp2", "pt2", "pt2_done", "av2", "o2_done"))
        h2_tr, h2_ev, qp_acc, qp_ev, sk_acc, sk_ev = (
            sem(n) for n in ("h2_tr", "h2_ev", "qp_acc", "qp_ev", "sk_acc", "sk_ev"))
        gate_exp, idx_ready, dots_done, gelu_done, w_ready = (
            sem(n) for n in ("gate_exp", "idx_ready", "dots_done", "gelu_done", "w_ready"))
        u_in = [sem(f"u_in{i}") for i in range(UR)]
        v_in = [sem(f"v_in{i}") for i in range(TOPK)]
        u_free = [sem(f"u_free{i}") for i in range(UR)]
        v_free = [sem(f"v_free{i}") for i in range(TOPK)]
        staged, diag_ready, y_acc, y_ready, y_out, issued = (
            sem(n) for n in ("staged", "diag_ready", "y_acc", "y_ready", "y_out", "issued"))

        pj_jobs = [(n, t) for n in range(9) for t in range(T + (n in (2, 5, 6, 7, 8)))]
        QK = sum(n < 7 for n, _ in pj_jobs)
        ln_base = [0, 5, 9, 13]

        def by_pe(t):
            return [k for k in range(TOPK) if t < T - 1 or k % 4 != 3]

        def chunk(eng, c):
            eng.wait_ge(w_load[c % WR], 16 * (c // WR + 1))

        def rows_of(t):
            return P if t < T else META

        pv_jobs = []
        for t in range(T):
            for h in range(8):
                pv_jobs.append((t, 16 * t + h, 1, h))
            for h in range(4):
                pv_jobs.append((t, 16 * t + 8 + 2 * h, 2, h))
        pv_of = {s + j: i for i, (t, s, n, h) in enumerate(pv_jobs) for j in range(n)}
        NPV = len(pv_jobs)

        block = ctx.enter_context(nc.Block())

        @block.sync
        def _(sp):
            for t in range(T):
                sp.dma_start(x[:, t, :], x_in[t]).then_inc(x_in_s[t], 16)
            for c in range(WR):
                sp.dma_start(ring[:, c, :], wst[c]).then_inc(w_load[c], 16)
            whole = (NCHUNK - WR) // WR
            with sp.Fori(0, whole) as i:
                for c in range(WR):
                    sp.wait_ge(w_used, i * WR + (c + 1))
                    sp.dma_start(ring[:, c, :], wst[bass.ds(i * WR + (WR + c), 1), :, :].rearrange("a p n -> p (a n)")
                                 ).then_inc(w_load[c], 16)
            for c in range(WR * (whole + 1), NCHUNK):
                sp.wait_ge(w_used, c - WR + 1)
                sp.dma_start(ring[:, c % WR, :], wst[c]).then_inc(w_load[c % WR], 16)
            for t in range(T):
                sp.wait_ge(y_ready, t + 1)
                sp.dma_start(out[t], x[:, t, :]).then_inc(y_out, 16)
            sp.wait_ge(y_out, 16 * T)

        @block.gpsimd
        def _(pool):
            pool.memset(qz, 0.0).then_inc(setup_pool, 1)
            pool.wait_ge(mixt_ev, T)
            pool.dma_start(crow, rowsb_in[:, RB_C:RB_C + D].broadcast_to([P, D])).then_inc(crow_in_s, 16)
            for m in range(48):
                if m >= 4:
                    pool.wait_ge(ada_used, m - 3)
                pool.dma_start(adar[:, m % 4, :], wada[m]).then_inc(ada_load[m % 4], 16)
            pool.wait_ge(gate_ev, 2)
            pool.wait_ge(ln_tr, 13)
            pool.memset(ftok, 0.0)
            pool.drain()
            pool.memset(ftok[:, 0:2, :, HD:HD + 1], 1.0)
            pool.memset(ftok[:, 2:4, :, HD + 1:HD + 2], 1.0)
            pool.drain().then_inc(setup_pool, 1)
            pool.wait_ge(av2, T * HEADS2)
            pool.dma_start(subk, subk_in).then_inc(subk_in_s, 16)

            for free in (*u_free, *v_free):
                pool.sem_inc(free, 1)
            pool.wait_ge(ln_tr, 17)
            copies = 0
            for s in range(T + 1):
                kinds = ([0] if s < T else []) + ([1] if s else [])
                if s == 1:
                    pool.wait_ge(w_used, NCHUNK)
                    pool.wait_ge(qp_ev, 16)
                with pool.Fori(0, PH // 2) as pair:
                    for g in range(2):
                        stage = {}
                        for n, kind in enumerate(kinds):
                            first = (s - kind) * PH + g
                            if kind == 0:
                                pool.wait_ge(idx_ready, pair * 2 + (first + 1))
                            stage[kind] = istage[:, (2 * kind + g) * TOPK:(2 * kind + g + 1) * TOPK]
                            pool.tensor_copy(stage[kind], idx[:, bass.ds(pair * (2 * TOPK) + first * TOPK, TOPK)]
                                             ).then_inc(staged, 1)
                            pool.wait_ge(staged, pair * (2 * len(kinds)) + (copies + g * len(kinds) + n + 1))
                        pool.sem_inc(issued, 1)
                        for k in range(TOPK):
                            for kind in kinds:
                                first = (s - kind) * PH + g
                                if kind == 0:
                                    slot, free, got = urows[k % UR], u_free[k % UR], u_in[k % UR]
                                    pool.wait_ge(free, pair * 4 + (2 * first + k // UR + 1))
                                else:
                                    slot, free, got = vrows[:, k, :], v_free[k], v_in[k]
                                    pool.wait_ge(free, pair * 2 + (first + 1))
                                pool.sem_inc(issued, 1)
                                pool.indirect_dma_start(
                                    slot, None, (peer_u, peer_v)[kind],
                                    bass.IndirectOffsetOnAxis(ap=stage[kind][:, k:k + 1], axis=0)
                                ).then_inc(got, 16)
                copies += PH * len(kinds)

        @block.scalar
        def _(act):
            act.dma_start(const[:], const_in).then_inc(const_in_s, 16)
            act.dma_start(cols[:], cols_in).then_inc(const_in_s, 16)
            act.dma_start(xmeta[0:META, :], meta_in).then_inc(x_in_s[4], 16)
            act.dma_start(ropec, rope_in).then_inc(rope_in_s, 16)
            act.dma_start(ropeg, rowsa_in[:, 0:512].broadcast_to([P, 512])).then_inc(rope_in_s, 16)
            act.dma_start(rowsa[:], rowsa_in[:, 512:NRA].broadcast_to([P, NRA - 512])).then_inc(rope_in_s, 16)
            act.dma_start(rowsb[:], rowsb_in[:, D:NRB].broadcast_to([P, NRB - D])).then_inc(rowsb_in_s, 16)
            act.dma_start(pos[:], pos_in).then_inc(rowsb_in_s, 16)

            def norm(layer, tiles, junk):
                for t in tiles:
                    o, n = ln_base[layer] + t, rows_of(t)
                    if layer == 0:
                        act.wait_ge(x_in_s[t], 16)
                        if t == 0:
                            act.wait_ge(setup_dve, 1)
                    elif layer == 2:
                        act.wait_ge(down_add, 2 * (t + 1))
                    else:
                        act.wait_ge(out_add, 16 * (layer // 3) + 4 * (t + 1))
                    if t >= 2:
                        act.wait_ge(ln_tr, o - 1)
                    src = xmeta[0:n, :] if t == T else x[:, t, :]
                    act.activation(junk[0:n, t % 2, :], src, ACT.Square, scale=1 / 32, bias=zero[0:n, :],
                                   accum_out=lnst[0:n, 0, o:o + 1])
                    act.drain()
                    act.activation(lnst[0:n, 1, o:o + 1], lnst[0:n, 0, o:o + 1], ACT.Sqrt,
                                   bias=eps[0:n, :]).then_inc(ln_rms, 1)

            norm(0, range(T + 1), xn)

            def pj_sqrt(j):
                n, t = pj_jobs[j]
                r = rows_of(t)
                act.wait_ge(pj_red, j + 1)
                act.activation(qst[0:r, j % 4, 1, :], qst[0:r, j % 4, 0, :], ACT.Sqrt,
                               bias=eps[0:r, :]).then_inc(pj_rms, 1)

            def pj_evac(j):
                n, t = pj_jobs[j]
                r, s = rows_of(t), t * P
                act.wait_ge(pj_tr, j + 1)
                if j == 0:
                    act.wait_ge(setup_pool, 1)
                b = ps[:, j % 4, 0:256].rearrange("p (c n) -> p c n", c=2)
                if n in (0, 1, 3, 4):
                    h = 4 * n if n < 2 else 8 + 4 * (n - 3)
                    act.activation(qz[0:64, h:h + 4:2, s:s + P], b[0:64], ACT.Copy)
                    act.activation(qz[64:P, h + 1:h + 4:2, s:s + P], b[64:P], ACT.Copy).then_inc(pj_ev, 1)
                elif n == 2:
                    act.activation(kTa[:, :, s:s + r], b[:, :, 0:r], ACT.Copy).then_inc(pj_ev, 1)
                else:
                    act.activation(kTb[:, 2 * (n - 5):2 * (n - 5) + 2, s:s + r], b[:, :, 0:r],
                                   ACT.Copy).then_inc(pj_ev, 1)

            for j, (n, t) in enumerate(pj_jobs):
                r = rows_of(t)
                act.wait_ge(pj_acc, j + 1)
                b = ps[0:r, 4 + j % 4, 0:256]
                if n < 7:
                    w = P if n == 2 else 256
                    if j >= 2:
                        act.wait_ge(pj_red, j - 1)
                    if j >= 3:
                        act.wait_ge(pj_tok, j - 2)
                    act.activation(sqb[0:r, j % 2, 0:w], b[:, 0:w], ACT.Square, scale=1 / 8, bias=zero[0:r, :])
                    if n == 2:
                        act.activation(va[0:r, t, :], b[:, P:256], ACT.Copy)
                    act.activation(raw[0:r, j % 3, 0:w], b[:, 0:w], ACT.Copy)
                else:
                    act.activation(vb[0:r, t, (n - 7) * 256:(n - 6) * 256], b, ACT.Copy)
                act.drain().then_inc(pj_raw, 1)
                if 1 <= j <= QK:
                    pj_sqrt(j - 1)
                if 3 <= j < QK + 3:
                    pj_evac(j - 3)

            act.wait_ge(once_dve, LAM_SUMS)
            act.activation(neglam[:, 2:4], neglam[:, 0:2], ACT.Exp, bias=zero[:]).then_inc(once_act, 1)

            def softmax(s):
                act.wait_ge(max_ready, s + 1)
                if s >= 4:
                    act.wait_ge(pt_ready, pv_of[s - 4] + 1)
                act.activation(prob[:, s % 4, :].rearrange("p (a b) -> p a b", a=2),
                               ps[:, 2 * (s % 2):2 * (s % 2) + 2, 0:HALF], ACT.Exp, scale=SCALE,
                               bias=sst[:, 1, s:s + 1], accum_out=sst[:, 2, s:s + 1])
                act.drain().then_inc(exp_done, 1)

            def prob_evac(p):
                act.wait_ge(pt_ready, p + 1)
                if p >= 2:
                    act.wait_ge(av_ready, p - 1)
                act.activation(probT[:, p % 2, 0:512], ps[:, 4 + p % 2, :], ACT.Copy).then_inc(pta_done, 1)

            for i in range(NPV + 1):
                if i < NPV:
                    _, s, n, _ = pv_jobs[i]
                    for j in range(n):
                        softmax(s + j)
                if i >= 1:
                    prob_evac(i - 1)

            for t in range(T):
                act.wait_ge(sub_sq, t + 1)
                act.activation(ost[:, 1, 4 * t:4 * t + 4], ost[:, 0, 4 * t:4 * t + 4], ACT.Sqrt,
                               bias=eps[:], scale=1 / 128).then_inc(sub_rms, 1)
            def mix_and_norm(first, layer, junk):
                for t in range(T + 1):
                    if t < T:
                        act.wait_ge(mixt_tr, first + t + 1)
                        act.activation(hT[:, :, t * P:(t + 1) * P],
                                       ps[:, 0:2, :].rearrange("p a (b n) -> p (a b) n", n=P),
                                       ACT.Copy).then_inc(mixt_ev, 1)
                    if t:
                        norm(layer, [t - 1], junk)

            mix_and_norm(0, 1, xn1)

            def high_part(f):
                chunk(act, W_GU + f)
                act.activation(w_hi[:, f % 2, :], ring[:, (W_GU + f) % WR, :], ACT.Copy).then_inc(w_hi_done, 1)

            high_part(0)
            high_part(1)

            act.wait_ge(crow_in_s, 16)
            act.activation(ctmp, crow, ACT.Exp, scale=-1.0, bias=zero[:]).then_inc(once_act, 1)

            for f in range(NF):
                act.wait_ge(gu_acc, f + 1)
                if f >= 2:
                    act.wait_ge(act_ready, f - 1)
                act.activation(sg[:, f % 2, :], ps[:, 2 * (f % 2), :], ACT.Silu, bias=zero[:]).then_inc(silu_done, 1)
                if f + 2 < NF:
                    high_part(f + 2)
            for g in range(2):
                act.wait_ge(gate_acc, g + 1)
                act.activation(gates[:, g, :].rearrange("p (a b) -> p a b", a=2),
                               ps[:, 4 + 2 * g:6 + 2 * g, :], ACT.Copy).then_inc(gate_ev, 1)

            norm(2, range(T), xn)

            act.wait_ge(once_dve, ANGLES)
            act.activation(trig[:, 0:2, :], trig[:, 2:4, :], ACT.Sin, bias=zero[:]).then_inc(once_act, 1)

            def fx_sqrt(k):
                act.wait_ge(fx_red, k + 1)
                act.activation(fst[:, 1, k, :], fst[:, 0, k, :], ACT.Sqrt, bias=eps[:]).then_inc(fx_rms, 1)

            def fx_evac(k):
                n, t = 3 + k // T, k % T
                dst = qT_fox if n < 5 else kT_fox
                h = 4 * ((n - 3) % 2)
                act.wait_ge(fx_tr, k + 1)
                act.activation(dst[:, h:h + 4, t * P:(t + 1) * P],
                               ps[:, k % 4, :].rearrange("p (a n) -> p a n", a=4), ACT.Copy).then_inc(fx_ev, 1)

            for j in range(9 * T):
                n, t = j // T, j % T
                k = j - 3 * T
                act.wait_ge(p2_acc, j + 1)
                b = ps[:, 4 + j % 4, 0:256]
                if n < 3:
                    w = 256 if n < 2 else LAT - 512
                    act.activation(lat[:, t, 256 * n:256 * n + w], b[:, 0:w], ACT.Copy)
                elif n < 7:
                    if k >= 1:
                        act.wait_ge(fx_red, k)
                    if k >= 2:
                        act.wait_ge(fx_tok, k - 1)
                    act.activation(fsq, b, ACT.Square, scale=1 / 8, bias=zero[:])
                    act.activation(fraw[:, k % 2, :], b, ACT.Copy)
                else:
                    act.activation(v_fox[:, t, 256 * (n - 7):256 * (n - 6)], b, ACT.Copy)
                act.drain().then_inc(p2_ev, 1)
                if n == 2 and t == T - 1:
                    act.wait_ge(once_dve, LOGITS)
                    act.activation(logf[:, 1, :], logf[:, 1, :], ACT.Exp, bias=zero[:])
                    act.drain()
                    act.activation(logf[:, 1, :], logf[:, 1, :], ACT.Ln, bias=ones[:, 0:1]).then_inc(once_act, 1)
                if 1 <= k <= 16:
                    fx_sqrt(k - 1)
                if 3 <= k < 19:
                    fx_evac(k - 3)

            def latent_evac(t):
                for g in range(4):
                    dst = qT_mla if g < 2 else kT_mla
                    act.wait_ge(mq_tr, 4 * t + g + 1)
                    act.activation(dst[0:MLA_QK, 4 * (g % 2):4 * (g % 2) + 4, t * P:(t + 1) * P],
                                   ps[0:MLA_QK, 6 + g % 2, :].rearrange("p (a n) -> p a n", a=4),
                                   ACT.Copy).then_inc(mq_ev, 1)

            act.wait_ge(p2_acc, 9 * T)
            junk = msq[:, 0].rearrange("p a b -> p (a b)")
            for t in range(T):
                for i, (at, n) in enumerate(((0, QR), (QR, KVR))):
                    act.drain()
                    act.activation(junk[:, 0:n], lat[:, t, at:at + n], ACT.Square, scale=n ** -0.5, bias=zero[:],
                                   accum_out=lst[:, 0, 2 * t + i:2 * t + i + 1])
            act.drain()
            act.activation(lst[:, 1, :], lst[:, 0, :], ACT.Sqrt, bias=eps[:]).then_inc(la_rms, 1)
            for t in range(T):
                qtok, ktok = qktok[t % 2]
                act.wait_ge(la_acc, t + 1)
                if t >= 2:
                    act.wait_ge(mq_tr, 4 * (t - 1))
                if t >= 1:
                    act.wait_ge(mq_red, t)
                if t == 0:
                    act.wait_ge(fx_tr, 16)
                act.activation(qtok, ps[:, 2:4, 0:384].rearrange("p a (b n) -> p a b n", n=MLA_QK), ACT.Copy)
                kv = ps[:, 4:6, :].rearrange("p a (b n) -> p (a b) n", n=P)
                act.activation(ktok[:, :, 0:64], kv[:, :, 0:64], ACT.Copy)
                act.activation(v_mla[:, t, :].rearrange("p (h n) -> p h n", h=8), kv[:, :, 64:P], ACT.Copy)
                act.activation(ktok[:, :, 64:96], each(lat[:, t, 640:672], 8), ACT.Copy)
                act.drain()
                act.activation(msq[:, 0], qtok, ACT.Square, bias=zero[:])
                act.activation(msq[:, 1], ktok, ACT.Square, bias=zero[:])
                act.drain().then_inc(la_ev, 1)
                if t:
                    latent_evac(t - 1)
                act.wait_ge(mq_red, t + 1)
                act.activation(mst[:, 1, t, :], mst[:, 0, t, :], ACT.Sqrt, bias=eps[:],
                               scale=1 / MLA_QK).then_inc(mq_rms, 1)
            latent_evac(T - 1)

            for i in range(T * HEADS2 + 1):
                if i < T * HEADS2:
                    t, h = i // HEADS2, i % HEADS2
                    act.wait_ge(max2, i + 1)
                    if i >= 4:
                        act.wait_ge(pt2, i - 3)
                    act.activation(prob2[:, i % 4, 0:(t + 1) * P], ps[:, i % 2, 0:(t + 1) * P], ACT.Exp,
                                   scale=MLA_SCALE if h < 8 else SCALE, bias=sst2[:, 1, i:i + 1],
                                   accum_out=sst2[:, 2, i:i + 1])
                    act.drain().then_inc(exp2, 1)
                if i >= 1:
                    u = i - 1
                    act.wait_ge(pt2, u + 1)
                    if u >= 2:
                        act.wait_ge(av2, u - 1)
                    n = (u // HEADS2 + 1) * P
                    act.activation(probT2[:, u % 2, 0:n], ps[:, 2 + u % 2, 0:n], ACT.Copy).then_inc(pt2_done, 1)

            mix_and_norm(T, 3, xn4)

            for t in range(T):
                act.wait_ge(h2_tr, t + 1)
                act.activation(h2[:, t, :].rearrange("p (a b) -> p a b", a=2),
                               ps[:, 4 + 2 * (t % 2):6 + 2 * (t % 2), :], ACT.Copy).then_inc(h2_ev, 1)
            for c in range(17):
                if c < 16:
                    act.wait_ge(qp_acc, c + 1)
                    if c >= 4:
                        act.wait_ge(sk_acc, c - 3)
                    act.activation(qpT[:, c % 4, :], ps[:, c % 4, :], ACT.Copy).then_inc(qp_ev, 1)
                if c >= 1:
                    act.wait_ge(sk_acc, c)
                    act.activation(scf[:, :, (c - 1) * P:c * P],
                                   ps[:, 4 + (c - 1) % 4, :].rearrange("p (t n) -> p t n", t=T),
                                   ACT.Copy).then_inc(sk_ev, 1)
            for t in range(T):
                act.wait_ge(dots_done, PH * (t + 1))
                g = gate[:, t * SLOTS:(t + 1) * SLOTS]
                act.activation(g, g, ACT.Exp, bias=zero[:]).then_inc(gate_exp, 1)
                act.activation(dots, dots, ACT.Gelu_apprx_tanh, bias=zero[:]).then_inc(gelu_done, 1)
                act.wait_ge(w_ready, t + 1)
                own = by_pe(t)
                if t == T - 1:
                    for k in range(12, TOPK):
                        act.wait_ge(v_free[k], t * PH + 1)
                with act.Fori(0, PH) as h:
                    for j, k in enumerate(own):
                        if j >= 4:
                            act.wait_ge(v_free[own[j - 4]], h + (t * PH + 2))
                        else:
                            act.wait_ge(v_free[own[j - 4]], h + (t * PH + 1))
                        act.activation(diag[:, j % 4, :], ident, ACT.Copy,
                                       scale=wts[:, t % 2, bass.ds(h * TOPK + k, 1)]).then_inc(diag_ready, 1)

        @block.vector
        def _(v):
            v.memset(zero[:], 0.0)
            v.memset(eps[:], EPS)
            v.drain().then_inc(setup_dve, 1)

            def norm(layer, tiles, buf):
                tiles = list(tiles)

                def scaled(t):
                    o, n = ln_base[layer] + t, rows_of(t)
                    v.wait_ge(ln_rms, o + 1)
                    v.reciprocal(lnst[0:n, 2, o:o + 1], lnst[0:n, 1, o:o + 1])
                    v.drain()
                    src = xmeta[0:n, :] if t == T else x[:, t, :]
                    v.tensor_scalar(buf[0:n, t % 2, :], src, lnst[0:n, 2, o:o + 1], None, ALU.mult).then_inc(ln_xn, 1)

                def evac(t):
                    o, n = ln_base[layer] + t, rows_of(t)
                    v.wait_ge(ln_tr, o + 1)
                    b = 2 if layer in (1, 3) else 2 * (t % 2)
                    src = ps[:, b:b + 2, :].rearrange("p a (b n) -> p (a b) n", n=P)[:, :, 0:n]
                    dst = hT[:, :, t * P:t * P + n]
                    g = [cols[:, C_G1:C_G1 + KD], cols[:, C_GF:C_GF + KD], gs[:, 0, :], gs[:, 1, :]][layer]
                    if layer == 0:
                        v.tensor_tensor(dst, src, over(g, n), ALU.mult).then_inc(ln_hT, 1)
                    elif layer == 1:
                        full, high = h_full[:, :, t * P:t * P + n], h_hi[:, :, t * P:t * P + n]
                        v.tensor_tensor(full, src, over(g, n), ALU.mult)
                        v.drain()
                        v.tensor_copy(high, full)
                        v.drain()
                        v.tensor_tensor(h_lo[:, :, t * P:t * P + n], full, high.bitcast(F32),
                                        ALU.subtract).then_inc(ln_hT, 1)
                    else:
                        shift = mod[:, 24 * (layer - 2):24 * (layer - 2) + KD]
                        v.tensor_tensor(dst, src, over(g, n), ALU.mult)
                        v.drain()
                        v.tensor_tensor(dst, dst, over(shift, n), ALU.add).then_inc(ln_hT, 1)

                return scaled, evac

            def norm_all(layer, tiles, buf):
                scaled, evac = norm(layer, tiles, buf)
                for t in tiles:
                    scaled(t)
                    if t:
                        evac(t - 1)
                evac(tiles[-1])

            v.wait_ge(const_in_s, 32)
            norm_all(0, range(T + 1), xn)
            v.wait_ge(rope_in_s, 48)
            for kind in range(4):
                for sw in range(2):
                    v.tensor_tensor(rope[:, 2 * kind + sw], ropec[:, 2 * (kind // 2) + sw],
                                    each(ropeg[:, 2 * kind + sw, :], 5), ALU.mult)
            v.drain()

            def pj_reduce(j):
                n, t = pj_jobs[j]
                r, hh = rows_of(t), 2 if n == 2 else 4
                v.wait_ge(pj_raw, j + 1)
                v.tensor_reduce(qst[0:r, j % 4, 0, 0:hh],
                                sqb[0:r, j % 2, 0:64 * hh].rearrange("p (h d) -> p h d", h=hh), AX.X, ALU.add)
                if hh == 2:
                    v.memset(qst[0:r, j % 4, 0, 2:4], 1.0)
                v.drain().then_inc(pj_red, 1)

            def pj_rope(j):
                n, t = pj_jobs[j]
                r, hh = rows_of(t), 2 if n == 2 else 4
                kind = (0, 0, 1, 2, 2, 3, 3)[n]
                w = 64 * hh
                v.wait_ge(pj_rms, j + 1)
                v.reciprocal(qst[0:r, j % 4, 2, 0:hh], qst[0:r, j % 4, 1, 0:hh])
                v.drain()
                src = raw[0:r, j % 3, 0:w].rearrange("p (h d) -> p h d", h=hh)
                a = xr[0:r, 0:w].rearrange("p (h d) -> p h d", h=hh)
                v.tensor_tensor(a, src, over(qst[0:r, j % 4, 2, 0:hh], HD), ALU.mult)
                v.drain()
                straight = ra[0:r, 0:w].rearrange("p (h d) -> p h d", h=hh)
                swapped = rb[0:r, 0:w].rearrange("p (h i two) -> p h i two", h=hh, two=2)
                a2 = xr[0:r, 0:w].rearrange("p (h i two) -> p h i two", h=hh, two=2)
                tb = rope[0:r, 2 * kind + 1, t, :].rearrange("p (i two) -> p i two", two=2)
                v.tensor_tensor(straight, a, each(rope[0:r, 2 * kind, t, :], hh), ALU.mult)
                v.tensor_tensor(swapped[:, :, :, 0], a2[:, :, :, 1], each(tb[:, :, 0], hh), ALU.mult)
                v.tensor_tensor(swapped[:, :, :, 1], a2[:, :, :, 0], each(tb[:, :, 1], hh), ALU.mult)
                v.drain()
                if j >= 3:
                    v.wait_ge(pj_tr, j - 2)
                if n == 2:
                    dst = tok[0:r, j % 3, :].rearrange("p (h two d) -> p h two d", h=2, two=2)
                    rb3 = rb[0:r, 0:w].rearrange("p (h d) -> p h d", h=hh)
                    v.tensor_tensor(dst[:, :, 0, :], straight, rb3, ALU.add)
                    v.tensor_tensor(dst[:, :, 1, :], straight, rb3, ALU.add)
                    v.drain().then_inc(pj_tok, 1)
                else:
                    v.tensor_tensor(tok[0:r, j % 3, :], ra[0:r, :], rb[0:r, :], ALU.add).then_inc(pj_tok, 1)
                    v.drain()

            for j in range(QK + 1):
                if j < QK:
                    pj_reduce(j)
                if j >= 1:
                    pj_rope(j - 1)

            lq = rowsa[:, RA_LAM - 512:RA_LAM - 256].rearrange("p (a d) -> p a d", a=4)
            v.tensor_tensor(xr[:, 0:64], lq[:, 0, :], lq[:, 1, :], ALU.mult)
            v.tensor_tensor(xr[:, 64:128], lq[:, 2, :], lq[:, 3, :], ALU.mult)
            v.drain()
            v.tensor_reduce(neglam[:, 0:2], xr[:, 0:128].rearrange("p (a d) -> p a d", a=2), AX.X,
                            ALU.add).then_inc(once_dve, 1)
            v.wait_ge(once_act, LAM_EXP)
            v.tensor_tensor(neglam[:, 0:1], neglam[:, 3:4], neglam[:, 2:3], ALU.subtract)
            v.drain()
            v.tensor_scalar(neglam[:, 1:2], neglam[:, 0:1], LAM_INIT, None, ALU.subtract)
            v.drain()

            def score_max(s):
                v.wait_ge(s_ready, s + 1)
                v.tensor_reduce(sst[:, 0, s:s + 1], ps[:, 2 * (s % 2):2 * (s % 2) + 2, 0:HALF], AX.XY, ALU.max)
                v.drain()
                v.tensor_scalar(sst[:, 1, s:s + 1], sst[:, 0, s:s + 1], -SCALE, None, ALU.mult).then_inc(max_ready, 1)

            def finish_probs(i):
                t, s, n, h = pv_jobs[i]
                v.wait_ge(exp_done, s + n)
                v.reciprocal(sst[:, 3, s:s + n], sst[:, 2, s:s + n])
                v.drain()
                if n == 2:
                    c = 4 * t + h
                    v.tensor_scalar(coef[:, c:c + 1], sst[:, 2, s:s + 1], sst[:, 3, s + 1:s + 2], neglam[:, 1:2],
                                    ALU.mult, ALU.mult)
                    v.drain()
                    v.scalar_tensor_tensor(out=prob[:, s % 4, :], in0=prob[:, (s + 1) % 4, :], scalar=coef[:, c:c + 1],
                                           in1=prob[:, s % 4, :], op0=ALU.mult, op1=ALU.add)
                    v.drain().then_inc(comb_done, 1)

            def meta_probs(i):
                v.wait_ge(pt_ready, i + 1)
                if i >= 2:
                    v.wait_ge(av_ready, i - 1)
                v.tensor_copy(probT[0:META, i % 2, 512:640], ps[0:META, 6 + i % 2, 0:P]).then_inc(ptb_done, 1)

            def head_out(i):
                t, s, n, h = pv_jobs[i]
                v.wait_ge(av_ready, i + 1)
                o = P
                if n == 1:
                    o += 64 * (h // 4)
                    v.tensor_scalar(mixed[:, t, 64 * h:64 * h + 64], ps[:, 6 + i % 2, o:o + 64], sst[:, 3, s:s + 1], None,
                                    ALU.mult).then_inc(o_done, 1)
                else:
                    at = 512 + P * h
                    v.tensor_scalar(mixed[:, t, at:at + P], ps[:, 6 + i % 2, o:o + P], sst[:, 3, s:s + 1], None,
                                    ALU.mult).then_inc(o_done, 1)

            for i in range(NPV + 2):
                if i < NPV:
                    _, s, n, _ = pv_jobs[i]
                    for j in range(n):
                        score_max(s + j)
                if i >= 1 and i - 1 < NPV:
                    finish_probs(i - 1) if i - 1 < 0 else None
                if i < NPV:
                    finish_probs(i)
                if 1 <= i <= NPV:
                    meta_probs(i - 1)
                if i >= 2:
                    head_out(i - 2)

            for t in range(T):
                o = mixed[:, t, 512:D]
                v.drain()
                v.tensor_tensor(sqo, o, o, ALU.mult)
                v.drain()
                v.tensor_reduce(ost[:, 0, 4 * t:4 * t + 4], sqo.rearrange("p (h d) -> p h d", h=4), AX.X,
                                ALU.add).then_inc(sub_sq, 1)
            for t in range(T):
                o = mixed[:, t, 512:D].rearrange("p (h d) -> p h d", h=4)
                v.wait_ge(sub_rms, t + 1)
                v.reciprocal(ost[:, 2, 4 * t:4 * t + 4], ost[:, 1, 4 * t:4 * t + 4])
                v.drain()
                v.tensor_tensor(o, o, over(ost[:, 2, 4 * t:4 * t + 4], P), ALU.mult)
                v.drain()
                v.scalar_tensor_tensor(out=o, in0=o, scalar=1.0 - LAM_INIT,
                                       in1=each(rowsa[:, 0:P], 4), op0=ALU.mult, op1=ALU.mult).then_inc(mix_ready, 1)

            def low_part(f):
                v.wait_ge(w_hi_done, f + 1)
                slot = (W_GU + f) % WR
                v.tensor_tensor(w_lo[:, slot, :], ring[:, slot, :], w_hi[:, f % 2, :].bitcast(F32),
                                ALU.subtract).then_inc(w_lo_done, 1)

            scaled, evac = norm(1, range(T), xn1)
            for t in range(T):
                for n in range(4):
                    v.wait_ge(out_acc, 4 * t + n + 1)
                    xs = x[:, t, 256 * n:256 * n + 256]
                    v.tensor_tensor(xs, xs, ps[:, 4 + n, 0:256], ALU.add).then_inc(out_add, 1)
                scaled(t)
                if t:
                    evac(t - 1)
            low_part(0)
            evac(T - 1)
            low_part(1)

            v.wait_ge(once_act, C_EXP)
            v.tensor_scalar(ctmp, ctmp, 1.0, None, ALU.add)
            v.drain()
            v.reciprocal(ctmp, ctmp)
            v.drain()
            v.tensor_tensor(crow, crow, ctmp, ALU.mult)
            v.drain()

            def modulation(m):
                v.wait_ge(ada_load[m % 4], 16 * (m // 4 + 1))
                v.tensor_tensor_reduce(out=adar[:, m % 4, :], in0=adar[:, m % 4, :], in1=crow, scale=1.0, scalar=0.0,
                                       op0=ALU.mult, op1=ALU.add, accum_out=mod[:, m:m + 1])
                v.drain().then_inc(ada_used, 1)

            for f in range(NF):
                v.wait_ge(silu_done, f + 1)
                v.tensor_tensor(aT[:, f, :], sg[:, f % 2, :], ps[:, 2 * (f % 2) + 1, :], ALU.mult).then_inc(act_ready, 1)
                if f + 2 < NF:
                    low_part(f + 2)
                for m in range(3 * f, min(3 * f + 3, 48)):
                    modulation(m)
            v.tensor_tensor(mod[:], mod[:], cols[:, C_BADA:C_BADA + 48], ALU.add)
            v.drain()
            for g in range(2):
                scale = mod[:, 24 * g + KD:24 * g + 2 * KD]
                gain = cols[:, C_N1 + KD * g:C_N1 + KD * g + KD]
                v.scalar_tensor_tensor(out=gs[:, g, :], in0=scale, scalar=1.0, in1=gain, op0=ALU.add, op1=ALU.mult)
                if g:
                    v.wait_ge(gate_acc, 1)
                v.tensor_copy(gbc, over(mod[:, 24 * g + 16:24 * g + 24], P)).then_inc(gbc_ready, 1)

            for t in range(T):
                for half in range(2):
                    v.wait_ge(down_acc, 2 * t + half + 1)
                    xs = x[:, t, 512 * half:512 * half + 512]
                    v.tensor_tensor(xs, xs, ps[:, 2 * t + half, :], ALU.add).then_inc(down_add, 1)

            norm_all(2, range(T), xn)

            v.wait_ge(rowsb_in_s, 32)
            posf = fst[:, 0, 0, :]
            v.tensor_copy(posf, pos[:])
            v.drain()
            ang, turn = trig[:, 4, :], trig[:, 0, :]
            v.tensor_tensor(ang.rearrange("p (t f) -> p t f", t=T), over(posf, 16), each(freq, T), ALU.mult)
            v.drain()
            for q, quarter in ((2, 0.25), (3, 0.0)):
                red = trig[:, q, :]
                v.tensor_scalar(turn, ang, 1.0 / TWO_PI, quarter, ALU.mult, ALU.add)
                v.drain()
                v.tensor_scalar(turn, turn, ROUND, None, ALU.add)
                v.drain()
                v.tensor_scalar(turn, turn, ROUND, None, ALU.subtract)
                v.drain()
                src = ang
                for part in (PI2_A, PI2_B, PI2_C):
                    v.scalar_tensor_tensor(out=red, in0=turn, scalar=-part, in1=src, op0=ALU.mult, op1=ALU.add)
                    v.drain()
                    src = red
                if quarter:
                    v.tensor_scalar(red, red, float(np.pi / 2), None, ALU.add)
                    v.drain()
                v.tensor_scalar(red, red, PI_F, -PI_F, ALU.min, ALU.max)
                v.drain()
            v.drain().then_inc(once_dve, 1)

            v.wait_ge(p2_ev, 3 * T)
            y = logf[:, 0, :]
            v.tensor_tensor(y.rearrange("p (t h) -> p t h", t=T), lat[:, :, 672:680],
                            each(rowsb[:, RB_BF - D:RB_BF - D + 8], T), ALU.add)
            v.drain()
            v.scalar_tensor_tensor(out=logf[:, 1, :], in0=y, scalar=-1.0, in1=y, op0=ALU.mult, op1=ALU.min).then_inc(once_dve, 1)
            v.wait_ge(once_act, LOG)
            v.tensor_scalar(logf[:, 2, :], y, 0.0, None, ALU.min)
            v.drain()
            v.tensor_tensor(logf[:, 2, :], logf[:, 2, :], logf[:, 1, :], ALU.subtract).then_inc(once_dve, 1)
            v.wait_ge(fc_acc, 1)
            f8 = ps[:, 3, 0:32].rearrange("p (t h) -> p t h", t=T)
            v.tensor_scalar(fcum[:, 0], f8, 8.0, None, ALU.mult)
            v.tensor_scalar(fcum[:, 1], f8, -8.0, None, ALU.mult)
            v.drain().then_inc(once_dve, 1)

            v.wait_ge(setup_pool, 2)
            for k in range(17):
                if k < 16:
                    v.wait_ge(p2_ev, 3 * T + k + 1)
                    v.tensor_reduce(fst[:, 0, k, :], fsq.rearrange("p (h d) -> p h d", h=4), AX.X, ALU.add).then_inc(fx_red, 1)
                if k >= 1:
                    q = k - 1
                    n, t = 3 + q // T, q % T
                    isk = n >= 5
                    g = rowsb[:, (RB_FK if isk else RB_FQ) - D:][:, 0:64]
                    v.wait_ge(fx_rms, q + 1)
                    v.reciprocal(fst[:, 2, q, :], fst[:, 1, q, :])
                    v.drain()
                    src = fraw[:, q % 2, :].rearrange("p (h d) -> p h d", h=4)
                    v.tensor_tensor(src, src, over(fst[:, 2, q, :], HD), ALU.mult)
                    if q >= 2:
                        v.wait_ge(fx_tr, q - 1)
                    else:
                        v.drain()
                    buf = ftok[:, 2 * isk + q % 2]
                    v.drain()
                    v.tensor_tensor(buf[:, :, 0:64], src, each(g, 4), ALU.mult)
                    at = HD if isk else HD + 1
                    h = 4 * ((n - 3) % 2)
                    v.tensor_copy(buf[:, :, at], fcum[:, 1 if isk else 0, t, h:h + 4])
                    v.drain().then_inc(fx_tok, 1)

            v.wait_ge(la_rms, 1)
            v.reciprocal(lst[:, 2, :], lst[:, 1, :])
            v.drain()
            v.wait_ge(once_act, SINES)
            def latent_in(t):
                if t:
                    v.wait_ge(la_tr, t)
                v.tensor_scalar(latn[:, 0:QR], lat[:, t, 0:QR], lst[:, 2, 2 * t:2 * t + 1], None, ALU.mult)
                v.tensor_scalar(latn[:, QR:640], lat[:, t, QR:640], lst[:, 2, 2 * t + 1:2 * t + 2], None, ALU.mult)
                v.drain().then_inc(la_n, 1)
                v.wait_ge(la_tr, t + 1)
                if t >= 2:
                    v.wait_ge(la_acc, t - 1)
                dst = latT[:, t % 2, :].rearrange("p (a n) -> p a n", a=5)
                v.tensor_tensor(dst[:, 0:3], ps[:, 0, 0:QR].rearrange("p (a n) -> p a n", a=3),
                                over(cols[:, C_QA:C_QA + 3], P), ALU.mult)
                v.tensor_tensor(dst[:, 3:5], ps[:, 1, 0:KVR].rearrange("p (a n) -> p a n", a=2),
                                over(cols[:, C_KVA:C_KVA + 2], P), ALU.mult)
                v.drain().then_inc(la_T, 1)

            latent_in(0)
            for t in range(T):
                if t + 1 < T:
                    latent_in(t + 1)
                v.wait_ge(la_ev, t + 1)
                v.tensor_reduce(mst[:, 0, t, :].rearrange("p (a b) -> p a b", a=2), msq, AX.X, ALU.add).then_inc(mq_red, 1)
                v.wait_ge(mq_rms, t + 1)
                v.reciprocal(mst[:, 2, t, :], mst[:, 1, t, :])
                v.drain()
                bufs = list(enumerate(qktok[t % 2]))
                for i, buf in bufs:
                    v.tensor_tensor(buf, buf, over(mst[:, 2, t, 8 * i:8 * i + 8], MLA_QK), ALU.mult)
                v.drain()
                for i, buf in bufs:
                    row = (RB_MQ, RB_MK)[i] - D
                    v.tensor_tensor(buf, buf, each(rowsb[:, row:row + MLA_QK], 8), ALU.mult)
                v.drain()
                cos = each(trig[:, 0, 16 * t:16 * t + 16], 8)
                sin = each(trig[:, 1, 16 * t:16 * t + 16], 8)
                for i, buf in bufs:
                    lo, hi = buf[:, :, 64:80], buf[:, :, 80:96]
                    v.tensor_tensor(rp[:, 0], lo, cos, ALU.mult)
                    v.tensor_tensor(rp[:, 1], hi, sin, ALU.mult)
                    v.tensor_tensor(rp[:, 2], hi, cos, ALU.mult)
                    v.tensor_tensor(rp[:, 3], lo, sin, ALU.mult)
                    v.drain()
                    v.tensor_tensor(lo, rp[:, 0], rp[:, 1], ALU.subtract)
                    v.tensor_tensor(hi, rp[:, 2], rp[:, 3], ALU.add)
                    v.drain().then_inc(mq_tok, 1)

            for i in range(T * HEADS2 + 2):
                if i < T * HEADS2:
                    t, h = i // HEADS2, i % HEADS2
                    v.wait_ge(s2_ready, i + 1)
                    v.tensor_reduce(sst2[:, 0, i:i + 1], ps[:, i % 2, 0:(t + 1) * P], AX.X, ALU.max)
                    v.drain()
                    v.tensor_scalar(sst2[:, 1, i:i + 1], sst2[:, 0, i:i + 1], -MLA_SCALE if h < 8 else -SCALE, None,
                                    ALU.mult).then_inc(max2, 1)
                if i >= 2:
                    u = i - 2
                    t, h = u // HEADS2, u % HEADS2
                    v.wait_ge(exp2, u + 1)
                    v.reciprocal(sst2[:, 3, u:u + 1], sst2[:, 2, u:u + 1])
                    v.drain()
                    v.wait_ge(av2, u + 1)
                    o = 64 * (h % 2)
                    v.tensor_scalar(mixed2[:, t, 64 * h:64 * h + 64], ps[:, 4 + u % 2, o:o + 64], sst2[:, 3, u:u + 1],
                                    None, ALU.mult).then_inc(o2_done, 1)

            scaled, evac = norm(3, range(T), xn4)
            for t in range(T):
                for n in range(4):
                    v.wait_ge(out_acc, 4 * (T + t) + n + 1)
                    tmp = gtmp[:, n % 2, :]
                    v.tensor_tensor(tmp, ps[:, 4 + n, 0:256], gates[:, 0, 256 * n:256 * n + 256], ALU.mult)
                    v.drain()
                    xs = x[:, t, 256 * n:256 * n + 256]
                    v.tensor_tensor(xs, xs, tmp, ALU.add).then_inc(out_add, 1)
                v.drain()
                scaled(t)
                if t:
                    evac(t - 1)
            evac(T - 1)

            def best(src, spare, vals, inds):
                v.max(vals[:, 0:8], src)
                v.drain()
                v.max_index(inds[:, 0:8], vals[:, 0:8], src)
                v.match_replace(out=spare, in_to_replace=vals[:, 0:8], in_values=src, imm_value=LOW)
                v.drain()
                v.max(vals[:, 8:16], spare)
                v.drain()
                v.max_index(inds[:, 8:16], vals[:, 8:16], spare)
                v.drain()

            PARTS = 5

            def choose(part, head):
                if part == 0:
                    v.tensor_copy(hsc.rearrange("p a b -> p (a b)"), sc[:, bass.ds(head * 256, 256)])
                    v.drain()
                    best(hsc[:, 0, :], sc2, topv[:, 0, :], topi[:, 0, :])
                elif part == 1:
                    best(hsc[:, 1, :], sc2, topv[:, 1, :], topi[:, 1, :])
                    v.tensor_tensor(cand[:, 0, :].rearrange("p (a b) -> p a b", a=TOPK), over(topv[:, 0, :], TOPK),
                                    each(topv[:, 1, :], TOPK), ALU.add)
                    v.tensor_copy(topf, topi)
                    v.drain()
                elif part == 2:
                    best(cand[:, 0, :], cand[:, 1, :], bestv, besti)
                elif part == 3:
                    v.tensor_scalar(gate[:, bass.ds(head * TOPK, TOPK)], bestv, bestv[:, 0:1], None, ALU.subtract)
                    v.tensor_scalar(bits[:, 0, :], besti, 4, None, ALU.logical_shift_right)
                    v.tensor_scalar(bits[:, 1, :], besti, 15, None, ALU.bitwise_and)
                    v.drain()
                    v.tensor_copy(bitf, bits)
                    v.drain()
                else:
                    for half in range(2):
                        v.tensor_tensor(hot, over(bitf[:, half, :], 16), each(iota, TOPK), ALU.is_equal)
                        v.drain()
                        v.tensor_tensor(hot, hot, each(topf[:, half, :], TOPK), ALU.mult)
                        v.drain()
                        v.tensor_reduce(e12[:, half, :], hot, AX.X, ALU.add)
                        v.drain()
                    v.scalar_tensor_tensor(out=expf, in0=e12[:, 0, :], scalar=float(NKEYS), in1=e12[:, 1, :],
                                           op0=ALU.mult, op1=ALU.add)
                    v.drain()
                    v.tensor_copy(idx[:, bass.ds(head * TOPK, TOPK)], expf).then_inc(idx_ready, 1)

            def dots_of(t, h, following):
                for k in range(TOPK):
                    v.wait_ge(u_in[k % UR], h * 32 + (2 * t * PH + k // UR + 1) * 16)
                    v.tensor_tensor_reduce(out=urows[k % UR], in0=urows[k % UR], in1=h2[:, t, :], scale=1.0,
                                           scalar=0.0, op0=ALU.mult, op1=ALU.add,
                                           accum_out=dstage[:, k:k + 1]).then_inc(u_free[k % UR], 1)
                    if following is not None and k % 3 == 1:
                        choose(k // 3, following)
                v.drain()
                v.tensor_copy(dots[:, bass.ds(h * TOPK, TOPK)], dstage).then_inc(dots_done, 1)
                v.drain()

            def finish(t):
                v.wait_ge(y_acc, t + 1)
                y = ps[:, 2 * (t % 2):2 * (t % 2) + 2, :]
                if t == T - 1:
                    v.tensor_tensor(y, y, yacc.rearrange("p (a b) -> p a b", a=2), ALU.add)
                    v.drain()
                v.tensor_tensor(y, y, gates[:, 1, :].rearrange("p (a b) -> p a b", a=2), ALU.mult)
                v.drain()
                xt = x[:, t, :].rearrange("p (a b) -> p a b", a=2)
                v.tensor_tensor(xt, xt, y, ALU.add).then_inc(y_ready, 1)
                v.drain()

            v.memset(zmat, 0.0)
            v.drain().then_inc(setup_dve, 1)
            v.wait_ge(sk_ev, 2)
            for part in range(PARTS):
                choose(part, 0)
            v.wait_ge(h2_ev, T)
            for t in range(T):
                with v.Fori(0, PH - 1) as h:
                    if t == 0:
                        v.wait_ge(sk_ev, h * 2 + 4)
                    dots_of(t, h, h + (t * PH + 1))
                if t == 0:
                    v.wait_ge(sk_ev, 16)
                dots_of(t, PH - 1, (t + 1) * PH if t + 1 < T else None)
                g3 = gate[:, t * SLOTS:(t + 1) * SLOTS].rearrange("p (h k) -> p h k", h=PH)
                v.wait_ge(gate_exp, t + 1)
                v.tensor_reduce(gst[:, 0, :], g3, AX.X, ALU.add)
                v.drain()
                v.reciprocal(gst[:, 1, :], gst[:, 0, :])
                v.drain()
                v.tensor_tensor(g3, g3, over(gst[:, 1, :], TOPK), ALU.mult)
                v.drain()
                v.wait_ge(gelu_done, t + 1)
                v.tensor_tensor(wts[:, t % 2, :], dots, gate[:, t * SLOTS:(t + 1) * SLOTS], ALU.mult).then_inc(w_ready, 1)
                v.drain()
                if t:
                    finish(t - 1)
            v.memset(yacc, 0.0)
            v.drain()
            with v.Fori(0, PH) as h:
                for k in range(TOPK):
                    if k not in by_pe(T - 1):
                        v.wait_ge(v_in[k], h * 16 + ((T - 1) * PH + 1) * 16)
                        v.scalar_tensor_tensor(out=yacc, in0=vrows[:, k, :],
                                               scalar=wts[:, (T - 1) % 2, bass.ds(h * TOPK + k, 1)], in1=yacc,
                                               op0=ALU.mult, op1=ALU.add).then_inc(v_free[k], 1)
                        v.drain()
            finish(T - 1)

        @block.tensor
        def _(pe):
            pe.wait_ge(const_in_s, 32)

            def norm(layer, tiles, buf):
                for t in tiles:
                    o, n = ln_base[layer] + t, rows_of(t)
                    pe.wait_ge(ln_xn, o + 1)
                    if layer in (1, 3):
                        b = 2
                        if t:
                            pe.wait_ge(ln_hT, o)
                    else:
                        b = 2 * (t % 2)
                        if t >= 2:
                            pe.wait_ge(ln_hT, o - 1)
                    for k in range(KD):
                        mm = pe.transpose(ps[:, b + k // 4, P * (k % 4):P * (k % 4) + n],
                                          buf[0:n, t % 2, P * k:P * k + P], ident[0:n, 0:n])
                    mm.then_inc(ln_tr, 1)

            norm(0, range(T + 1), xn)

            def linear(c, t, bank, r=P, w=256):
                wt = ring[:, c % WR, :].rearrange("p (k n) -> p k n", k=KD)
                for k in range(KD):
                    mm = pe.matmul(ps[0:r, bank, 0:w], hT[:, k, t * P:t * P + r], wt[:, k, 0:w],
                                   start=(k == 0), stop=(k == KD - 1))
                return mm

            def pj_transposes(j):
                n, t = pj_jobs[j]
                r = rows_of(t)
                pe.wait_ge(pj_tok, j + 1)
                if j >= 4:
                    pe.wait_ge(pj_ev, j - 3)
                for c in range(2):
                    mm = pe.transpose(ps[:, j % 4, P * c:P * c + r], tok[0:r, j % 3, P * c:P * c + P], ident[0:r, 0:r])
                mm.then_inc(pj_tr, 1)

            for j, (n, t) in enumerate(pj_jobs):
                chunk(pe, W_IN + n)
                pe.wait_ge(ln_hT, t + 1)
                if j >= 4:
                    pe.wait_ge(pj_raw, j - 3)
                mm = linear(W_IN + n, t, 4 + j % 4, rows_of(t))
                mm.then_inc(pj_acc, 1)
                if j + 1 == len(pj_jobs) or pj_jobs[j + 1][0] != n:
                    pe.drain().then_inc(w_used, 1)
                if 3 <= j < QK + 3:
                    pj_transposes(j - 3)

            pe.wait_ge(pj_ev, QK)
            pe.wait_ge(pj_raw, len(pj_jobs))

            def scores(s):
                t, l = s // 16, s % 16
                head = l
                kT = kTa[:, l // 4, :] if l < 8 else kTb[:, (l - 8) // 2, :]
                if s >= 2:
                    pe.wait_ge(exp_done, s - 1)
                for a in range(2):
                    mm = pe.matmul(ps[:, 2 * (s % 2) + a, 0:HALF], qz[:, head, t * P:(t + 1) * P],
                                   kT[:, a * HALF:(a + 1) * HALF], start=True, stop=True)
                mm.then_inc(s_ready, 1)

            def prob_transposes(i):
                t, s, n, h = pv_jobs[i]
                pe.wait_ge(exp_done, s + n)
                if n == 2:
                    pe.wait_ge(comb_done, 4 * t + h + 1)
                if i >= 2:
                    pe.wait_ge(pta_done, i - 1)
                    pe.wait_ge(ptb_done, i - 1)
                    pe.wait_ge(o_done, i - 1)
                pr = prob[:, s % 4, :]
                for k in range(T):
                    pe.transpose(ps[:, 4 + i % 2, P * k:P * k + P], pr[:, P * k:P * k + P], ident)
                mm = pe.transpose(ps[0:META, 6 + i % 2, 0:P], pr[:, 512:KEYS], ident)
                mm.then_inc(pt_ready, 1)

            def values(i):
                t, s, n, h = pv_jobs[i]
                pe.wait_ge(pta_done, i + 1)
                pe.wait_ge(ptb_done, i + 1)
                if i >= 2:
                    pe.wait_ge(o_done, i - 1)
                for k in range(T + 1):
                    r = rows_of(k)
                    vals = va[0:r, k, :] if n == 1 else vb[0:r, k, P * h:P * h + P]
                    mm = pe.matmul(ps[:, 6 + i % 2, P:2 * P], probT[0:r, i % 2, P * k:P * k + P],
                                   vals, start=(k == 0), stop=(k == T))
                mm.then_inc(av_ready, 1)

            for i in range(NPV + 2):
                if i < NPV:
                    _, s, n, _ = pv_jobs[i]
                    for j in range(n):
                        scores(s + j)
                if 1 <= i <= NPV:
                    prob_transposes(i - 1)
                if i >= 2:
                    values(i - 2)

            def mixed_linear(src, first, c0, layer, buf, ready):
                def transposes(t):
                    ready(t)
                    if t:
                        pe.wait_ge(mixt_ev, first + t)
                    for k in range(KD):
                        mm = pe.transpose(ps[:, k // 4, P * (k % 4):P * (k % 4) + P], src[:, t, P * k:P * k + P], ident)
                    mm.then_inc(mixt_tr, 1)

                transposes(0)
                for t in range(T):
                    if t + 1 < T:
                        transposes(t + 1)
                    pe.wait_ge(mixt_ev, first + t + 1)
                    for n in range(4):
                        chunk(pe, c0 + n)
                        if t:
                            pe.wait_ge(out_add, 4 * (first + t - 1) + n + 1)
                        mm = linear(c0 + n, t, 4 + n)
                        mm.then_inc(out_acc, 1)
                        if t == T - 1:
                            pe.drain().then_inc(w_used, 1)
                    if t:
                        norm(layer, [t - 1], buf)
                norm(layer, [T - 1], buf)

            pe.wait_ge(o_done, NPV)
            mixed_linear(mixed, 0, W_OUT, 1, xn1, lambda t: pe.wait_ge(mix_ready, t + 1))

            pe.wait_ge(ln_hT, 9)
            for f in range(NF):
                pe.wait_ge(w_lo_done, f + 1)
                if f >= 2:
                    pe.wait_ge(act_ready, f - 1)
                whi, wlo = (w.rearrange("p (k u n) -> p k u n", k=KD, u=2)
                            for w in (w_hi[:, f % 2, :], w_lo[:, (W_GU + f) % WR, :]))
                for u in range(2):
                    for k in range(KD):
                        for i, (w, h) in enumerate(((whi, h_hi), (whi, h_lo), (wlo, h_hi))):
                            mm = pe.matmul(ps[:, 2 * (f % 2) + u, :], w[:, k, u, :], h[:, k, 0:512],
                                           start=(k == 0 and i == 0), stop=(k == KD - 1 and i == 2))
                mm.then_inc(gu_acc, 1)
                pe.drain().then_inc(w_used, 1)
            pe.wait_ge(act_ready, NF)
            for g in range(2):
                pe.wait_ge(gbc_ready, g + 1)
                for k in range(KD):
                    mm = pe.matmul(ps[:, 4 + 2 * g + k // 4, P * (k % 4):P * (k % 4) + P], gbc[:, k, :], ident,
                                   start=True, stop=True)
                mm.then_inc(gate_acc, 1)
            pe.wait_ge(gate_ev, 2)
            for f in range(NF):
                c = W_DOWN + f // 2
                chunk(pe, c)
                wt = ring[:, c % WR, :].rearrange("p (j n) -> p j n", j=2)
                for t in range(T):
                    for half in range(2):
                        mm = pe.matmul(ps[:, 2 * t + half, :], aT[:, f, t * P:(t + 1) * P],
                                       wt[:, f % 2, 512 * half:512 * half + 512], start=(f == 0), stop=(f == NF - 1))
                        if f == NF - 1:
                            mm.then_inc(down_acc, 1)
                if f % 2:
                    pe.drain().then_inc(w_used, 1)

            norm(2, range(T), xn)


            def fx_transposes(k):
                pe.wait_ge(fx_tok, k + 1)
                if k >= 4:
                    pe.wait_ge(fx_ev, k - 3)
                buf = ftok[:, 2 * (k >= 8) + k % 2]
                for c in range(4):
                    mm = pe.transpose(ps[:, k % 4, P * c:P * c + P], buf[:, c, :], ident)
                mm.then_inc(fx_tr, 1)

            for j in range(9 * T):
                n, t = j // T, j % T
                k = j - 3 * T
                chunk(pe, W_IN2 + n)
                pe.wait_ge(ln_hT, 9 + t + 1)
                if j >= 4:
                    pe.wait_ge(p2_ev, j - 3)
                mm = linear(W_IN2 + n, t, 4 + j % 4, w=256 if n != 2 else LAT - 512)
                mm.then_inc(p2_acc, 1)
                if t == T - 1:
                    pe.drain().then_inc(w_used, 1)
                if k == 0:
                    pe.wait_ge(once_dve, LOG_GATES)
                    for u in range(T):
                        for w in range(u + 1):
                            mm = pe.matmul(ps[:, 3, 8 * u:8 * u + 8], triu if w == u else ones,
                                           logf[:, 2, 8 * w:8 * w + 8], start=(w == 0), stop=(w == u))
                    mm.then_inc(fc_acc, 1)
                    pe.wait_ge(once_dve, GATE_SUMS)
                if 3 <= k < 19:
                    fx_transposes(k - 3)

            for c in range(3):
                chunk(pe, W_LAT + c)
            uq = [ring[:, (W_LAT + k // 2) % WR, 768 * (k % 2):768 * (k % 2) + 768] for k in range(3)]
            ukv = ring[:, (W_LAT + 2) % WR, :].rearrange("p (k n) -> p k n", k=2)
            pe.wait_ge(fx_ev, 16)
            pe.wait_ge(p2_ev, 9 * T)
            def latent_out(t):
                for g in range(4):
                    buf = qktok[t % 2][g // 2]
                    pe.wait_ge(mq_tok, 2 * t + g // 2 + 1)
                    if 4 * t + g >= 2:
                        pe.wait_ge(mq_ev, 4 * t + g - 1)
                    for c in range(4):
                        mm = pe.transpose(ps[0:MLA_QK, 6 + g % 2, P * c:P * c + P], buf[:, 4 * (g % 2) + c, :], ident)
                    mm.then_inc(mq_tr, 1)

            for t in range(T):
                pe.wait_ge(la_n, t + 1)
                for k in range(5):
                    bank, at = (0, P * k) if k < 3 else (1, P * (k - 3))
                    mm = pe.transpose(ps[:, bank, at:at + P], latn[:, P * k:P * k + P], ident)
                mm.then_inc(la_tr, 1)
                pe.wait_ge(la_T, t + 1)
                if t:
                    pe.wait_ge(la_ev, t)
                lT = latT[:, t % 2, :].rearrange("p (a n) -> p a n", a=5)
                for half in range(2):
                    for k in range(3):
                        pe.matmul(ps[:, 2 + half, 0:384], lT[:, k, :], uq[k][:, 384 * half:384 * half + 384],
                                  start=(k == 0), stop=(k == 2))
                for half in range(2):
                    for k in range(2):
                        mm = pe.matmul(ps[:, 4 + half, :], lT[:, 3 + k, :], ukv[:, k, 512 * half:512 * half + 512],
                                       start=(k == 0), stop=(k == 1))
                mm.then_inc(la_acc, 1)
                if t:
                    latent_out(t - 1)
            latent_out(T - 1)
            pe.drain().then_inc(w_used, 3)
            pe.wait_ge(mq_ev, 4 * T)

            NU = T * HEADS2
            for i in range(NU + 2):
                if i < NU:
                    t, h = i // HEADS2, i % HEADS2
                    if i >= 2:
                        pe.wait_ge(exp2, i - 1)
                    n = (t + 1) * P
                    q = qT_mla[0:MLA_QK, h, t * P:n] if h < 8 else qT_fox[:, h - 8, t * P:n]
                    kk = kT_mla[0:MLA_QK, h, 0:n] if h < 8 else kT_fox[:, h - 8, 0:n]
                    pe.matmul(ps[:, i % 2, 0:n], q, kk, start=True, stop=False)
                    pe.matmul(ps[:, i % 2, t * P:n], ident, maskt, start=False, stop=True).then_inc(s2_ready, 1)
                if 1 <= i <= NU:
                    u = i - 1
                    pe.wait_ge(exp2, u + 1)
                    if u >= 2:
                        pe.wait_ge(pt2_done, u - 1)
                    for k in range(u // HEADS2 + 1):
                        mm = pe.transpose(ps[:, 2 + u % 2, P * k:P * k + P], prob2[:, u % 4, P * k:P * k + P], ident)
                    mm.then_inc(pt2, 1)
                if i >= 2:
                    u = i - 2
                    t, h = u // HEADS2, u % HEADS2
                    pe.wait_ge(pt2_done, u + 1)
                    if u >= 2:
                        pe.wait_ge(o2_done, u - 1)
                    for k in range(t + 1):
                        vv, hh = (v_mla, h) if h < 8 else (v_fox, h - 8)
                        mm = pe.matmul(ps[:, 4 + u % 2, 0:P], probT2[:, u % 2, P * k:P * k + P],
                                       vv[:, k, P * (hh // 2):P * (hh // 2) + P], start=(k == 0), stop=(k == t))
                    mm.then_inc(av2, 1)

            mixed_linear(mixed2, T, W_O2, 3, xn4, lambda t: pe.wait_ge(o2_done, NU))
            for t in range(T):
                pe.wait_ge(ln_hT, 13 + t + 1)
                if t == 0:
                    pe.wait_ge(out_add, 8 * T)
                if t >= 2:
                    pe.wait_ge(h2_ev, t - 1)
                b = 4 + 2 * (t % 2)
                for k in range(KD):
                    mm = pe.transpose(ps[:, b + k // 4, P * (k % 4):P * (k % 4) + P], hT[:, k, t * P:(t + 1) * P], ident)
                mm.then_inc(h2_tr, 1)
            pe.wait_ge(ln_hT, 17)
            pe.wait_ge(subk_in_s, 16)
            for c in range(17):
                if c < 16:
                    w = W_PQ + c // 2
                    chunk(pe, w)
                    if c >= 4:
                        pe.wait_ge(qp_ev, c - 3)
                    wt = ring[:, w % WR, :].rearrange("p (k n) -> p k n", k=KD)
                    for k in range(KD):
                        mm = pe.matmul(ps[:, c % 4, :], wt[:, k, P * (c % 2):P * (c % 2) + P], hT[:, k, 0:512],
                                       start=(k == 0), stop=(k == KD - 1))
                    mm.then_inc(qp_acc, 1)
                    if c % 2:
                        pe.drain().then_inc(w_used, 1)
                if c >= 1:
                    q = c - 1
                    pe.wait_ge(qp_ev, q + 1)
                    pe.wait_ge(h2_ev, T)
                    if q >= 4:
                        pe.wait_ge(sk_ev, q - 3)
                    for t in range(T):
                        mm = pe.matmul(ps[:, 4 + q % 4, P * t:P * t + P], qpT[:, q % 4, t * P:(t + 1) * P], subk[:, q, :],
                                       start=True, stop=True)
                    mm.then_inc(sk_acc, 1)

            pe.wait_ge(setup_dve, 2)
            for t in range(T):
                b = 2 * (t % 2)
                if t >= 2:
                    pe.wait_ge(y_ready, t - 1)
                for half in range(2):
                    pe.matmul(ps[:, b + half, :], zmat, const[:, 0:512], start=True, stop=False,
                              skip_group_check=True)
                own = by_pe(t)
                with pe.Fori(0, PH) as h:
                    for j, k in enumerate(own):
                        pe.wait_ge(diag_ready, h * len(own) + (t * SLOTS + j + 1))
                        pe.wait_ge(v_in[k], h * 16 + (t * PH + 1) * 16)
                        for half in range(2):
                            mm = pe.matmul(ps[:, b + half, :], diag[:, j % 4, :], vrows[:, k, 512 * half:512 * half + 512],
                                           start=False, stop=False, skip_group_check=True)
                        mm.then_inc(v_free[k], 1)
                pe.drain().then_inc(y_acc, 1)


def _chunks(w, np):
    k, n = w.shape
    w = np.pad(w, ((0, 0), (0, -n % 256)))
    return w.reshape(k // P, P, -1, 256).transpose(2, 1, 0, 3).reshape(-1, P, CH)


def kernel(**inputs):
    import numpy as _np
    import concourse.bacc as _bacc
    from concourse import mybir as _mybir
    from concourse.bass_utils import run_bass_kernel_spmd as _run

    g = {k: _np.asarray(v) for k, v in inputs.items()}
    f = _np.float32

    gu = _np.stack([g["w_gate"][0], g["w_up"][0]]).reshape(2, KD, P, NF, P).transpose(3, 2, 1, 0, 4).reshape(NF, P, CH)
    down = g["w_down"][0].reshape(NF // 2, 2, P, D).transpose(0, 2, 1, 3).reshape(NF // 2, P, CH)
    w2 = g["w_in_2"]
    lat = _np.concatenate([w2[:, 0:672], w2[:, 2208:2216]], axis=1)
    w2 = _np.concatenate([_np.pad(lat, ((0, 0), (0, 768 - LAT))), w2[:, 672:2208]], axis=1)
    uq = g["w_uq_2"].reshape(3, P, 768)
    uq01 = _np.pad(_np.concatenate([uq[0], uq[1]], axis=1), ((0, 0), (0, CH - 1536)))
    uq2 = _np.pad(uq[2], ((0, 0), (0, CH - 768)))
    ukv = g["w_ukv_2"].reshape(2, P, D).transpose(1, 0, 2).reshape(P, CH)
    wst = _np.concatenate([_chunks(g["w_in"][0], _np), _chunks(g["w_out"][0], _np), gu, down, _chunks(w2, _np),
                           uq01[None], uq2[None], ukv[None], _chunks(g["w_o_2"], _np), _chunks(g["w_pq_2"], _np)])
    wada = _np.ascontiguousarray(g["w_ada_2"].T).reshape(48, P, D)

    def by_partition(v):
        return v.reshape(-1, P).T

    cols = _np.concatenate([by_partition(g[n]) for n in ("attn_norm_g", "ffn_norm_g", "norm1_g_2", "norm2_g_2",
                                                         "b_ada_2", "mla_qa_g_2", "mla_kva_g_2")], axis=1)
    gains = []
    for n in ("a_q_norm_g", "a_k_norm_g", "b_q_norm_g", "b_k_norm_g"):
        v = g[n][0]
        gains += [v, v.reshape(-1, 2)[:, ::-1].reshape(-1)]
    rowsa = _np.concatenate([*gains, g["b_subln_g"][0], g["b_lambda_q1"][0], g["b_lambda_k1"][0], g["b_lambda_q2"][0],
                             g["b_lambda_k2"][0]])[None]
    rowsb = _np.concatenate([g["c_2"][0], g["mla_q_g_2"], g["mla_k_g_2"], g["fox_q_g_2"], g["fox_k_g_2"],
                             g["b_f_2"]])[None]
    real = _np.arange(T * P)
    inv = (10000.0 ** (-_np.arange(0, HD, 2, dtype=f) / HD)).astype(f)
    inva = (10000.0 ** (-_np.arange(0, HD // 2, 2, dtype=f) / (HD // 2))).astype(f)
    ang_a = _np.zeros((5 * P, HD // 2), f)
    ang_a[:T * P] = _np.concatenate([(real // 64).astype(f)[:, None] * inva, (real % 64).astype(f)[:, None] * inva], 1)
    ang_b = _np.zeros((5 * P, HD // 2), f)
    ang_b[:T * P] = (real + META).astype(f)[:, None] * inv
    ang_b[T * P:T * P + META] = _np.arange(META, dtype=f)[:, None] * inv
    tables = []
    for ang in (ang_a, ang_b):
        c, s = _np.cos(ang), _np.sin(ang)
        tables += [_np.stack([c, c], -1), _np.stack([-s, s], -1)]
    rope = _np.stack(tables).reshape(4, 5, P, HD).transpose(2, 0, 1, 3).reshape(P, 4 * 5 * HD).astype(f)
    const = _np.zeros((P, NCONST), f)
    const[:, K_ID:K_ID + P] = _np.eye(P)
    const[:, K_TRIU:K_TRIU + P] = _np.triu(_np.ones((P, P)))
    const[:, K_MASK:K_MASK + P] = _np.triu(_np.ones((P, P)), 1) * MASK
    const[:, K_ONES:K_ONES + P] = 1.0
    const[:, K_IOTA:K_IOTA + 16] = _np.arange(16)
    const[:, K_FREQ:K_FREQ + 16] = 10000.0 ** (-_np.arange(0, 32, 2, dtype=f) / 32)
    arrays = {
        "wst": wst, "wada": wada, "x_in": g["x"].reshape(T, P, D), "meta_in": g["meta_tokens"], "cols_in": cols,
        "rowsa_in": rowsa, "rowsb_in": rowsb, "rope_in": rope, "const_in": const,
        "pos_in": g["positions_2"].reshape(T, P).T,
        "subk_in": g["sub_keys_2"].reshape(16, NKEYS, P).transpose(2, 0, 1).reshape(P, CH),
        "peer_u": g["peer_u_2"], "peer_v": g["peer_v_2"],
    }
    arrays = {k: _np.ascontiguousarray(v) for k, v in arrays.items()}
    nc = _bacc.Bacc("TRN2", target_bir_lowering=False, num_devices=1)
    args = {n: nc.dram_tensor(n, a.shape, _mybir.dt.from_np(a.dtype), kind="ExternalInput").ap()
            for n, a in arrays.items()}
    out = nc.dram_tensor("out", (T, P, D), F32, kind="ExternalOutput").ap()
    build(nc, out=out, **args)
    r = _run(nc, [arrays], core_ids=[0])
    return r.results[0]["out"].reshape(1, T * P, D)
```

```python
from contextlib import ExitStack

import numpy as np

import concourse.bass as bass
from concourse import mybir

ALU = mybir.AluOpType
ACT = mybir.ActivationFunctionType
F32 = mybir.dt.float32
F32R = mybir.dt.float32r
I32 = mybir.dt.int32
U32 = mybir.dt.uint32
AX = mybir.AxisListType

P = 128
D = 1024
KD = D // P
T = 4
META = 16
KEYS = T * P + META
HALF = KEYS // 2
FF = 2816
NF = FF // P
EPS = 1e-6
HD = 64
SCALE = HD ** -0.5
LAM_INIT = 0.2
MLA_QK = 96
MLA_SCALE = MLA_QK ** -0.5
QR, KVR = 384, 256
LAT = 680
HEADS2 = 16
PH, TOPK, NKEYS = 8, 16, 128
SLOTS = PH * TOPK
ROWS = 8
NHEAD = 4 * PH
LAG = 2
LOW = -3.0e38
MASK = -(2.0 ** 100)

CH = 2048
W_IN, W_OUT = 0, 9
W_GU = W_OUT + 4
W_DOWN = W_GU + NF
W_IN2 = W_DOWN + NF // 2
W_LAT = W_IN2 + 9
W_O2 = W_LAT + 3
W_PQ = W_O2 + 4
NCHUNK = W_PQ + 8
WR = 6

C_G1, C_GF, C_N1, C_N2, C_BADA, C_QA, C_KVA, NCOL = 0, 8, 16, 24, 32, 80, 83, 85
K_ID, K_TRIU, K_MASK, K_ONES, K_IOTA, K_FREQ, NCONST = 0, 128, 256, 384, 512, 528, 544
RA_ROPE, RA_SUB, RA_LAM, NRA = 0, 512, 640, 896
RB_C, RB_MQ, RB_MK, RB_FQ, RB_FK, RB_BF, NRB = 0, 1024, 1120, 1216, 1280, 1344, 1352

TWO_PI = 2.0 * np.pi
PI2_A = 6.28125
PI2_B = float(np.floor((TWO_PI - PI2_A) * 2.0 ** 20) / 2.0 ** 20)
PI2_C = float(TWO_PI - PI2_A - PI2_B)
ROUND = 1.5 * 2.0 ** 23
PI_F = 3.1415925


def build(nc, wst, wada, x_in, meta_in, cols_in, rowsa_in, rowsb_in, rope_in, const_in, pos_in,
          subk_in, peer_u, peer_v, out):
    ctx = ExitStack()
    with ctx:
        def sb(name, shape, dt=F32):
            return ctx.enter_context(nc.sbuf_tensor(name, shape, dt))

        def sem(name):
            return ctx.enter_context(nc.semaphore(name))

        def cut(arena, at, *dims):
            n = int(np.prod(dims))
            v = arena[:, at:at + n]
            if len(dims) == 2:
                return v.rearrange("p (a b) -> p a b", a=dims[0])
            if len(dims) == 3:
                return v.rearrange("p (a b c) -> p a b c", a=dims[0], b=dims[1])
            return v

        def over(ap, n):
            return ap.unsqueeze(len(ap.shape)).broadcast_to([*ap.shape, n])

        def each(ap, n):
            return ap.unsqueeze(1).broadcast_to([ap.shape[0], n, *ap.shape[1:]])

        ps = ctx.enter_context(nc.psum_tensor("ps", [P, 8, 512], F32))

        x = sb("x", [P, T, D])
        big_at = -(-nc.sbuf_base // 32) * 32
        big = sb("big", [P, WR * CH + 4224])
        r2 = sb("r2", [P, 17312])
        r2_at = big_at + 4 * (WR * CH + 4224)
        assert nc.sbuf_base == r2_at + 4 * 17312
        r1 = sb("r1", [P, 11360])
        gates = sb("gates", [P, 2, D])
        const = sb("const", [P, NCONST])
        cols = sb("cols", [P, NCOL])
        rowsa = sb("rowsa", [P, NRA - 512])
        rowsb = sb("rowsb", [P, NRB - D])
        mod = sb("mod", [P, 48])
        gs = sb("gs", [P, 2, KD])
        lnst = sb("lnst", [P, 3, 20])
        neglam = sb("neglam", [P, 4])
        zero = sb("zero", [P, 1])
        eps = sb("eps", [P, 1])
        pos = sb("pos", [P, T], I32)

        ident = const[:, K_ID:K_ID + P]
        triu = const[:, K_TRIU:K_TRIU + P]
        maskt = const[:, K_MASK:K_MASK + P]
        ones = const[:, K_ONES:K_ONES + P]
        iota = const[:, K_IOTA:K_IOTA + 16]
        freq = const[:, K_FREQ:K_FREQ + 16]

        ring = cut(big, 0, WR, CH)
        hT = cut(big, WR * CH, KD, KEYS)
        qz = cut(r1, 0, 16, 512)
        kTa = cut(r1, 8192, 2, KEYS)
        kTb = cut(r1, 8192 + 2 * KEYS, 4, KEYS)
        va = cut(r2, 0, T + 1, 128)
        vb = cut(r2, 640, T + 1, 512)
        rope = cut(r2, 3200, 8, 5, HD)
        sqb = cut(r2, 5760, 2, 256)
        raw = cut(r2, 6272, 3, 256)
        xr = cut(r2, 7040, 256)
        ra = cut(r2, 7296, 256)
        rb = cut(r2, 7552, 256)
        tok = cut(r2, 7808, 3, 256)
        qst = cut(r2, 8576, 4, 3, 4)
        mixed = cut(r2, 8832, T, D)
        xmeta = cut(r2, 8832, D)
        ropec = cut(r2, 9856, 4, 5, HD)
        ropeg = cut(r2, 11136, 8, HD)
        xn = cut(r2, 12928, 2, D)
        prob = cut(r2, 12928, 4, KEYS)
        probT = cut(r2, 15040, 2, 640)
        sqo = cut(r2, 16320, 512)
        sst = sb("sst", [P, 4, 64])
        ost = sb("ost", [P, 3, 16])
        coef = sb("coef", [P, 32])
        aT = cut(r1, 0, NF, 512)
        sg = cut(r2, 7168, 2, 512)
        xn1 = cut(r1, 4096, 2, D)
        adar = cut(r2, 0, 4, D)
        crow = cut(r2, 4096, D)
        ctmp = cut(r2, 5120, D)
        gbc = cut(r2, 6144, KD, P)
        def halves(name, byte, n):
            return nc.alloc_sbuf_tensor_at(name, [P, n], F32R, offset=byte)

        w_hi_f = halves("w_hi", r2_at + 4 * 8192, 2 * CH)
        w_lo_f = halves("w_lo", big_at, WR * CH)
        h_hi_f = halves("h_hi", big_at + 4 * WR * CH, KD * KEYS)
        h_lo_f = halves("h_lo", r2_at + 4 * 13216, KD * 512)
        mid_f = halves("mid", r2_at + 4 * 4096, 2 * CH)
        mid_hi, mid_lo = cut(mid_f, 0, 2, CH), cut(mid_f, 0, KD, 512)
        a_hi_f = halves("a_hi", big_at + 4 * WR * CH, 2 * D)
        a_lo_f = halves("a_lo", big_at + 4 * (WR * CH + 2 * D), 2 * D)
        a_hi, a_lo = cut(a_hi_f, 0, 2, 2, 512), cut(a_lo_f, 0, 2, 2, 512)
        h2_lo_f = halves("h2_lo", r2_at, KD * 512)
        w2_hi_f = halves("w2_hi", big_at + 4 * (WR * CH + 4224 + 17312), 2 * CH)
        h2_lo, w2_hi = cut(h2_lo_f, 0, KD, 512), cut(w2_hi_f, 0, 2, CH)
        o2_hi = cut(h2_lo_f, 0, 2, CH)
        h2_full = cut(r2, 0, KD, 512)
        w_hi, w_lo = cut(w_hi_f, 0, 2, CH), cut(w_lo_f, 0, WR, CH)
        h_hi, h_lo = cut(h_hi_f, 0, KD, KEYS), cut(h_lo_f, 0, KD, 512)
        h_full = cut(r2, 13216, KD, 512)
        kT_mla = cut(r1, 0, 8, 512)
        kT_fox = cut(r1, 4096, 8, 512)
        v_fox = cut(r1, 8192, T, 512)
        qT_mla = cut(r2, 0, 8, 512)
        qT_fox = cut(r2, 4096, 8, 512)
        v_mla = cut(r2, 8192, T, 512)
        lat = cut(r2, 10240, T, LAT)
        qktok = [[cut(r2, at, 8, MLA_QK), cut(r2, at + 768, 8, MLA_QK)] for at in (12960, 14496)]
        ftok = cut(r2, 14496, 4, 4, P)
        lat_junk = cut(r2, 12960, QR)
        fsq = cut(r2, 16544, 256)
        fraw = cut(r2, 16800, 2, 256)
        mixed2 = cut(r2, 10240, T, D)
        latn = cut(big, WR * CH, 640)
        latT = cut(big, WR * CH + 640, 2, 5 * P)
        msq = cut(big, WR * CH + 1920, 2, 8, MLA_QK)
        rp = cut(big, WR * CH + 3456, 4, 8, 16)
        prob2 = cut(big, WR * CH, 4, 512)
        probT2 = cut(big, WR * CH + 2048, 2, 512)
        trig = cut(r1, 10240, 5, T * 16)
        fst = cut(r1, 10560, 3, 16, 4)
        mst = cut(r1, 10752, 3, T, 16)
        logf = cut(r1, 10944, 3, 32)
        fcum = cut(r1, 11040, 2, T, 8)
        lst = cut(r1, 11104, 3, 8)
        sst2 = sst
        qpT = cut(r1, 0, 4, 512)
        subk = cut(r1, 2048, 16, P)
        zmat = cut(r1, 4096, P)
        idx = cut(r1, 4224, T * SLOTS).bitcast(U32)
        topi = cut(r1, 4736, 2, TOPK).bitcast(U32)
        besti = cut(r1, 4768, TOPK).bitcast(U32)
        bits = cut(r1, 4784, 2, TOPK).bitcast(U32)
        sc = cut(r2, 0, T * 2048)
        scf = cut(r2, 0, T, 2048)
        h2 = cut(r2, 8192, T, D)
        xn4 = cut(r2, 14336, 2, D)
        urows = [cut(r1, 4992 + D * i, D) for i in range(6)] + [cut(r2, 12288 + D * i, D) for i in range(2)]
        v_slots = [c % WR for c in range(NCHUNK - WR, NCHUNK - 2)]
        vrows = [cut(big, CH * slot + D * i, D) for slot in v_slots for i in range(CH // D)]
        hsc = cut(r2, 14336, 2, P)
        sc2 = cut(r2, 14592, P)
        cand = cut(r2, 14720, 2, 256)
        topv = cut(r2, 15232, 2, TOPK)
        topf = cut(r2, 15264, 2, TOPK)
        bestv = cut(r2, 15296, TOPK)
        bitf = cut(r2, 15312, 2, TOPK)
        e12 = cut(r2, 15344, 2, TOPK)
        hot = cut(r2, 15376, TOPK, 16)
        dstage = cut(r2, 15632, TOPK)
        gst = cut(r2, 15648, 2, PH)
        gate = cut(r2, 15664, T * SLOTS)
        wts = cut(r2, 16176, T * SLOTS)
        diag = cut(r2, 16688, 4, P)
        expf = cut(r2, 17200, TOPK)
        gtmp = cut(r1, 8192, 2, 256)
        istage = cut(r1, 11136, 4 * TOPK).bitcast(U32)

        x_in_s = [sem(f"x_in{t}") for t in range(5)]
        const_in_s, rope_in_s, rowsb_in_s = sem("const_in_s"), sem("rope_in_s"), sem("rowsb_in_s")
        crow_in_s, subk_in_s = sem("crow_in_s"), sem("subk_in_s")
        w_load = [sem(f"w_load{i}") for i in range(WR)]
        w_used = sem("w_used")
        setup_pool, setup_dve, rope_ready = sem("setup_pool"), sem("setup_dve"), sem("rope_ready")
        ln_rms, ln_xn, ln_tr, ln_hT = sem("ln_rms"), sem("ln_xn"), sem("ln_tr"), sem("ln_hT")
        pj_acc, pj_raw, pj_red, pj_rms, pj_tok, pj_tr, pj_ev = (
            sem(n) for n in ("pj_acc", "pj_raw", "pj_red", "pj_rms", "pj_tok", "pj_tr", "pj_ev"))
        s_ready, max_ready, exp_done, comb_done, pt_ready, pta_done, ptb_done, av_ready, o_done = (
            sem(n) for n in ("s_ready", "max_ready", "exp_done", "comb_done", "pt_ready", "pta_done",
                             "ptb_done", "av_ready", "o_done"))
        once_act, once_dve = sem("once_act"), sem("once_dve")
        LAM_EXP, C_EXP, LOG, SINES = 1, 2, 3, 4
        LAM_SUMS, LOGITS, LOG_GATES, ANGLES, GATE_SUMS = 1, 2, 3, 4, 5
        sub_sq, sub_rms, mix_ready = sem("sub_sq"), sem("sub_rms"), sem("mix_ready")
        mixt_tr, mixt_ev = sem("mixt_tr"), sem("mixt_ev")
        out_acc, out_add = sem("out_acc"), sem("out_add")
        gu_acc, silu_done, act_ready = sem("gu_acc"), sem("silu_done"), sem("act_ready")
        w_hi_done, w_lo_done = sem("w_hi_done"), sem("w_lo_done")
        mixt_lo = sem("mixt_lo")
        a_hi_done, a_lo_done = sem("a_hi_done"), sem("a_lo_done")
        down_acc, down_add = sem("down_acc"), sem("down_add")
        ada_load = [sem(f"ada_load{i}") for i in range(4)]
        ada_used, gbc_ready, gate_acc, gate_ev = (
            sem(n) for n in ("ada_used", "gbc_ready", "gate_acc", "gate_ev"))
        p2_acc, p2_ev = sem("p2_acc"), sem("p2_ev")
        fx_red, fx_rms, fx_tok, fx_tr, fx_ev = (sem(n) for n in ("fx_red", "fx_rms", "fx_tok", "fx_tr", "fx_ev"))
        fc_acc = sem("fc_acc")
        la_rms, la_n, la_tr, la_T, la_acc, la_ev = (
            sem(n) for n in ("la_rms", "la_n", "la_tr", "la_T", "la_acc", "la_ev"))
        mq_red, mq_rms, mq_tok, mq_tr, mq_ev = (sem(n) for n in ("mq_red", "mq_rms", "mq_tok", "mq_tr", "mq_ev"))
        s2_ready, max2, exp2, pt2, pt2_done, av2, o2_done = (
            sem(n) for n in ("s2_ready", "max2", "exp2", "pt2", "pt2_done", "av2", "o2_done"))
        h2_tr, h2_ev, qp_acc, qp_ev, sk_acc, sk_ev = (
            sem(n) for n in ("h2_tr", "h2_ev", "qp_acc", "qp_ev", "sk_acc", "sk_ev"))
        gate_exp, idx_ready, dots_done, gelu_done, w_ready = (
            sem(n) for n in ("gate_exp", "idx_ready", "dots_done", "gelu_done", "w_ready"))
        u_in = [sem(f"u_in{i}") for i in range(ROWS)]
        v_in = [sem(f"v_in{i}") for i in range(ROWS)]
        u_free = [sem(f"u_free{i}") for i in range(ROWS)]
        v_free = [sem(f"v_free{i}") for i in range(ROWS)]
        staged, diag_ready, y_acc, y_ready, y_out, issued = (
            sem(n) for n in ("staged", "diag_ready", "y_acc", "y_ready", "y_out", "issued"))

        pj_jobs = [(n, t) for n in range(9) for t in range(T + (n in (2, 5, 6, 7, 8)))]
        QK = sum(n < 7 for n, _ in pj_jobs)
        ln_base = [0, 5, 9, 13]

        def chunk(eng, c):
            eng.wait_ge(w_load[c % WR], 16 * (c // WR + 1))

        def high_of(c):
            if c < W_GU:
                return (mid_hi if c < W_OUT + 2 else w2_hi)[:, (c - W_OUT) % 2, :]
            if c < W_LAT:
                return (w_hi if c < W_IN2 else w2_hi)[:, (c - W_GU) % 2, :]
            return (w2_hi if c < W_O2 + 2 else o2_hi)[:, (c - W_O2) % 2, :]

        def split_no(c):
            return c - W_OUT + 1 - (W_O2 - W_LAT if c >= W_O2 else 0)

        def passes(w_parts, h_parts):
            (whi, wlo), (hhi, hlo) = w_parts, h_parts
            return ((whi, hhi), (wlo, hhi), (whi, hlo))

        gate_at = (NF - 5, NF - 3)

        def rows_of(t):
            return P if t < T else META

        pv_jobs = []
        for t in range(T):
            for h in range(8):
                pv_jobs.append((t, 16 * t + h, 1, h))
            for h in range(4):
                pv_jobs.append((t, 16 * t + 8 + 2 * h, 2, h))
        pv_of = {s + j: i for i, (t, s, n, h) in enumerate(pv_jobs) for j in range(n)}
        NPV = len(pv_jobs)

        block = ctx.enter_context(nc.Block())

        @block.sync
        def _(sp):
            for t in range(T):
                sp.dma_start(x[:, t, :], x_in[t]).then_inc(x_in_s[t], 16)
            for c in range(WR):
                sp.dma_start(ring[:, c, :], wst[c]).then_inc(w_load[c], 16)
            whole = (NCHUNK - WR) // WR
            with sp.Fori(0, whole) as i:
                for c in range(WR):
                    sp.wait_ge(w_used, i * WR + (c + 1))
                    sp.dma_start(ring[:, c, :], wst[bass.ds(i * WR + (WR + c), 1), :, :].rearrange("a p n -> p (a n)")
                                 ).then_inc(w_load[c], 16)
            for c in range(WR * (whole + 1), NCHUNK):
                sp.wait_ge(w_used, c - WR + 1)
                sp.dma_start(ring[:, c % WR, :], wst[c]).then_inc(w_load[c % WR], 16)
            for t in range(T):
                sp.wait_ge(y_ready, t + 1)
                sp.dma_start(out[t], x[:, t, :]).then_inc(y_out, 16)
            sp.wait_ge(y_out, 16 * T)

        @block.gpsimd
        def _(pool):
            pool.memset(qz, 0.0).then_inc(setup_pool, 1)

            def split(c):
                chunk(pool, c)
                pool.tensor_copy(high_of(c), ring[:, c % WR, :]).then_inc(w_hi_done, 1)
                pool.wait_ge(w_hi_done, split_no(c))
                pool.tensor_tensor(w_lo[:, c % WR, :], ring[:, c % WR, :], high_of(c).bitcast(F32),
                                   ALU.subtract).then_inc(w_lo_done, 1)

            pool.wait_ge(exp_done, 32)
            split(W_OUT)
            split(W_OUT + 1)
            pool.wait_ge(exp_done, 16 * (T - 1) + 8)
            split(W_OUT + 2)
            split(W_OUT + 3)
            pool.wait_ge(mixt_ev, T)
            for m in range(48):
                if m == 4:
                    pool.wait_ge(out_acc, 4 * T)
                    pool.dma_start(crow, rowsb_in[:, RB_C:RB_C + D].broadcast_to([P, D])).then_inc(crow_in_s, 16)
                if m >= 4:
                    pool.wait_ge(ada_used, m - 3)
                pool.dma_start(adar[:, m % 4, :], wada[m]).then_inc(ada_load[m % 4], 16)
            pool.wait_ge(gate_ev, 2)
            pool.wait_ge(ln_tr, 13)
            pool.memset(ftok, 0.0)
            pool.drain()
            pool.memset(ftok[:, 0:2, :, HD:HD + 1], 1.0)
            pool.memset(ftok[:, 2:4, :, HD + 1:HD + 2], 1.0)
            pool.drain().then_inc(setup_pool, 1)
            pool.wait_ge(exp2, HEADS2 * (T - 1) + 8)
            split(W_O2)
            split(W_O2 + 1)
            pool.wait_ge(w_used, W_PQ)
            pool.dma_start(subk, subk_in).then_inc(subk_in_s, 16)

            for free in (*u_free, *v_free):
                pool.sem_inc(free, 1)
            pool.wait_ge(ln_tr, 17)

            def gathers(r, step, kinds, copies):
                stage = {}
                for n, kind in enumerate(kinds):
                    head = step - LAG * kind
                    if kind == 0:
                        pool.wait_ge(idx_ready, r + (head + 1))
                    at = (2 * kind + step % 2) * TOPK
                    stage[kind] = istage[:, at:at + TOPK]
                    pool.tensor_copy(stage[kind], idx[:, bass.ds(r * TOPK + head * TOPK, TOPK)]).then_inc(staged, 1)
                    pool.wait_ge(staged, r * copies[0] + (copies[1] + n + 1))
                pool.sem_inc(issued, 1)
                for k in range(TOPK):
                    for kind in kinds:
                        head = step - LAG * kind
                        rows, free, got = ((urows, u_free, u_in), (vrows, v_free, v_in))[kind]
                        pool.wait_ge(free[k % ROWS], r * 2 + (2 * head + k // ROWS + 1))
                        pool.sem_inc(issued, 1)
                        pool.indirect_dma_start(
                            rows[k % ROWS], None, (peer_u, peer_v)[kind],
                            bass.IndirectOffsetOnAxis(ap=stage[kind][:, k:k + 1], axis=0)
                        ).then_inc(got[k % ROWS], 16)

            for step in range(LAG):
                gathers(0, step, [0], (0, step))
            pool.wait_ge(w_used, NCHUNK - 2)
            with pool.Fori(0, (NHEAD - LAG) // 2) as pair:
                for g in range(2):
                    gathers(pair * 2, LAG + g, [0, 1], (2, LAG + 2 * g))
            for step in range(NHEAD, NHEAD + LAG):
                gathers(0, step, [1], (0, 2 * NHEAD - LAG + step - NHEAD))

        @block.scalar
        def _(act):
            act.dma_start(const[:], const_in).then_inc(const_in_s, 16)
            act.dma_start(cols[:], cols_in).then_inc(const_in_s, 16)
            act.dma_start(xmeta[0:META, :], meta_in).then_inc(x_in_s[4], 16)
            act.dma_start(ropec, rope_in).then_inc(rope_in_s, 16)
            act.dma_start(ropeg, rowsa_in[:, 0:512].broadcast_to([P, 512])).then_inc(rope_in_s, 16)
            act.dma_start(rowsa[:], rowsa_in[:, 512:NRA].broadcast_to([P, NRA - 512])).then_inc(rope_in_s, 16)
            act.dma_start(rowsb[:], rowsb_in[:, D:NRB].broadcast_to([P, NRB - D])).then_inc(rowsb_in_s, 16)
            act.dma_start(pos[:], pos_in).then_inc(rowsb_in_s, 16)

            def norm(layer, tiles, junk):
                for t in tiles:
                    o, n = ln_base[layer] + t, rows_of(t)
                    if layer == 0:
                        act.wait_ge(x_in_s[t], 16)
                        if t == 0:
                            act.wait_ge(setup_dve, 1)
                    elif layer == 2:
                        act.wait_ge(down_add, 2 * (t + 1))
                    else:
                        act.wait_ge(out_add, 16 * (layer // 3) + 4 * (t + 1))
                    if t >= 2:
                        act.wait_ge(ln_tr, o - 1)
                    src = xmeta[0:n, :] if t == T else x[:, t, :]
                    act.activation(junk[0:n, t % 2, :], src, ACT.Square, scale=1 / 32, bias=zero[0:n, :],
                                   accum_out=lnst[0:n, 0, o:o + 1])
                    act.drain()
                    act.activation(lnst[0:n, 1, o:o + 1], lnst[0:n, 0, o:o + 1], ACT.Sqrt,
                                   bias=eps[0:n, :]).then_inc(ln_rms, 1)

            norm(0, range(T + 1), xn)

            def pj_sqrt(j):
                n, t = pj_jobs[j]
                r = rows_of(t)
                act.wait_ge(pj_red, j + 1)
                act.activation(qst[0:r, j % 4, 1, :], qst[0:r, j % 4, 0, :], ACT.Sqrt,
                               bias=eps[0:r, :]).then_inc(pj_rms, 1)

            def pj_evac(j):
                n, t = pj_jobs[j]
                r, s = rows_of(t), t * P
                act.wait_ge(pj_tr, j + 1)
                if j == 0:
                    act.wait_ge(setup_pool, 1)
                b = ps[:, j % 4, 0:256].rearrange("p (c n) -> p c n", c=2)
                if n in (0, 1, 3, 4):
                    h = 4 * n if n < 2 else 8 + 4 * (n - 3)
                    act.activation(qz[0:64, h:h + 4:2, s:s + P], b[0:64], ACT.Copy)
                    act.activation(qz[64:P, h + 1:h + 4:2, s:s + P], b[64:P], ACT.Copy).then_inc(pj_ev, 1)
                elif n == 2:
                    act.activation(kTa[:, :, s:s + r], b[:, :, 0:r], ACT.Copy).then_inc(pj_ev, 1)
                else:
                    act.activation(kTb[:, 2 * (n - 5):2 * (n - 5) + 2, s:s + r], b[:, :, 0:r],
                                   ACT.Copy).then_inc(pj_ev, 1)

            for j, (n, t) in enumerate(pj_jobs):
                r = rows_of(t)
                act.wait_ge(pj_acc, j + 1)
                b = ps[0:r, 4 + j % 4, 0:256]
                if n < 7:
                    w = P if n == 2 else 256
                    if j >= 2:
                        act.wait_ge(pj_red, j - 1)
                    if j >= 3:
                        act.wait_ge(pj_tok, j - 2)
                    act.activation(sqb[0:r, j % 2, 0:w], b[:, 0:w], ACT.Square, scale=1 / 8, bias=zero[0:r, :])
                    if n == 2:
                        act.activation(va[0:r, t, :], b[:, P:256], ACT.Copy)
                    act.activation(raw[0:r, j % 3, 0:w], b[:, 0:w], ACT.Copy)
                else:
                    act.activation(vb[0:r, t, (n - 7) * 256:(n - 6) * 256], b, ACT.Copy)
                act.drain().then_inc(pj_raw, 1)
                if 1 <= j <= QK:
                    pj_sqrt(j - 1)
                if 3 <= j < QK + 3:
                    pj_evac(j - 3)

            act.wait_ge(once_dve, LAM_SUMS)
            act.activation(neglam[:, 2:4], neglam[:, 0:2], ACT.Exp, bias=zero[:]).then_inc(once_act, 1)

            def high_part(c):
                chunk(act, c)
                if W_GU + 2 <= c < W_LAT:
                    act.wait_ge(w_used, c - 1 if c < W_IN2 else max(c - 1, W_IN2))
                act.activation(high_of(c), ring[:, c % WR, :], ACT.Copy).then_inc(w_hi_done, 1)

            def softmax(s):
                act.wait_ge(max_ready, s + 1)
                if s >= 4:
                    act.wait_ge(pt_ready, pv_of[s - 4] + 1)
                act.activation(prob[:, s % 4, :].rearrange("p (a b) -> p a b", a=2),
                               ps[:, 2 * (s % 2):2 * (s % 2) + 2, 0:HALF], ACT.Exp, scale=SCALE,
                               bias=sst[:, 1, s:s + 1], accum_out=sst[:, 2, s:s + 1])
                act.drain().then_inc(exp_done, 1)

            def prob_evac(p):
                act.wait_ge(pt_ready, p + 1)
                if p >= 2:
                    act.wait_ge(av_ready, p - 1)
                act.activation(probT[:, p % 2, 0:512], ps[:, 4 + p % 2, :], ACT.Copy).then_inc(pta_done, 1)

            for i in range(NPV + 1):
                if i < NPV:
                    _, s, n, _ = pv_jobs[i]
                    for j in range(n):
                        softmax(s + j)
                if i >= 1:
                    prob_evac(i - 1)

            for t in range(T):
                act.wait_ge(sub_sq, t + 1)
                act.activation(ost[:, 1, 4 * t:4 * t + 4], ost[:, 0, 4 * t:4 * t + 4], ACT.Sqrt,
                               bias=eps[:], scale=1 / 128).then_inc(sub_rms, 1)
            def mix_and_norm(first, layer, junk):
                for t in range(T + 1):
                    if t < T:
                        act.wait_ge(mixt_tr, first + t + 1)
                        act.activation(h_hi[:, :, t * P:(t + 1) * P],
                                       ps[:, 0:2, :].rearrange("p a (b n) -> p (a b) n", n=P),
                                       ACT.Copy).then_inc(mixt_ev, 1)
                    if t == 0 and first:
                        act.wait_ge(w_lo_done, split_no(W_O2 + 1))
                        high_part(W_O2 + 2)
                        high_part(W_O2 + 3)
                    if t:
                        norm(layer, [t - 1], junk)

            mix_and_norm(0, 1, xn1)

            def high_act(g):
                if g >= 2:
                    act.wait_ge(w_used, W_DOWN + g - 1)
                act.activation(a_hi[:, g % 2], aT[:, 2 * g:2 * g + 2, :], ACT.Copy).then_inc(a_hi_done, 1)

            high_part(W_GU)
            high_part(W_GU + 1)

            act.wait_ge(crow_in_s, 16)
            act.activation(ctmp, crow, ACT.Exp, scale=-1.0, bias=zero[:]).then_inc(once_act, 1)

            for f in range(NF):
                act.wait_ge(gu_acc, f + 1)
                if f >= 2:
                    act.wait_ge(act_ready, f - 1)
                act.activation(sg[:, f % 2, :], ps[:, 2 * (f % 2), :], ACT.Silu, bias=zero[:]).then_inc(silu_done, 1)
                if f == NF - 1:
                    high_act(0)
                high_part(W_GU + f + 2)
                for g in range(2):
                    if f == gate_at[g] + 1:
                        act.wait_ge(gate_acc, g + 1)
                        act.activation(gates[:, g, :].rearrange("p (a b) -> p a b", a=2),
                                       ps[:, 4 + 2 * g:6 + 2 * g, :], ACT.Copy).then_inc(gate_ev, 1)
            high_act(1)
            for g in range(2, NF // 2):
                high_part(W_DOWN + g)
                high_act(g)

            norm(2, range(2), xn)
            high_part(W_IN2)
            norm(2, range(2, T), xn)
            high_part(W_IN2 + 1)

            def fx_sqrt(k):
                act.wait_ge(fx_red, k + 1)
                act.activation(fst[:, 1, k, :], fst[:, 0, k, :], ACT.Sqrt, bias=eps[:]).then_inc(fx_rms, 1)

            def fx_evac(k):
                n, t = 3 + k // T, k % T
                dst = qT_fox if n < 5 else kT_fox
                h = 4 * ((n - 3) % 2)
                act.wait_ge(fx_tr, k + 1)
                act.activation(dst[:, h:h + 4, t * P:(t + 1) * P],
                               ps[:, k % 4, :].rearrange("p (a n) -> p a n", a=4), ACT.Copy).then_inc(fx_ev, 1)

            def latent_squares(t):
                for i, (at, n) in enumerate(((0, QR), (QR, KVR))):
                    act.drain()
                    act.activation(lat_junk[:, 0:n], lat[:, t, at:at + n], ACT.Square, scale=n ** -0.5, bias=zero[:],
                                   accum_out=lst[:, 0, 2 * t + i:2 * t + i + 1])
                if t == T - 1:
                    act.drain()
                    act.activation(lst[:, 1, :], lst[:, 0, :], ACT.Sqrt, bias=eps[:]).then_inc(la_rms, 1)

            for j in range(9 * T):
                n, t = j // T, j % T
                k = j - 3 * T
                act.wait_ge(p2_acc, j + 1)
                if t == 0 and 1 <= n < 8:
                    high_part(W_IN2 + n + 1)
                b = ps[:, 4 + j % 4, 0:256]
                if n < 3:
                    first = 256 * ((n + 2) % 3)
                    w = min(256, LAT - first)
                    act.activation(lat[:, t, first:first + w], b[:, 0:w], ACT.Copy)
                elif n < 7:
                    if k >= 1:
                        act.wait_ge(fx_red, k)
                    if k >= 2:
                        act.wait_ge(fx_tok, k - 1)
                    act.activation(fsq, b, ACT.Square, scale=1 / 8, bias=zero[:])
                    act.activation(fraw[:, k % 2, :], b, ACT.Copy)
                else:
                    act.activation(v_fox[:, t, 256 * (n - 7):256 * (n - 6)], b, ACT.Copy)
                act.drain().then_inc(p2_ev, 1)
                if n == 1 and t == T - 1:
                    act.wait_ge(once_dve, ANGLES)
                    act.activation(trig[:, 0:2, :], trig[:, 2:4, :], ACT.Sin, bias=zero[:]).then_inc(once_act, 1)
                if n == 0 and t == T - 1:
                    act.wait_ge(once_dve, LOGITS)
                    act.activation(logf[:, 1, :], logf[:, 1, :], ACT.Exp, bias=zero[:])
                    act.drain()
                    act.activation(logf[:, 1, :], logf[:, 1, :], ACT.Ln, bias=ones[:, 0:1]).then_inc(once_act, 1)
                if 16 <= k < 20:
                    latent_squares(k - 16)
                if 1 <= k <= 16:
                    fx_sqrt(k - 1)
                if 3 <= k < 19:
                    fx_evac(k - 3)

            def latent_evac(t):
                for g in range(4):
                    dst = qT_mla if g < 2 else kT_mla
                    act.wait_ge(mq_tr, 4 * t + g + 1)
                    act.activation(dst[0:MLA_QK, 4 * (g % 2):4 * (g % 2) + 4, t * P:(t + 1) * P],
                                   ps[0:MLA_QK, 6 + g % 2, :].rearrange("p (a n) -> p a n", a=4),
                                   ACT.Copy).then_inc(mq_ev, 1)

            for t in range(T):
                qtok, ktok = qktok[t % 2]
                act.wait_ge(la_acc, t + 1)
                if t == 0:
                    act.wait_ge(p2_acc, 9 * T)
                if t >= 2:
                    act.wait_ge(mq_tr, 4 * (t - 1))
                if t >= 1:
                    act.wait_ge(mq_red, t)
                if t == 0:
                    act.wait_ge(fx_tr, 16)
                act.activation(qtok, ps[:, 2:4, 0:384].rearrange("p a (b n) -> p a b n", n=MLA_QK), ACT.Copy)
                kv = ps[:, 4:6, :].rearrange("p a (b n) -> p (a b) n", n=P)
                act.activation(ktok[:, :, 0:64], kv[:, :, 0:64], ACT.Copy)
                act.activation(v_mla[:, t, :].rearrange("p (h n) -> p h n", h=8), kv[:, :, 64:P], ACT.Copy)
                act.activation(ktok[:, :, 64:96], each(lat[:, t, 640:672], 8), ACT.Copy)
                act.drain()
                act.activation(msq[:, 0], qtok, ACT.Square, bias=zero[:])
                act.activation(msq[:, 1], ktok, ACT.Square, bias=zero[:])
                act.drain().then_inc(la_ev, 1)
                if t:
                    latent_evac(t - 1)
                act.wait_ge(mq_red, t + 1)
                act.activation(mst[:, 1, t, :], mst[:, 0, t, :], ACT.Sqrt, bias=eps[:],
                               scale=1 / MLA_QK).then_inc(mq_rms, 1)
            latent_evac(T - 1)

            for i in range(T * HEADS2 + 1):
                if i < T * HEADS2:
                    t, h = i // HEADS2, i % HEADS2
                    act.wait_ge(max2, i + 1)
                    if i >= 4:
                        act.wait_ge(pt2, i - 3)
                    act.activation(prob2[:, i % 4, 0:(t + 1) * P], ps[:, i % 2, 0:(t + 1) * P], ACT.Exp,
                                   scale=MLA_SCALE if h < 8 else SCALE, bias=sst2[:, 1, i:i + 1],
                                   accum_out=sst2[:, 2, i:i + 1])
                    act.drain().then_inc(exp2, 1)
                if i >= 1:
                    u = i - 1
                    act.wait_ge(pt2, u + 1)
                    if u >= 2:
                        act.wait_ge(av2, u - 1)
                    n = (u // HEADS2 + 1) * P
                    act.activation(probT2[:, u % 2, 0:n], ps[:, 2 + u % 2, 0:n], ACT.Copy).then_inc(pt2_done, 1)

            mix_and_norm(T, 3, xn4)

            for t in range(T):
                act.wait_ge(h2_tr, t + 1)
                act.activation(h2[:, t, :].rearrange("p (a b) -> p a b", a=2),
                               ps[:, 4 + 2 * (t % 2):6 + 2 * (t % 2), :], ACT.Copy).then_inc(h2_ev, 1)
            first_heads = (10, 14)

            def head_gates(r, head):
                act.wait_ge(idx_ready, r + (head + 1))
                g = gate[:, bass.ds(r * TOPK + head * TOPK, TOPK)]
                act.activation(g, g, ACT.Exp, bias=zero[:]).then_inc(gate_exp, 1)

            def head_gelu(r, head):
                act.wait_ge(dots_done, r + (head + 1))
                d = wts[:, bass.ds(r * TOPK + head * TOPK, TOPK)]
                act.activation(d, d, ACT.Gelu_apprx_tanh, bias=zero[:]).then_inc(gelu_done, 1)

            for c in range(17):
                if c in first_heads:
                    head_gates(0, first_heads.index(c))
                    head_gelu(0, first_heads.index(c))
                if c < 16:
                    act.wait_ge(qp_acc, c + 1)
                    if c >= 4:
                        act.wait_ge(sk_acc, c - 3)
                    act.activation(qpT[:, c % 4, :], ps[:, c % 4, :], ACT.Copy).then_inc(qp_ev, 1)
                if c >= 1:
                    act.wait_ge(sk_acc, c)
                    act.activation(scf[:, :, (c - 1) * P:c * P],
                                   ps[:, 4 + (c - 1) % 4, :].rearrange("p (t n) -> p t n", t=T),
                                   ACT.Copy).then_inc(sk_ev, 1)
            def diagonals(r, head):
                act.wait_ge(w_ready, r + (head + 1))
                for k in range(TOPK):
                    before = 2 * head + 2 + (k - 4) // ROWS
                    act.wait_ge(v_free[(k - 4) % ROWS], r * 2 + before)
                    act.activation(diag[:, k % 4, :], ident, ACT.Copy,
                                   scale=wts[:, bass.ds(r * TOPK + (head * TOPK + k), 1)]).then_inc(diag_ready, 1)

            with act.Fori(0, NHEAD - LAG) as r:
                head_gates(r, LAG)
                diagonals(r, 0)
                head_gelu(r, LAG)
            for head in range(NHEAD - LAG, NHEAD):
                diagonals(0, head)

        @block.vector
        def _(v):
            v.memset(zero[:], 0.0)
            v.memset(eps[:], EPS)
            v.drain().then_inc(setup_dve, 1)

            def norm(layer, tiles, buf):
                tiles = list(tiles)

                def scaled(t):
                    o, n = ln_base[layer] + t, rows_of(t)
                    v.wait_ge(ln_rms, o + 1)
                    v.reciprocal(lnst[0:n, 2, o:o + 1], lnst[0:n, 1, o:o + 1])
                    v.drain()
                    src = xmeta[0:n, :] if t == T else x[:, t, :]
                    v.tensor_scalar(buf[0:n, t % 2, :], src, lnst[0:n, 2, o:o + 1], None, ALU.mult).then_inc(ln_xn, 1)

                def evac(t):
                    o, n = ln_base[layer] + t, rows_of(t)
                    v.wait_ge(ln_tr, o + 1)
                    b = 2 if layer in (1, 3) else 2 * (t % 2)
                    src = ps[:, b:b + 2, :].rearrange("p a (b n) -> p (a b) n", n=P)[:, :, 0:n]
                    dst = hT[:, :, t * P:t * P + n]
                    g = [cols[:, C_G1:C_G1 + KD], cols[:, C_GF:C_GF + KD], gs[:, 0, :], gs[:, 1, :]][layer]
                    if layer == 0:
                        v.tensor_tensor(dst, src, over(g, n), ALU.mult).then_inc(ln_hT, 1)
                        return
                    if layer == 3:
                        shift = mod[:, 24:24 + KD]
                        v.tensor_tensor(dst, src, over(g, n), ALU.mult)
                        v.drain()
                        v.tensor_tensor(dst, dst, over(shift, n), ALU.add).then_inc(ln_hT, 1)
                        return
                    at = slice(t * P, t * P + n)
                    full, high, low = (h_full if layer == 1 else h2_full)[:, :, at], h_hi[:, :, at], (h_lo if layer == 1 else h2_lo)[:, :, at]
                    v.tensor_tensor(full, src, over(g, n), ALU.mult)
                    v.drain()
                    if layer == 2:
                        v.tensor_tensor(full, full, over(mod[:, 0:KD], n), ALU.add)
                        v.drain()
                    v.tensor_copy(high, full)
                    v.drain()
                    v.tensor_tensor(low, full, high.bitcast(F32), ALU.subtract).then_inc(ln_hT, 1)

                return scaled, evac

            def norm_all(layer, tiles, buf):
                scaled, evac = norm(layer, tiles, buf)
                for t in tiles:
                    scaled(t)
                    if t:
                        evac(t - 1)
                evac(tiles[-1])

            v.wait_ge(const_in_s, 32)
            norm_all(0, range(T + 1), xn)
            v.wait_ge(rope_in_s, 48)
            for kind in range(4):
                for sw in range(2):
                    v.tensor_tensor(rope[:, 2 * kind + sw], ropec[:, 2 * (kind // 2) + sw],
                                    each(ropeg[:, 2 * kind + sw, :], 5), ALU.mult)
            v.drain()

            def pj_reduce(j):
                n, t = pj_jobs[j]
                r, hh = rows_of(t), 2 if n == 2 else 4
                v.wait_ge(pj_raw, j + 1)
                v.tensor_reduce(qst[0:r, j % 4, 0, 0:hh],
                                sqb[0:r, j % 2, 0:64 * hh].rearrange("p (h d) -> p h d", h=hh), AX.X, ALU.add)
                if hh == 2:
                    v.memset(qst[0:r, j % 4, 0, 2:4], 1.0)
                v.drain().then_inc(pj_red, 1)

            def pj_rope(j):
                n, t = pj_jobs[j]
                r, hh = rows_of(t), 2 if n == 2 else 4
                kind = (0, 0, 1, 2, 2, 3, 3)[n]
                w = 64 * hh
                v.wait_ge(pj_rms, j + 1)
                v.reciprocal(qst[0:r, j % 4, 2, 0:hh], qst[0:r, j % 4, 1, 0:hh])
                v.drain()
                src = raw[0:r, j % 3, 0:w].rearrange("p (h d) -> p h d", h=hh)
                a = xr[0:r, 0:w].rearrange("p (h d) -> p h d", h=hh)
                v.tensor_tensor(a, src, over(qst[0:r, j % 4, 2, 0:hh], HD), ALU.mult)
                v.drain()
                straight = ra[0:r, 0:w].rearrange("p (h d) -> p h d", h=hh)
                swapped = rb[0:r, 0:w].rearrange("p (h i two) -> p h i two", h=hh, two=2)
                a2 = xr[0:r, 0:w].rearrange("p (h i two) -> p h i two", h=hh, two=2)
                tb = rope[0:r, 2 * kind + 1, t, :].rearrange("p (i two) -> p i two", two=2)
                v.tensor_tensor(straight, a, each(rope[0:r, 2 * kind, t, :], hh), ALU.mult)
                v.tensor_tensor(swapped[:, :, :, 0], a2[:, :, :, 1], each(tb[:, :, 0], hh), ALU.mult)
                v.tensor_tensor(swapped[:, :, :, 1], a2[:, :, :, 0], each(tb[:, :, 1], hh), ALU.mult)
                v.drain()
                if j >= 3:
                    v.wait_ge(pj_tr, j - 2)
                if n == 2:
                    dst = tok[0:r, j % 3, :].rearrange("p (h two d) -> p h two d", h=2, two=2)
                    rb3 = rb[0:r, 0:w].rearrange("p (h d) -> p h d", h=hh)
                    v.tensor_tensor(dst[:, :, 0, :], straight, rb3, ALU.add)
                    v.tensor_tensor(dst[:, :, 1, :], straight, rb3, ALU.add)
                    v.drain().then_inc(pj_tok, 1)
                else:
                    v.tensor_tensor(tok[0:r, j % 3, :], ra[0:r, :], rb[0:r, :], ALU.add).then_inc(pj_tok, 1)
                    v.drain()

            for j in range(QK + 1):
                if j < QK:
                    pj_reduce(j)
                if j >= 1:
                    pj_rope(j - 1)

            lq = rowsa[:, RA_LAM - 512:RA_LAM - 256].rearrange("p (a d) -> p a d", a=4)
            v.tensor_tensor(xr[:, 0:64], lq[:, 0, :], lq[:, 1, :], ALU.mult)
            v.tensor_tensor(xr[:, 64:128], lq[:, 2, :], lq[:, 3, :], ALU.mult)
            v.drain()
            v.tensor_reduce(neglam[:, 0:2], xr[:, 0:128].rearrange("p (a d) -> p a d", a=2), AX.X,
                            ALU.add).then_inc(once_dve, 1)
            v.wait_ge(once_act, LAM_EXP)
            v.tensor_tensor(neglam[:, 0:1], neglam[:, 3:4], neglam[:, 2:3], ALU.subtract)
            v.drain()
            v.tensor_scalar(neglam[:, 1:2], neglam[:, 0:1], LAM_INIT, None, ALU.subtract)
            v.drain()

            def low_part(c):
                v.wait_ge(w_hi_done, split_no(c))
                v.tensor_tensor(w_lo[:, c % WR, :], ring[:, c % WR, :], high_of(c).bitcast(F32),
                                ALU.subtract).then_inc(w_lo_done, 1)

            def mixed_low(first, t, low):
                v.wait_ge(mixt_ev, first + t + 1)
                at = slice(t * P, (t + 1) * P)
                v.tensor_tensor(low[:, :, at], ps[:, 0:2, :].rearrange("p a (b n) -> p (a b) n", n=P),
                                h_hi[:, :, at].bitcast(F32), ALU.subtract).then_inc(mixt_lo, 1)

            def score_max(s):
                v.wait_ge(s_ready, s + 1)
                v.tensor_reduce(sst[:, 0, s:s + 1], ps[:, 2 * (s % 2):2 * (s % 2) + 2, 0:HALF], AX.XY, ALU.max)
                v.drain()
                v.tensor_scalar(sst[:, 1, s:s + 1], sst[:, 0, s:s + 1], -SCALE, None, ALU.mult).then_inc(max_ready, 1)

            def finish_probs(i):
                t, s, n, h = pv_jobs[i]
                v.wait_ge(exp_done, s + n)
                v.reciprocal(sst[:, 3, s:s + n], sst[:, 2, s:s + n])
                v.drain()
                if n == 2:
                    c = 4 * t + h
                    v.tensor_scalar(coef[:, c:c + 1], sst[:, 2, s:s + 1], sst[:, 3, s + 1:s + 2], neglam[:, 1:2],
                                    ALU.mult, ALU.mult)
                    v.drain()
                    v.scalar_tensor_tensor(out=prob[:, s % 4, :], in0=prob[:, (s + 1) % 4, :], scalar=coef[:, c:c + 1],
                                           in1=prob[:, s % 4, :], op0=ALU.mult, op1=ALU.add)
                    v.drain().then_inc(comb_done, 1)

            def meta_probs(i):
                v.wait_ge(pt_ready, i + 1)
                if i >= 2:
                    v.wait_ge(av_ready, i - 1)
                v.tensor_copy(probT[0:META, i % 2, 512:640], ps[0:META, 6 + i % 2, 0:P]).then_inc(ptb_done, 1)

            def head_out(i):
                t, s, n, h = pv_jobs[i]
                v.wait_ge(av_ready, i + 1)
                o = P
                if n == 1:
                    o += 64 * (h // 4)
                    v.tensor_scalar(mixed[:, t, 64 * h:64 * h + 64], ps[:, 6 + i % 2, o:o + 64], sst[:, 3, s:s + 1], None,
                                    ALU.mult).then_inc(o_done, 1)
                else:
                    at = 512 + P * h
                    v.tensor_scalar(mixed[:, t, at:at + P], ps[:, 6 + i % 2, o:o + P], sst[:, 3, s:s + 1], None,
                                    ALU.mult).then_inc(o_done, 1)

            for i in range(NPV + 2):
                if i < NPV:
                    _, s, n, _ = pv_jobs[i]
                    for j in range(n):
                        score_max(s + j)
                if i < NPV:
                    finish_probs(i)
                if 1 <= i <= NPV:
                    meta_probs(i - 1)
                if i >= 2:
                    head_out(i - 2)

            for t in range(T):
                o = mixed[:, t, 512:D]
                v.drain()
                v.tensor_tensor(sqo, o, o, ALU.mult)
                v.drain()
                v.tensor_reduce(ost[:, 0, 4 * t:4 * t + 4], sqo.rearrange("p (h d) -> p h d", h=4), AX.X,
                                ALU.add).then_inc(sub_sq, 1)
            for t in range(T):
                o = mixed[:, t, 512:D].rearrange("p (h d) -> p h d", h=4)
                if t == 2:
                    mixed_low(0, 0, h_lo)
                v.wait_ge(sub_rms, t + 1)
                v.reciprocal(ost[:, 2, 4 * t:4 * t + 4], ost[:, 1, 4 * t:4 * t + 4])
                v.drain()
                v.tensor_tensor(o, o, over(ost[:, 2, 4 * t:4 * t + 4], P), ALU.mult)
                v.drain()
                v.scalar_tensor_tensor(out=o, in0=o, scalar=1.0 - LAM_INIT,
                                       in1=each(rowsa[:, 0:P], 4), op0=ALU.mult, op1=ALU.mult).then_inc(mix_ready, 1)

            def low_act(g):
                v.wait_ge(a_hi_done, g + 1)
                v.tensor_tensor(a_lo[:, g % 2], aT[:, 2 * g:2 * g + 2, :], a_hi[:, g % 2].bitcast(F32),
                                ALU.subtract).then_inc(a_lo_done, 1)

            scaled, evac = norm(1, range(T), xn1)
            for t in range(T):
                if t + 1 < T:
                    mixed_low(0, t + 1, h_lo)
                for n in range(4):
                    v.wait_ge(out_acc, 4 * t + n + 1)
                    xs = x[:, t, 256 * n:256 * n + 256]
                    v.tensor_tensor(xs, xs, ps[:, 4 + n, 0:256], ALU.add).then_inc(out_add, 1)
                scaled(t)
                if t:
                    evac(t - 1)
            low_part(W_GU)
            evac(T - 1)
            low_part(W_GU + 1)

            v.wait_ge(once_act, C_EXP)
            v.tensor_scalar(ctmp, ctmp, 1.0, None, ALU.add)
            v.drain()
            v.reciprocal(ctmp, ctmp)
            v.drain()
            v.tensor_tensor(crow, crow, ctmp, ALU.mult)
            v.drain()

            def modulation(m):
                v.wait_ge(ada_load[m % 4], 16 * (m // 4 + 1))
                v.tensor_tensor_reduce(out=adar[:, m % 4, :], in0=adar[:, m % 4, :], in1=crow, scale=1.0, scalar=0.0,
                                       op0=ALU.mult, op1=ALU.add, accum_out=mod[:, m:m + 1])
                v.drain().then_inc(ada_used, 1)

            for f in range(NF):
                v.wait_ge(silu_done, f + 1)
                v.tensor_tensor(aT[:, f, :], sg[:, f % 2, :], ps[:, 2 * (f % 2) + 1, :], ALU.mult).then_inc(act_ready, 1)
                if f == NF - 1:
                    low_act(0)
                low_part(W_GU + f + 2)
                for m in range(3 * f, min(3 * f + 3, 48)):
                    modulation(m)
                if f == 16:
                    v.tensor_tensor(mod[:], mod[:], cols[:, C_BADA:C_BADA + 48], ALU.add)
                    v.drain()
                for g in range(2):
                    if f == gate_at[g] - 1:
                        scale = mod[:, 24 * g + KD:24 * g + 2 * KD]
                        gain = cols[:, C_N1 + KD * g:C_N1 + KD * g + KD]
                        v.scalar_tensor_tensor(out=gs[:, g, :], in0=scale, scalar=1.0, in1=gain, op0=ALU.add, op1=ALU.mult)
                        if g:
                            v.wait_ge(gate_acc, 1)
                        v.tensor_copy(gbc, over(mod[:, 24 * g + 16:24 * g + 24], P)).then_inc(gbc_ready, 1)
            low_act(1)

            for g in range(2, NF // 2):
                low_part(W_DOWN + g)
                low_act(g)

            for t in range(T):
                for half in range(2):
                    v.wait_ge(down_acc, 2 * t + half + 1)
                    xs = x[:, t, 512 * half:512 * half + 512]
                    v.tensor_tensor(xs, xs, ps[:, 2 * t + half, :], ALU.add).then_inc(down_add, 1)

            scaled, evac = norm(2, range(T), xn)
            scaled(0)
            scaled(1)
            evac(0)
            low_part(W_IN2)
            for t in range(2, T):
                scaled(t)
                evac(t - 1)
            evac(T - 1)
            low_part(W_IN2 + 1)

            v.wait_ge(rowsb_in_s, 32)
            v.wait_ge(p2_ev, T)
            y = logf[:, 0, :]
            v.tensor_tensor(y.rearrange("p (t h) -> p t h", t=T), lat[:, :, 672:680],
                            each(rowsb[:, RB_BF - D:RB_BF - D + 8], T), ALU.add)
            v.drain()
            v.scalar_tensor_tensor(out=logf[:, 1, :], in0=y, scalar=-1.0, in1=y, op0=ALU.mult, op1=ALU.min).then_inc(once_dve, 1)
            v.wait_ge(once_act, LOG)
            v.tensor_scalar(logf[:, 2, :], y, 0.0, None, ALU.min)
            v.drain()
            v.tensor_tensor(logf[:, 2, :], logf[:, 2, :], logf[:, 1, :], ALU.subtract).then_inc(once_dve, 1)
            low_part(W_IN2 + 2)

            posf = fst[:, 0, 0, :]
            v.tensor_copy(posf, pos[:])
            v.drain()
            ang, turn = trig[:, 4, :], trig[:, 0, :]
            v.tensor_tensor(ang.rearrange("p (t f) -> p t f", t=T), over(posf, 16), each(freq, T), ALU.mult)
            v.drain()
            for q, quarter in ((2, 0.25), (3, 0.0)):
                red = trig[:, q, :]
                v.tensor_scalar(turn, ang, 1.0 / TWO_PI, quarter, ALU.mult, ALU.add)
                v.drain()
                v.tensor_scalar(turn, turn, ROUND, None, ALU.add)
                v.drain()
                v.tensor_scalar(turn, turn, ROUND, None, ALU.subtract)
                v.drain()
                src = ang
                for part in (PI2_A, PI2_B, PI2_C):
                    v.scalar_tensor_tensor(out=red, in0=turn, scalar=-part, in1=src, op0=ALU.mult, op1=ALU.add)
                    v.drain()
                    src = red
                if quarter:
                    v.tensor_scalar(red, red, float(np.pi / 2), None, ALU.add)
                    v.drain()
                v.tensor_scalar(red, red, PI_F, -PI_F, ALU.min, ALU.max)
                v.drain()
            v.drain().then_inc(once_dve, 1)

            low_part(W_IN2 + 3)
            v.wait_ge(fc_acc, 1)
            f8 = ps[:, 3, 0:32].rearrange("p (t h) -> p t h", t=T)
            v.tensor_scalar(fcum[:, 0], f8, 8.0, None, ALU.mult)
            v.tensor_scalar(fcum[:, 1], f8, -8.0, None, ALU.mult)
            v.drain().then_inc(once_dve, 1)

            v.wait_ge(setup_pool, 2)
            for k in range(17):
                if k < 16:
                    v.wait_ge(p2_ev, 3 * T + k + 1)
                    v.tensor_reduce(fst[:, 0, k, :], fsq.rearrange("p (h d) -> p h d", h=4), AX.X, ALU.add).then_inc(fx_red, 1)
                    if k % 4 == 0:
                        low_part(W_IN2 + k // 4 + 4)
                if k == 16:
                    low_part(W_IN2 + 8)
                if k >= 1:
                    q = k - 1
                    n, t = 3 + q // T, q % T
                    isk = n >= 5
                    g = rowsb[:, (RB_FK if isk else RB_FQ) - D:][:, 0:64]
                    v.wait_ge(fx_rms, q + 1)
                    v.reciprocal(fst[:, 2, q, :], fst[:, 1, q, :])
                    v.drain()
                    src = fraw[:, q % 2, :].rearrange("p (h d) -> p h d", h=4)
                    v.tensor_tensor(src, src, over(fst[:, 2, q, :], HD), ALU.mult)
                    if q >= 2:
                        v.wait_ge(fx_tr, q - 1)
                    else:
                        v.drain()
                    buf = ftok[:, 2 * isk + q % 2]
                    v.drain()
                    v.tensor_tensor(buf[:, :, 0:64], src, each(g, 4), ALU.mult)
                    at = HD if isk else HD + 1
                    h = 4 * ((n - 3) % 2)
                    v.tensor_copy(buf[:, :, at], fcum[:, 1 if isk else 0, t, h:h + 4])
                    v.drain().then_inc(fx_tok, 1)

            v.wait_ge(p2_acc, 9 * T)
            v.wait_ge(la_rms, 1)
            v.reciprocal(lst[:, 2, :], lst[:, 1, :])
            v.drain()
            v.wait_ge(once_act, SINES)
            def latent_in(t):
                if t:
                    v.wait_ge(la_tr, t)
                v.tensor_scalar(latn[:, 0:QR], lat[:, t, 0:QR], lst[:, 2, 2 * t:2 * t + 1], None, ALU.mult)
                v.tensor_scalar(latn[:, QR:640], lat[:, t, QR:640], lst[:, 2, 2 * t + 1:2 * t + 2], None, ALU.mult)
                v.drain().then_inc(la_n, 1)
                v.wait_ge(la_tr, t + 1)
                if t >= 2:
                    v.wait_ge(la_acc, t - 1)
                dst = latT[:, t % 2, :].rearrange("p (a n) -> p a n", a=5)
                v.tensor_tensor(dst[:, 0:3], ps[:, 0, 0:QR].rearrange("p (a n) -> p a n", a=3),
                                over(cols[:, C_QA:C_QA + 3], P), ALU.mult)
                v.tensor_tensor(dst[:, 3:5], ps[:, 1, 0:KVR].rearrange("p (a n) -> p a n", a=2),
                                over(cols[:, C_KVA:C_KVA + 2], P), ALU.mult)
                v.drain().then_inc(la_T, 1)

            latent_in(0)
            for t in range(T):
                if t + 1 < T:
                    latent_in(t + 1)
                v.wait_ge(la_ev, t + 1)
                v.tensor_reduce(mst[:, 0, t, :].rearrange("p (a b) -> p a b", a=2), msq, AX.X, ALU.add).then_inc(mq_red, 1)
                v.wait_ge(mq_rms, t + 1)
                v.reciprocal(mst[:, 2, t, :], mst[:, 1, t, :])
                v.drain()
                bufs = list(enumerate(qktok[t % 2]))
                for i, buf in bufs:
                    v.tensor_tensor(buf, buf, over(mst[:, 2, t, 8 * i:8 * i + 8], MLA_QK), ALU.mult)
                v.drain()
                for i, buf in bufs:
                    row = (RB_MQ, RB_MK)[i] - D
                    v.tensor_tensor(buf, buf, each(rowsb[:, row:row + MLA_QK], 8), ALU.mult)
                v.drain()
                cos = each(trig[:, 0, 16 * t:16 * t + 16], 8)
                sin = each(trig[:, 1, 16 * t:16 * t + 16], 8)
                for i, buf in bufs:
                    lo, hi = buf[:, :, 64:80], buf[:, :, 80:96]
                    v.tensor_tensor(rp[:, 0], lo, cos, ALU.mult)
                    v.tensor_tensor(rp[:, 1], hi, sin, ALU.mult)
                    v.tensor_tensor(rp[:, 2], hi, cos, ALU.mult)
                    v.tensor_tensor(rp[:, 3], lo, sin, ALU.mult)
                    v.drain()
                    v.tensor_tensor(lo, rp[:, 0], rp[:, 1], ALU.subtract)
                    v.tensor_tensor(hi, rp[:, 2], rp[:, 3], ALU.add)
                    v.drain().then_inc(mq_tok, 1)

            for i in range(T * HEADS2 + 2):
                if i < T * HEADS2:
                    t, h = i // HEADS2, i % HEADS2
                    v.wait_ge(s2_ready, i + 1)
                    v.tensor_reduce(sst2[:, 0, i:i + 1], ps[:, i % 2, 0:(t + 1) * P], AX.X, ALU.max)
                    v.drain()
                    v.tensor_scalar(sst2[:, 1, i:i + 1], sst2[:, 0, i:i + 1], -MLA_SCALE if h < 8 else -SCALE, None,
                                    ALU.mult).then_inc(max2, 1)
                if i >= 2:
                    u = i - 2
                    t, h = u // HEADS2, u % HEADS2
                    v.wait_ge(exp2, u + 1)
                    v.reciprocal(sst2[:, 3, u:u + 1], sst2[:, 2, u:u + 1])
                    v.drain()
                    v.wait_ge(av2, u + 1)
                    o = 64 * (h % 2)
                    v.tensor_scalar(mixed2[:, t, 64 * h:64 * h + 64], ps[:, 4 + u % 2, o:o + 64], sst2[:, 3, u:u + 1],
                                    None, ALU.mult).then_inc(o2_done, 1)

            scaled, evac = norm(3, range(T), xn4)
            mixed_low(T, 0, mid_lo)
            low_part(W_O2 + 2)
            low_part(W_O2 + 3)
            for t in range(T):
                if t + 1 < T:
                    mixed_low(T, t + 1, mid_lo)
                for n in range(4):
                    v.wait_ge(out_acc, 4 * (T + t) + n + 1)
                    tmp = gtmp[:, n % 2, :]
                    v.tensor_tensor(tmp, ps[:, 4 + n, 0:256], gates[:, 0, 256 * n:256 * n + 256], ALU.mult)
                    v.drain()
                    xs = x[:, t, 256 * n:256 * n + 256]
                    v.tensor_tensor(xs, xs, tmp, ALU.add).then_inc(out_add, 1)
                v.drain()
                scaled(t)
                if t:
                    evac(t - 1)
            evac(T - 1)

            def best(src, spare, vals, inds):
                v.max(vals[:, 0:8], src)
                v.drain()
                v.max_index(inds[:, 0:8], vals[:, 0:8], src)
                v.match_replace(out=spare, in_to_replace=vals[:, 0:8], in_values=src, imm_value=LOW)
                v.drain()
                v.max(vals[:, 8:16], spare)
                v.drain()
                v.max_index(inds[:, 8:16], vals[:, 8:16], spare)
                v.drain()

            PARTS = 5

            def choose(part, head):
                if part == 0:
                    v.tensor_copy(hsc.rearrange("p a b -> p (a b)"), sc[:, bass.ds(head * 256, 256)])
                    v.drain()
                    best(hsc[:, 0, :], sc2, topv[:, 0, :], topi[:, 0, :])
                elif part == 1:
                    best(hsc[:, 1, :], sc2, topv[:, 1, :], topi[:, 1, :])
                    v.tensor_tensor(cand[:, 0, :].rearrange("p (a b) -> p a b", a=TOPK), over(topv[:, 0, :], TOPK),
                                    each(topv[:, 1, :], TOPK), ALU.add)
                    v.tensor_copy(topf, topi)
                    v.drain()
                elif part == 2:
                    best(cand[:, 0, :], cand[:, 1, :], bestv, besti)
                elif part == 3:
                    v.tensor_scalar(gate[:, bass.ds(head * TOPK, TOPK)], bestv, bestv[:, 0:1], None, ALU.subtract)
                    v.tensor_scalar(bits[:, 0, :], besti, 4, None, ALU.logical_shift_right)
                    v.tensor_scalar(bits[:, 1, :], besti, 15, None, ALU.bitwise_and)
                    v.drain()
                    v.tensor_copy(bitf, bits)
                    v.drain()
                else:
                    for half in range(2):
                        v.tensor_tensor(hot, over(bitf[:, half, :], 16), each(iota, TOPK), ALU.is_equal)
                        v.drain()
                        v.tensor_tensor(hot, hot, each(topf[:, half, :], TOPK), ALU.mult)
                        v.drain()
                        v.tensor_reduce(e12[:, half, :], hot, AX.X, ALU.add)
                        v.drain()
                    v.scalar_tensor_tensor(out=expf, in0=e12[:, 0, :], scalar=float(NKEYS), in1=e12[:, 1, :],
                                           op0=ALU.mult, op1=ALU.add)
                    v.drain()
                    v.tensor_copy(idx[:, bass.ds(head * TOPK, TOPK)], expf).then_inc(idx_ready, 1)

            def weights(r, head):
                at = bass.ds(r * TOPK + head * TOPK, TOPK)
                v.wait_ge(gate_exp, r + (head + 1))
                v.tensor_reduce(gst[:, 0, 0:1], gate[:, at], AX.X, ALU.add)
                v.drain()
                v.reciprocal(gst[:, 1, 0:1], gst[:, 0, 0:1])
                v.drain()
                v.wait_ge(gelu_done, r + (head + 1))
                v.scalar_tensor_tensor(out=wts[:, at], in0=wts[:, at], scalar=gst[:, 1, 0:1], in1=gate[:, at],
                                       op0=ALU.mult, op1=ALU.mult).then_inc(w_ready, 1)

            def dots_of(t, r, head, first=False, last=False):
                for k in range(TOPK):
                    v.wait_ge(u_in[k % ROWS], r * 32 + (2 * head + k // ROWS + 1) * 16)
                    v.tensor_tensor_reduce(out=urows[k % ROWS], in0=urows[k % ROWS], in1=h2[:, t, :], scale=1.0,
                                           scalar=0.0, op0=ALU.mult, op1=ALU.add,
                                           accum_out=dstage[:, k:k + 1]).then_inc(u_free[k % ROWS], 1)
                    if not last and k % 3 == 1:
                        choose(k // 3, r + (head + 1))
                    if not first and k == 9:
                        weights(r, head - 1)
                v.drain()
                v.tensor_copy(wts[:, bass.ds(r * TOPK + head * TOPK, TOPK)], dstage).then_inc(dots_done, 1)
                v.drain()

            def finish(t):
                v.wait_ge(y_acc, t + 1)
                y = ps[:, 2 * (t % 2):2 * (t % 2) + 2, :]
                v.tensor_tensor(y, y, gates[:, 1, :].rearrange("p (a b) -> p a b", a=2), ALU.mult)
                v.drain()
                xt = x[:, t, :].rearrange("p (a b) -> p a b", a=2)
                v.tensor_tensor(xt, xt, y, ALU.add).then_inc(y_ready, 1)
                v.drain()

            v.memset(zmat, 0.0)
            v.drain().then_inc(setup_dve, 1)
            v.wait_ge(sk_ev, 2)
            for part in range(PARTS):
                choose(part, 0)
            v.wait_ge(h2_ev, T)
            v.wait_ge(sk_ev, 4)
            dots_of(0, 0, 0, first=True)
            with v.Fori(0, PH - 2) as r:
                v.wait_ge(sk_ev, r * 2 + 6)
                dots_of(0, r, 1)
            v.wait_ge(sk_ev, 16)
            dots_of(0, 0, PH - 1)
            for t in range(1, T):
                with v.Fori(0, PH - 1) as r:
                    dots_of(t, r, t * PH)
                dots_of(t, 0, (t + 1) * PH - 1, last=t == T - 1)
                finish(t - 1)
            weights(0, NHEAD - 1)
            finish(T - 1)

        @block.tensor
        def _(pe):
            pe.wait_ge(const_in_s, 32)

            def norm(layer, tiles, buf):
                for t in tiles:
                    o, n = ln_base[layer] + t, rows_of(t)
                    pe.wait_ge(ln_xn, o + 1)
                    if layer in (1, 3):
                        b = 2
                        if t:
                            pe.wait_ge(ln_hT, o)
                    else:
                        b = 2 * (t % 2)
                        if t >= 2:
                            pe.wait_ge(ln_hT, o - 1)
                    for k in range(KD):
                        mm = pe.transpose(ps[:, b + k // 4, P * (k % 4):P * (k % 4) + n],
                                          buf[0:n, t % 2, P * k:P * k + P], ident[0:n, 0:n])
                    mm.then_inc(ln_tr, 1)

            norm(0, range(T + 1), xn)

            def linear(c, t, bank, r=P, w=256):
                wt = ring[:, c % WR, :].rearrange("p (k n) -> p k n", k=KD)
                for k in range(KD):
                    mm = pe.matmul(ps[0:r, bank, 0:w], hT[:, k, t * P:t * P + r], wt[:, k, 0:w],
                                   start=(k == 0), stop=(k == KD - 1))
                return mm

            def pj_transposes(j):
                n, t = pj_jobs[j]
                r = rows_of(t)
                pe.wait_ge(pj_tok, j + 1)
                if j >= 4:
                    pe.wait_ge(pj_ev, j - 3)
                for c in range(2):
                    mm = pe.transpose(ps[:, j % 4, P * c:P * c + r], tok[0:r, j % 3, P * c:P * c + P], ident[0:r, 0:r])
                mm.then_inc(pj_tr, 1)

            for j, (n, t) in enumerate(pj_jobs):
                chunk(pe, W_IN + n)
                pe.wait_ge(ln_hT, t + 1)
                if j >= 4:
                    pe.wait_ge(pj_raw, j - 3)
                mm = linear(W_IN + n, t, 4 + j % 4, rows_of(t))
                mm.then_inc(pj_acc, 1)
                if j + 1 == len(pj_jobs) or pj_jobs[j + 1][0] != n:
                    pe.drain().then_inc(w_used, 1)
                if 3 <= j < QK + 3:
                    pj_transposes(j - 3)

            pe.wait_ge(pj_ev, QK)
            pe.wait_ge(pj_raw, len(pj_jobs))

            def scores(s):
                t, l = s // 16, s % 16
                head = l
                kT = kTa[:, l // 4, :] if l < 8 else kTb[:, (l - 8) // 2, :]
                if s >= 2:
                    pe.wait_ge(exp_done, s - 1)
                for a in range(2):
                    mm = pe.matmul(ps[:, 2 * (s % 2) + a, 0:HALF], qz[:, head, t * P:(t + 1) * P],
                                   kT[:, a * HALF:(a + 1) * HALF], start=True, stop=True)
                mm.then_inc(s_ready, 1)

            def prob_transposes(i):
                t, s, n, h = pv_jobs[i]
                pe.wait_ge(exp_done, s + n)
                if n == 2:
                    pe.wait_ge(comb_done, 4 * t + h + 1)
                if i >= 2:
                    pe.wait_ge(pta_done, i - 1)
                    pe.wait_ge(ptb_done, i - 1)
                    pe.wait_ge(o_done, i - 1)
                pr = prob[:, s % 4, :]
                for k in range(T):
                    pe.transpose(ps[:, 4 + i % 2, P * k:P * k + P], pr[:, P * k:P * k + P], ident)
                mm = pe.transpose(ps[0:META, 6 + i % 2, 0:P], pr[:, 512:KEYS], ident)
                mm.then_inc(pt_ready, 1)

            def values(i):
                t, s, n, h = pv_jobs[i]
                pe.wait_ge(pta_done, i + 1)
                pe.wait_ge(ptb_done, i + 1)
                if i >= 2:
                    pe.wait_ge(o_done, i - 1)
                for k in range(T + 1):
                    r = rows_of(k)
                    vals = va[0:r, k, :] if n == 1 else vb[0:r, k, P * h:P * h + P]
                    mm = pe.matmul(ps[:, 6 + i % 2, P:2 * P], probT[0:r, i % 2, P * k:P * k + P],
                                   vals, start=(k == 0), stop=(k == T))
                mm.then_inc(av_ready, 1)

            for i in range(NPV + 2):
                if i < NPV:
                    _, s, n, _ = pv_jobs[i]
                    for j in range(n):
                        scores(s + j)
                if 1 <= i <= NPV:
                    prob_transposes(i - 1)
                if i >= 2:
                    values(i - 2)

            def linear_split(c, t, bank, low):
                w_parts = [w.rearrange("p (k n) -> p k n", k=KD) for w in (high_of(c), w_lo[:, c % WR, :])]
                for k in range(KD):
                    for i, (w, h) in enumerate(passes(w_parts, (h_hi, low))):
                        mm = pe.matmul(ps[:, bank, 0:256], h[:, k, t * P:(t + 1) * P], w[:, k, :],
                                       start=(k == 0 and i == 0), stop=(k == KD - 1 and i == 2))
                return mm

            def mixed_linear(src, first, c0, layer, buf, low, ready):
                def transposes(t):
                    ready(t)
                    if t:
                        pe.wait_ge(mixt_ev, first + t)
                        pe.wait_ge(mixt_lo, first + t)
                    for k in range(KD):
                        mm = pe.transpose(ps[:, k // 4, P * (k % 4):P * (k % 4) + P], src[:, t, P * k:P * k + P], ident)
                    mm.then_inc(mixt_tr, 1)

                transposes(0)
                for t in range(T):
                    if t + 1 < T:
                        transposes(t + 1)
                    pe.wait_ge(mixt_lo, first + t + 1)
                    for n in range(4):
                        pe.wait_ge(w_lo_done, split_no(c0 + n))
                        if t:
                            pe.wait_ge(out_add, 4 * (first + t - 1) + n + 1)
                        mm = linear_split(c0 + n, t, 4 + n, low)
                        mm.then_inc(out_acc, 1)
                        if t == T - 1:
                            pe.drain().then_inc(w_used, 1)
                    if t:
                        norm(layer, [t - 1], buf)
                norm(layer, [T - 1], buf)

            pe.wait_ge(o_done, NPV)
            mixed_linear(mixed, 0, W_OUT, 1, xn1, h_lo, lambda t: pe.wait_ge(mix_ready, t + 1))

            pe.wait_ge(ln_hT, 9)
            for f in range(NF):
                pe.wait_ge(w_lo_done, split_no(W_GU + f))
                if f >= 2:
                    pe.wait_ge(act_ready, f - 1)
                w_parts = [w.rearrange("p (k u n) -> p k u n", k=KD, u=2)
                           for w in (high_of(W_GU + f), w_lo[:, (W_GU + f) % WR, :])]
                for u in range(2):
                    for k in range(KD):
                        for i, (w, h) in enumerate(passes(w_parts, (h_hi, h_lo))):
                            mm = pe.matmul(ps[:, 2 * (f % 2) + u, :], w[:, k, u, :], h[:, k, 0:512],
                                           start=(k == 0 and i == 0), stop=(k == KD - 1 and i == 2))
                mm.then_inc(gu_acc, 1)
                pe.drain().then_inc(w_used, 1)
                if f in gate_at:
                    g = gate_at.index(f)
                    pe.wait_ge(gbc_ready, g + 1)
                    for k in range(KD):
                        mm = pe.matmul(ps[:, 4 + 2 * g + k // 4, P * (k % 4):P * (k % 4) + P], gbc[:, k, :], ident,
                                       start=True, stop=True)
                    mm.then_inc(gate_acc, 1)
            pe.wait_ge(act_ready, NF)
            pe.wait_ge(gate_ev, 2)
            for f in range(NF):
                c, g = W_DOWN + f // 2, f // 2
                pe.wait_ge(w_lo_done, split_no(c))
                pe.wait_ge(a_lo_done, g + 1)
                w_parts = [w.rearrange("p (j n) -> p j n", j=2) for w in (high_of(c), w_lo[:, c % WR, :])]
                for t in range(T):
                    for half in range(2):
                        for i, (w, a) in enumerate(passes(w_parts, (a_hi[:, g % 2], a_lo[:, g % 2]))):
                            mm = pe.matmul(ps[:, 2 * t + half, :], a[:, f % 2, t * P:(t + 1) * P],
                                           w[:, f % 2, 512 * half:512 * half + 512],
                                           start=(f == 0 and i == 0), stop=(f == NF - 1 and i == 2))
                        if f == NF - 1:
                            mm.then_inc(down_acc, 1)
                if f % 2:
                    pe.drain().then_inc(w_used, 1)

            norm(2, range(2), xn)


            def fx_transposes(k):
                pe.wait_ge(fx_tok, k + 1)
                if k >= 4:
                    pe.wait_ge(fx_ev, k - 3)
                buf = ftok[:, 2 * (k >= 8) + k % 2]
                for c in range(4):
                    mm = pe.transpose(ps[:, k % 4, P * c:P * c + P], buf[:, c, :], ident)
                mm.then_inc(fx_tr, 1)

            for j in range(9 * T):
                n, t = j // T, j % T
                k = j - 3 * T
                c = W_IN2 + n
                pe.wait_ge(w_lo_done, split_no(c))
                pe.wait_ge(ln_hT, 9 + t + 1)
                if j >= 4:
                    pe.wait_ge(p2_ev, j - 3)
                mm = linear_split(c, t, 4 + j % 4, h2_lo)
                mm.then_inc(p2_acc, 1)
                if t == T - 1:
                    pe.drain().then_inc(w_used, 1)
                if j + 2 < T:
                    norm(2, [j + 2], xn)
                if j == 2 * T:
                    pe.wait_ge(once_dve, LOG_GATES)
                    for u in range(T):
                        for w in range(u + 1):
                            mm = pe.matmul(ps[:, 3, 8 * u:8 * u + 8], triu if w == u else ones,
                                           logf[:, 2, 8 * w:8 * w + 8], start=(w == 0), stop=(w == u))
                    mm.then_inc(fc_acc, 1)
                if k == 0:
                    pe.wait_ge(once_dve, GATE_SUMS)
                if 3 <= k < 19:
                    fx_transposes(k - 3)

            for c in range(3):
                chunk(pe, W_LAT + c)
            uq = [ring[:, (W_LAT + k // 2) % WR, 768 * (k % 2):768 * (k % 2) + 768] for k in range(3)]
            ukv = ring[:, (W_LAT + 2) % WR, :].rearrange("p (k n) -> p k n", k=2)
            pe.wait_ge(fx_ev, 16)
            pe.wait_ge(p2_ev, 9 * T)
            def latent_out(t):
                for g in range(4):
                    buf = qktok[t % 2][g // 2]
                    pe.wait_ge(mq_tok, 2 * t + g // 2 + 1)
                    if 4 * t + g >= 2:
                        pe.wait_ge(mq_ev, 4 * t + g - 1)
                    for c in range(4):
                        mm = pe.transpose(ps[0:MLA_QK, 6 + g % 2, P * c:P * c + P], buf[:, 4 * (g % 2) + c, :], ident)
                    mm.then_inc(mq_tr, 1)

            for t in range(T):
                pe.wait_ge(la_n, t + 1)
                for k in range(5):
                    bank, at = (0, P * k) if k < 3 else (1, P * (k - 3))
                    mm = pe.transpose(ps[:, bank, at:at + P], latn[:, P * k:P * k + P], ident)
                mm.then_inc(la_tr, 1)
                pe.wait_ge(la_T, t + 1)
                if t:
                    pe.wait_ge(la_ev, t)
                lT = latT[:, t % 2, :].rearrange("p (a n) -> p a n", a=5)
                for half in range(2):
                    for k in range(3):
                        pe.matmul(ps[:, 2 + half, 0:384], lT[:, k, :], uq[k][:, 384 * half:384 * half + 384],
                                  start=(k == 0), stop=(k == 2))
                for half in range(2):
                    for k in range(2):
                        mm = pe.matmul(ps[:, 4 + half, :], lT[:, 3 + k, :], ukv[:, k, 512 * half:512 * half + 512],
                                       start=(k == 0), stop=(k == 1))
                mm.then_inc(la_acc, 1)
                if t:
                    latent_out(t - 1)
            latent_out(T - 1)
            pe.drain().then_inc(w_used, 3)
            pe.wait_ge(mq_ev, 4 * T)

            NU = T * HEADS2
            for i in range(NU + 2):
                if i < NU:
                    t, h = i // HEADS2, i % HEADS2
                    if i >= 2:
                        pe.wait_ge(exp2, i - 1)
                    n = (t + 1) * P
                    q = qT_mla[0:MLA_QK, h, t * P:n] if h < 8 else qT_fox[:, h - 8, t * P:n]
                    kk = kT_mla[0:MLA_QK, h, 0:n] if h < 8 else kT_fox[:, h - 8, 0:n]
                    pe.matmul(ps[:, i % 2, 0:n], q, kk, start=True, stop=False)
                    pe.matmul(ps[:, i % 2, t * P:n], ident, maskt, start=False, stop=True).then_inc(s2_ready, 1)
                if 1 <= i <= NU:
                    u = i - 1
                    pe.wait_ge(exp2, u + 1)
                    if u >= 2:
                        pe.wait_ge(pt2_done, u - 1)
                    for k in range(u // HEADS2 + 1):
                        mm = pe.transpose(ps[:, 2 + u % 2, P * k:P * k + P], prob2[:, u % 4, P * k:P * k + P], ident)
                    mm.then_inc(pt2, 1)
                if i >= 2:
                    u = i - 2
                    t, h = u // HEADS2, u % HEADS2
                    pe.wait_ge(pt2_done, u + 1)
                    if u >= 2:
                        pe.wait_ge(o2_done, u - 1)
                    for k in range(t + 1):
                        vv, hh = (v_mla, h) if h < 8 else (v_fox, h - 8)
                        mm = pe.matmul(ps[:, 4 + u % 2, 0:P], probT2[:, u % 2, P * k:P * k + P],
                                       vv[:, k, P * (hh // 2):P * (hh // 2) + P], start=(k == 0), stop=(k == t))
                    mm.then_inc(av2, 1)

            mixed_linear(mixed2, T, W_O2, 3, xn4, mid_lo, lambda t: pe.wait_ge(o2_done, NU))
            for t in range(T):
                pe.wait_ge(ln_hT, 13 + t + 1)
                if t == 0:
                    pe.wait_ge(out_add, 8 * T)
                if t >= 2:
                    pe.wait_ge(h2_ev, t - 1)
                b = 4 + 2 * (t % 2)
                for k in range(KD):
                    mm = pe.transpose(ps[:, b + k // 4, P * (k % 4):P * (k % 4) + P], hT[:, k, t * P:(t + 1) * P], ident)
                mm.then_inc(h2_tr, 1)
            pe.wait_ge(ln_hT, 17)
            pe.wait_ge(subk_in_s, 16)
            for c in range(17):
                if c < 16:
                    w = W_PQ + c // 2
                    chunk(pe, w)
                    if c >= 4:
                        pe.wait_ge(qp_ev, c - 3)
                    wt = ring[:, w % WR, :].rearrange("p (k n) -> p k n", k=KD)
                    for k in range(KD):
                        mm = pe.matmul(ps[:, c % 4, :], wt[:, k, P * (c % 2):P * (c % 2) + P], hT[:, k, 0:512],
                                       start=(k == 0), stop=(k == KD - 1))
                    mm.then_inc(qp_acc, 1)
                    if c % 2:
                        pe.drain().then_inc(w_used, 1)
                if c >= 1:
                    q = c - 1
                    pe.wait_ge(qp_ev, q + 1)
                    pe.wait_ge(h2_ev, T)
                    if q >= 4:
                        pe.wait_ge(sk_ev, q - 3)
                    for t in range(T):
                        mm = pe.matmul(ps[:, 4 + q % 4, P * t:P * t + P], qpT[:, q % 4, t * P:(t + 1) * P], subk[:, q, :],
                                       start=True, stop=True)
                    mm.then_inc(sk_acc, 1)

            pe.wait_ge(setup_dve, 2)
            for t in range(T):
                b = 2 * (t % 2)
                if t >= 2:
                    pe.wait_ge(y_ready, t - 1)
                for half in range(2):
                    pe.matmul(ps[:, b + half, :], zmat, const[:, 0:512], start=True, stop=False,
                              skip_group_check=True)
                with pe.Fori(0, PH) as r:
                    for k in range(TOPK):
                        pe.wait_ge(diag_ready, r * TOPK + (t * SLOTS + k + 1))
                        pe.wait_ge(v_in[k % ROWS], r * 32 + (2 * t * PH + k // ROWS + 1) * 16)
                        for half in range(2):
                            mm = pe.matmul(ps[:, b + half, :], diag[:, k % 4, :], vrows[k % ROWS][:, 512 * half:512 * half + 512],
                                           start=False, stop=False, skip_group_check=True)
                        mm.then_inc(v_free[k % ROWS], 1)
                pe.drain().then_inc(y_acc, 1)


def _chunks(w, np):
    k, n = w.shape
    w = np.pad(w, ((0, 0), (0, -n % 256)))
    return w.reshape(k // P, P, -1, 256).transpose(2, 1, 0, 3).reshape(-1, P, CH)


def kernel(**inputs):
    import numpy as _np
    import concourse.bacc as _bacc
    from concourse import mybir as _mybir
    from concourse.bass_utils import run_bass_kernel_spmd as _run

    g = {k: _np.asarray(v) for k, v in inputs.items()}
    f = _np.float32

    gu = _np.stack([g["w_gate"][0], g["w_up"][0]]).reshape(2, KD, P, NF, P).transpose(3, 2, 1, 0, 4).reshape(NF, P, CH)
    down = g["w_down"][0].reshape(NF // 2, 2, P, D).transpose(0, 2, 1, 3).reshape(NF // 2, P, CH)
    w2 = g["w_in_2"]
    lat = _np.concatenate([w2[:, 0:672], w2[:, 2208:2216]], axis=1)
    w2 = _np.concatenate([_np.pad(lat[:, 512:], ((0, 0), (0, 768 - LAT))), lat[:, :512], w2[:, 672:2208]], axis=1)
    uq = g["w_uq_2"].reshape(3, P, 768)
    uq01 = _np.pad(_np.concatenate([uq[0], uq[1]], axis=1), ((0, 0), (0, CH - 1536)))
    uq2 = _np.pad(uq[2], ((0, 0), (0, CH - 768)))
    ukv = g["w_ukv_2"].reshape(2, P, D).transpose(1, 0, 2).reshape(P, CH)
    wst = _np.concatenate([_chunks(g["w_in"][0], _np), _chunks(g["w_out"][0], _np), gu, down, _chunks(w2, _np),
                           uq01[None], uq2[None], ukv[None], _chunks(g["w_o_2"], _np), _chunks(g["w_pq_2"], _np)])
    wada = _np.ascontiguousarray(g["w_ada_2"].T).reshape(48, P, D)

    def by_partition(v):
        return v.reshape(-1, P).T

    cols = _np.concatenate([by_partition(g[n]) for n in ("attn_norm_g", "ffn_norm_g", "norm1_g_2", "norm2_g_2",
                                                         "b_ada_2", "mla_qa_g_2", "mla_kva_g_2")], axis=1)
    gains = []
    for n in ("a_q_norm_g", "a_k_norm_g", "b_q_norm_g", "b_k_norm_g"):
        v = g[n][0]
        gains += [v, v.reshape(-1, 2)[:, ::-1].reshape(-1)]
    rowsa = _np.concatenate([*gains, g["b_subln_g"][0], g["b_lambda_q1"][0], g["b_lambda_k1"][0], g["b_lambda_q2"][0],
                             g["b_lambda_k2"][0]])[None]
    rowsb = _np.concatenate([g["c_2"][0], g["mla_q_g_2"], g["mla_k_g_2"], g["fox_q_g_2"], g["fox_k_g_2"],
                             g["b_f_2"]])[None]
    real = _np.arange(T * P)
    inv = (10000.0 ** (-_np.arange(0, HD, 2, dtype=f) / HD)).astype(f)
    inva = (10000.0 ** (-_np.arange(0, HD // 2, 2, dtype=f) / (HD // 2))).astype(f)
    ang_a = _np.zeros((5 * P, HD // 2), f)
    ang_a[:T * P] = _np.concatenate([(real // 64).astype(f)[:, None] * inva, (real % 64).astype(f)[:, None] * inva], 1)
    ang_b = _np.zeros((5 * P, HD // 2), f)
    ang_b[:T * P] = (real + META).astype(f)[:, None] * inv
    ang_b[T * P:T * P + META] = _np.arange(META, dtype=f)[:, None] * inv
    tables = []
    for ang in (ang_a, ang_b):
        c, s = _np.cos(ang), _np.sin(ang)
        tables += [_np.stack([c, c], -1), _np.stack([-s, s], -1)]
    rope = _np.stack(tables).reshape(4, 5, P, HD).transpose(2, 0, 1, 3).reshape(P, 4 * 5 * HD).astype(f)
    const = _np.zeros((P, NCONST), f)
    const[:, K_ID:K_ID + P] = _np.eye(P)
    const[:, K_TRIU:K_TRIU + P] = _np.triu(_np.ones((P, P)))
    const[:, K_MASK:K_MASK + P] = _np.triu(_np.ones((P, P)), 1) * MASK
    const[:, K_ONES:K_ONES + P] = 1.0
    const[:, K_IOTA:K_IOTA + 16] = _np.arange(16)
    const[:, K_FREQ:K_FREQ + 16] = 10000.0 ** (-_np.arange(0, 32, 2, dtype=f) / 32)
    arrays = {
        "wst": wst, "wada": wada, "x_in": g["x"].reshape(T, P, D), "meta_in": g["meta_tokens"], "cols_in": cols,
        "rowsa_in": rowsa, "rowsb_in": rowsb, "rope_in": rope, "const_in": const,
        "pos_in": g["positions_2"].reshape(T, P).T,
        "subk_in": g["sub_keys_2"].reshape(16, NKEYS, P).transpose(2, 0, 1).reshape(P, CH),
        "peer_u": g["peer_u_2"], "peer_v": g["peer_v_2"],
    }
    arrays = {k: _np.ascontiguousarray(v) for k, v in arrays.items()}
    nc = _bacc.Bacc("TRN2", target_bir_lowering=False, num_devices=1)
    args = {n: nc.dram_tensor(n, a.shape, _mybir.dt.from_np(a.dtype), kind="ExternalInput").ap()
            for n, a in arrays.items()}
    out = nc.dram_tensor("out", (T, P, D), F32, kind="ExternalOutput").ap()
    build(nc, out=out, **args)
    r = _run(nc, [arrays], core_ids=[0])
    return r.results[0]["out"].reshape(1, T * P, D)
```
